# Optimizing a Trainium2 kernel written in Bass

```python
import math
import jax
import jax.numpy as jnp
from jax import lax
import numpy as np

D_MODEL = 1024
BATCH = 1
SEQ = 512
DEPTH = 1

CHUNK = 64
CONV_K = 4
GDN_HEADS = 8
GDN_DK = 128
GDN_DV = 128
SSD_INNER = D_MODEL
SSD_HEADDIM = 64
SSD_HEADS = SSD_INNER // SSD_HEADDIM
SSD_GROUPS = 4
SSD_HPG = SSD_HEADS // SSD_GROUPS
SSD_STATE = 128
RET_HEADS = 4
RET_DK = 128
RET_DV = 256
ROPE_BASE = 10000.0
N_BRANCH = 3
MEM_LEN = 256
XA_HEADS = 4
XA_DH = D_MODEL // XA_HEADS
N_EXPERTS = 16
N_EXPERT_GROUPS = 4
EXPERTS_PER_GROUP = N_EXPERTS // N_EXPERT_GROUPS
TOP_K = 2
D_EXPERT = 512
MOE_BLOCK = 128
DN_ALPHA = (2 * DEPTH) ** 0.25
DN_BETA = (8 * DEPTH) ** -0.25
LN_EPS = 1e-5
RMS_EPS = 1e-6

GDN_QKV = 2 * GDN_HEADS * GDN_DK + GDN_HEADS * GDN_DV
SSD_XBC = SSD_INNER + 2 * SSD_GROUPS * SSD_STATE
SPLIT_SIZES = (GDN_QKV, GDN_HEADS * GDN_DV, GDN_HEADS, GDN_HEADS,
               SSD_XBC, SSD_INNER, SSD_HEADS,
               RET_HEADS * RET_DK, RET_HEADS * RET_DK, RET_HEADS * RET_DV, RET_HEADS * RET_DV,
               N_BRANCH * D_MODEL)
D_IN = (GDN_QKV + GDN_HEADS * GDN_DV + 2 * GDN_HEADS + SSD_XBC + SSD_INNER + SSD_HEADS
        + 2 * RET_HEADS * RET_DK + 2 * RET_HEADS * RET_DV + N_BRANCH * D_MODEL)

kernel_name = "hybrid_gdn_ssd_retention_moe_encoder"

def layer_norm(x, g, b):
    xf = x.astype(jnp.float32)
    mu = jnp.mean(xf, -1, keepdims=True)
    var = jnp.mean(jnp.square(xf - mu), -1, keepdims=True)
    return ((xf - mu) * lax.rsqrt(var + LN_EPS) * g + b).astype(x.dtype)

def causal_depthwise_conv(x, w, b=None):
    y = lax.conv_general_dilated(x, w[:, None, :], window_strides=(1,), padding=[(CONV_K - 1, 0)],
                                 dimension_numbers=('NWC', 'WIO', 'NWC'),
                                 feature_group_count=x.shape[-1])
    return y if b is None else y + b

def rotary(x, cos, sin):
    x1, x2 = jnp.split(x, 2, axis=-1)
    c, s = cos[None, :, None, :], sin[None, :, None, :]
    return jnp.concatenate([x1 * c - x2 * s, x2 * c + x1 * s], axis=-1)

def split_columns(h):
    return jnp.split(h, np.cumsum(SPLIT_SIZES)[:-1].tolist(), axis=-1)

def chunked_decay_attention(q, k, v, log_a):
    f32 = jnp.float32
    bsz, seq, g, n = q.shape
    r, p = v.shape[-2:]
    nc = seq // CHUNK
    q = q.astype(f32).reshape(bsz, nc, CHUNK, g, n)
    k = k.astype(f32).reshape(bsz, nc, CHUNK, g, n)
    v = v.astype(f32).reshape(bsz, nc, CHUNK, g, r, p)
    cum = jnp.cumsum(log_a.astype(f32).reshape(bsz, nc, CHUNK, g, r), axis=2)
    idx = jnp.arange(CHUNK)
    causal = idx[:, None] >= idx[None, :]
    seg = cum[:, :, :, None] - cum[:, :, None, :]
    decay = jnp.exp(jnp.where(causal[:, :, None, None], seg, -jnp.inf))
    scores = jnp.einsum('bctgn,bcsgn->bctsg', q, k)
    y_intra = jnp.einsum('bctsgr,bcsgrp->bctgrp', scores[..., None] * decay, v)
    last = cum[:, :, -1]
    k_w = jnp.exp(last[:, :, None] - cum)
    chunk_kv = jnp.einsum('bcsgn,bcsgrp->bcgrnp', k, v * k_w[..., None])

    def step(state, inp):
        kv_c, a_c = inp
        return state * jnp.exp(a_c)[..., None, None] + kv_c, state

    _, prev = lax.scan(step, jnp.zeros((bsz, g, r, n, p), f32),
                       (jnp.moveaxis(chunk_kv, 1, 0), jnp.moveaxis(last, 1, 0)))
    prev = jnp.moveaxis(prev, 0, 1)
    y_inter = jnp.einsum('bctgn,bcgrnp->bctgrp', q, prev) * jnp.exp(cum)[..., None]
    return (y_intra + y_inter).reshape(bsz, seq, g, r, p)

def chunked_gated_delta_rule(q, k, v, log_a, beta):
    f32 = jnp.float32
    bsz, seq, h, dk = q.shape
    dv = v.shape[-1]
    nc = seq // CHUNK
    q, k, v = (t.astype(f32).reshape(bsz, nc, CHUNK, h, -1) for t in (q, k, v))
    beta = beta.astype(f32).reshape(bsz, nc, CHUNK, h)
    cum = jnp.cumsum(log_a.astype(f32).reshape(bsz, nc, CHUNK, h), axis=2)
    cum_h = jnp.swapaxes(cum, 2, 3)
    seg = cum_h[..., :, None] - cum_h[..., None, :]
    idx = jnp.arange(CHUNK)
    causal = idx[:, None] >= idx[None, :]
    strict = idx[:, None] > idx[None, :]
    decay = jnp.exp(jnp.where(causal, seg, -jnp.inf))
    kb = k * beta[..., None]
    vb = v * beta[..., None]
    a_strict = jnp.where(strict, jnp.einsum('bcthd,bcshd->bchts', kb, k) * decay, 0.0)
    eye = jnp.eye(CHUNK, dtype=f32)
    t_mat = lax.linalg.triangular_solve(a_strict + eye, jnp.broadcast_to(eye, a_strict.shape),
                                        left_side=True, lower=True, unit_diagonal=True)
    u = jnp.einsum('bchts,bcshd->bcthd', t_mat, vb)
    w = jnp.einsum('bchts,bcshd->bcthd', t_mat, kb * jnp.exp(cum)[..., None])
    attn = jnp.where(causal, jnp.einsum('bcthd,bcshd->bchts', q, k) * decay, 0.0)
    last = cum[:, :, -1]
    q_dec = q * jnp.exp(cum)[..., None]
    k_dec = k * jnp.exp(last[:, :, None] - cum)[..., None]

    def step(state, inp):
        u_c, w_c, q_c, k_c, attn_c, a_c = inp
        v_new = u_c - jnp.einsum('bthk,bhkv->bthv', w_c, state)
        o_c = (jnp.einsum('bthk,bhkv->bthv', q_c, state)
               + jnp.einsum('bhts,bshv->bthv', attn_c, v_new))
        state = state * jnp.exp(a_c)[..., None, None] + jnp.einsum('bshk,bshv->bhkv', k_c, v_new)
        return state, o_c

    xs = tuple(jnp.moveaxis(t, 1, 0) for t in (u, w, q_dec, k_dec, attn, last))
    _, o = lax.scan(step, jnp.zeros((bsz, h, dk, dv), f32), xs)
    return jnp.moveaxis(o, 0, 1).reshape(bsz, seq, h, dv)

def gated_deltanet_branch(qkv, z, a, b, conv_w, a_log, dt_bias, norm_w):
    bsz, seq, _ = qkv.shape
    dtype = qkv.dtype
    qkv = jax.nn.silu(causal_depthwise_conv(qkv, conv_w))
    q, k, v = jnp.split(qkv, [GDN_HEADS * GDN_DK, 2 * GDN_HEADS * GDN_DK], axis=-1)
    q = q.astype(jnp.float32).reshape(bsz, seq, GDN_HEADS, GDN_DK)
    k = k.astype(jnp.float32).reshape(bsz, seq, GDN_HEADS, GDN_DK)
    v = v.reshape(bsz, seq, GDN_HEADS, GDN_DV)
    q = q * lax.rsqrt(jnp.sum(jnp.square(q), -1, keepdims=True) + RMS_EPS) * GDN_DK ** -0.5
    k = k * lax.rsqrt(jnp.sum(jnp.square(k), -1, keepdims=True) + RMS_EPS)
    log_a = -jnp.exp(a_log.astype(jnp.float32)) * jax.nn.softplus(a.astype(jnp.float32) + dt_bias)
    beta = jax.nn.sigmoid(b.astype(jnp.float32))
    o = chunked_gated_delta_rule(q, k, v, log_a, beta)
    o = o * lax.rsqrt(jnp.mean(jnp.square(o), -1, keepdims=True) + RMS_EPS) * norm_w
    o = o * jax.nn.silu(z.astype(jnp.float32)).reshape(bsz, seq, GDN_HEADS, GDN_DV)
    return o.reshape(bsz, seq, GDN_HEADS * GDN_DV).astype(dtype)

def ssd_branch(xbc, z, dt_raw, conv_w, conv_b, a_log, dt_bias, d_skip, norm_w):
    bsz, seq, _ = xbc.shape
    dtype = xbc.dtype
    xbc = jax.nn.silu(causal_depthwise_conv(xbc, conv_w, conv_b))
    xs, bm, cm = jnp.split(xbc, [SSD_INNER, SSD_INNER + SSD_GROUPS * SSD_STATE], axis=-1)
    xs = xs.astype(jnp.float32).reshape(bsz, seq, SSD_GROUPS, SSD_HPG, SSD_HEADDIM)
    bm = bm.reshape(bsz, seq, SSD_GROUPS, SSD_STATE)
    cm = cm.reshape(bsz, seq, SSD_GROUPS, SSD_STATE)
    dt = jax.nn.softplus(dt_raw.astype(jnp.float32) + dt_bias).reshape(bsz, seq, SSD_GROUPS, SSD_HPG)
    log_a = -jnp.exp(a_log.astype(jnp.float32)).reshape(SSD_GROUPS, SSD_HPG) * dt
    y = chunked_decay_attention(cm, bm, xs * dt[..., None], log_a)
    y = y + d_skip.reshape(SSD_GROUPS, SSD_HPG, 1) * xs
    y = y.reshape(bsz, seq, SSD_INNER) * jax.nn.silu(z.astype(jnp.float32))
    y = y.reshape(bsz, seq, SSD_GROUPS, SSD_INNER // SSD_GROUPS)
    y = y * lax.rsqrt(jnp.mean(jnp.square(y), -1, keepdims=True) + RMS_EPS)
    return (y.reshape(bsz, seq, SSD_INNER) * norm_w).astype(dtype)

def retention_branch(q, k, v, g, cos, sin):
    bsz, seq, _ = q.shape
    dtype = q.dtype
    q = rotary(q.reshape(bsz, seq, RET_HEADS, RET_DK), cos, sin)
    k = rotary(k.reshape(bsz, seq, RET_HEADS, RET_DK), cos, sin) * RET_DK ** -0.5
    v = v.reshape(bsz, seq, RET_HEADS, 1, RET_DV)
    log_gamma = jnp.log1p(-jnp.exp2(-5.0 - jnp.arange(RET_HEADS, dtype=jnp.float32)))
    log_a = jnp.broadcast_to(log_gamma[:, None], (bsz, seq, RET_HEADS, 1))
    o = chunked_decay_attention(q, k, v, log_a)[:, :, :, 0]
    mu = jnp.mean(o, -1, keepdims=True)
    var = jnp.mean(jnp.square(o - mu), -1, keepdims=True)
    o = ((o - mu) * lax.rsqrt(var + LN_EPS)).reshape(bsz, seq, RET_HEADS * RET_DV)
    return (jax.nn.silu(g.astype(jnp.float32)) * o).astype(dtype)

def hybrid_mixer(x, w_in, gdn_conv_w, gdn_a_log, gdn_dt_bias, gdn_norm_w,
                 ssd_conv_w, ssd_conv_b, ssd_a_log, ssd_dt_bias, ssd_d, ssd_norm_w,
                 w_proj_gdn, w_proj_ssd, w_proj_ret, w_out, cos, sin):
    bsz, seq, _ = x.shape
    (gdn_qkv, gdn_z, gdn_a, gdn_b, ssd_xbc, ssd_z, ssd_dt,
     ret_q, ret_k, ret_v, ret_g, gate_logits) = split_columns(x @ w_in)
    y_gdn = gated_deltanet_branch(gdn_qkv, gdn_z, gdn_a, gdn_b, gdn_conv_w, gdn_a_log, gdn_dt_bias, gdn_norm_w)
    y_ssd = ssd_branch(ssd_xbc, ssd_z, ssd_dt, ssd_conv_w, ssd_conv_b, ssd_a_log, ssd_dt_bias, ssd_d, ssd_norm_w)
    y_ret = retention_branch(ret_q, ret_k, ret_v, ret_g, cos, sin)
    gates = jax.nn.sigmoid(gate_logits).reshape(bsz, seq, N_BRANCH, D_MODEL)
    merged = (gates[:, :, 0] * (y_gdn @ w_proj_gdn)
              + gates[:, :, 1] * (y_ssd @ w_proj_ssd)
              + gates[:, :, 2] * (y_ret @ w_proj_ret))
    return merged @ w_out

def memory_cross_attention(x, mem, w_q, w_k, w_v, w_o):
    bsz, seq, _ = x.shape
    q = (x @ w_q).reshape(bsz, seq, XA_HEADS, XA_DH)
    k = (mem @ w_k).reshape(bsz, -1, XA_HEADS, XA_DH)
    v = (mem @ w_v).reshape(bsz, -1, XA_HEADS, XA_DH)
    s = jnp.einsum('bshd,bmhd->bhsm', q, k).astype(jnp.float32) * XA_DH ** -0.5
    p = jax.nn.softmax(s, axis=-1).astype(v.dtype)
    o = jnp.einsum('bhsm,bmhd->bshd', p, v).reshape(bsz, seq, D_MODEL)
    return o @ w_o

def group_limited_route(xt, w_router, b_router):
    t = xt.shape[0]
    scores = jax.nn.sigmoid((xt @ w_router).astype(jnp.float32))
    sel = (scores + b_router).reshape(t, N_EXPERT_GROUPS, EXPERTS_PER_GROUP)
    group_score = jnp.sum(lax.top_k(sel, 2)[0], axis=-1)
    g_idx = jnp.argmax(group_score, axis=-1)
    in_group = jnp.take_along_axis(sel, g_idx[:, None, None], axis=1)[:, 0]
    _, local = lax.top_k(in_group, TOP_K)
    expert = g_idx[:, None] * EXPERTS_PER_GROUP + local
    w = jnp.take_along_axis(scores, expert, axis=1)
    return expert, w / jnp.sum(w, -1, keepdims=True)

def moe_ffn(x, w_router, b_router, w_gate, w_up, w_down):
    bsz, seq, d = x.shape
    xt = x.reshape(-1, d)
    t = xt.shape[0]
    expert, gate = group_limited_route(xt, w_router, b_router)
    flat_e = expert.reshape(-1)
    flat_tok = jnp.repeat(jnp.arange(t, dtype=jnp.int32), TOP_K)
    order = jnp.argsort(flat_e)
    se, stok, sg = flat_e[order], flat_tok[order], gate.reshape(-1)[order]
    counts = jnp.bincount(flat_e, length=N_EXPERTS)
    padded = (counts + MOE_BLOCK - 1) // MOE_BLOCK * MOE_BLOCK
    start = jnp.cumsum(counts) - counts
    pend = jnp.cumsum(padded)
    dest = (pend - padded)[se] + jnp.arange(t * TOP_K) - start[se]
    n_blocks = (t * TOP_K + N_EXPERTS * (MOE_BLOCK - 1) + MOE_BLOCK - 1) // MOE_BLOCK
    npad = n_blocks * MOE_BLOCK
    buf_tok = jnp.full((npad,), t, jnp.int32).at[dest].set(stok)
    buf_g = jnp.zeros((npad,), xt.dtype).at[dest].set(sg.astype(xt.dtype))
    block_expert = jnp.minimum(
        jnp.searchsorted(pend, jnp.arange(n_blocks) * MOE_BLOCK, side='right'), N_EXPERTS - 1)
    xpad = jnp.concatenate([xt, jnp.zeros((1, d), xt.dtype)], axis=0)
    xb = xpad[buf_tok].reshape(n_blocks, MOE_BLOCK, d)

    def expert_block(args):
        xblk, e = args
        hid = jax.nn.silu(xblk @ w_gate[e]) * (xblk @ w_up[e])
        return hid @ w_down[e]

    yb = lax.map(expert_block, (xb, block_expert)).reshape(npad, d)
    y = jax.ops.segment_sum(yb * buf_g[:, None], buf_tok, num_segments=t + 1)[:t]
    return y.reshape(bsz, seq, d)

def setup_inputs(seed: int = 0) -> dict:
    key = jax.random.key(seed)
    ks = iter(jax.random.split(key, 40))
    f32 = jnp.float32
    L = DEPTH

    def nrm(shape, scale):
        return jax.random.normal(next(ks), shape, f32) * scale

    def gain(shape):
        return 1.0 + nrm(shape, 0.02)

    def a_log(shape):
        return jnp.log(jax.random.uniform(next(ks), shape, f32, 1.0, 16.0))

    def dt_bias(shape):
        dt = jnp.exp(jax.random.uniform(next(ks), shape, f32, math.log(1e-3), math.log(1e-1)))
        return dt + jnp.log(-jnp.expm1(-dt))

    return {
        "x": nrm((BATCH, SEQ, D_MODEL), 1.0),
        "mem": nrm((BATCH, MEM_LEN, D_MODEL), 1.0),
        "mix_w_in": nrm((L, D_MODEL, D_IN), D_MODEL ** -0.5),
        "gdn_conv_w": nrm((L, CONV_K, GDN_QKV), CONV_K ** -0.5),
        "gdn_a_log": a_log((L, GDN_HEADS)),
        "gdn_dt_bias": dt_bias((L, GDN_HEADS)),
        "gdn_norm_w": gain((L, GDN_DV)),
        "ssd_conv_w": nrm((L, CONV_K, SSD_XBC), CONV_K ** -0.5),
        "ssd_conv_b": nrm((L, SSD_XBC), 0.02),
        "ssd_a_log": a_log((L, SSD_HEADS)),
        "ssd_dt_bias": dt_bias((L, SSD_HEADS)),
        "ssd_d": gain((L, SSD_HEADS)),
        "ssd_norm_w": gain((L, SSD_INNER)),
        "w_proj_gdn": nrm((L, GDN_HEADS * GDN_DV, D_MODEL), (GDN_HEADS * GDN_DV) ** -0.5),
        "w_proj_ssd": nrm((L, SSD_INNER, D_MODEL), SSD_INNER ** -0.5),
        "w_proj_ret": nrm((L, RET_HEADS * RET_DV, D_MODEL), (RET_HEADS * RET_DV) ** -0.5),
        "mix_w_out": nrm((L, D_MODEL, D_MODEL), D_MODEL ** -0.5 * DN_BETA),
        "ln_mix_g": gain((L, D_MODEL)),
        "ln_mix_b": nrm((L, D_MODEL), 0.02),
        "xa_w_q": nrm((L, D_MODEL, D_MODEL), D_MODEL ** -0.5),
        "xa_w_k": nrm((L, D_MODEL, D_MODEL), D_MODEL ** -0.5),
        "xa_w_v": nrm((L, D_MODEL, D_MODEL), D_MODEL ** -0.5 * DN_BETA),
        "xa_w_o": nrm((L, D_MODEL, D_MODEL), D_MODEL ** -0.5 * DN_BETA),
        "ln_xa_g": gain((L, D_MODEL)),
        "ln_xa_b": nrm((L, D_MODEL), 0.02),
        "router_w": nrm((D_MODEL, N_EXPERTS), D_MODEL ** -0.5),
        "router_b": nrm((N_EXPERTS,), 0.01),
        "moe_w_gate": nrm((L, N_EXPERTS, D_MODEL, D_EXPERT), D_MODEL ** -0.5),
        "moe_w_up": nrm((L, N_EXPERTS, D_MODEL, D_EXPERT), D_MODEL ** -0.5),
        "moe_w_down": nrm((L, N_EXPERTS, D_EXPERT, D_MODEL), D_EXPERT ** -0.5 * DN_BETA),
        "ln_moe_g": gain((L, D_MODEL)),
        "ln_moe_b": nrm((L, D_MODEL), 0.02),
    }

def reference(x, mem, mix_w_in, gdn_conv_w, gdn_a_log, gdn_dt_bias, gdn_norm_w,
              ssd_conv_w, ssd_conv_b, ssd_a_log, ssd_dt_bias, ssd_d, ssd_norm_w,
              w_proj_gdn, w_proj_ssd, w_proj_ret, mix_w_out, ln_mix_g, ln_mix_b,
              xa_w_q, xa_w_k, xa_w_v, xa_w_o, ln_xa_g, ln_xa_b,
              router_w, router_b, moe_w_gate, moe_w_up, moe_w_down, ln_moe_g, ln_moe_b):
    seq = x.shape[1]
    pos = jnp.arange(seq, dtype=jnp.float32)
    inv_freq = ROPE_BASE ** (-jnp.arange(0, RET_DK, 2, dtype=jnp.float32) / RET_DK)
    ang = pos[:, None] * inv_freq[None, :]
    cos, sin = jnp.cos(ang), jnp.sin(ang)
    for l in range(DEPTH):
        mix = hybrid_mixer(x, mix_w_in[l], gdn_conv_w[l], gdn_a_log[l], gdn_dt_bias[l], gdn_norm_w[l],
                           ssd_conv_w[l], ssd_conv_b[l], ssd_a_log[l], ssd_dt_bias[l], ssd_d[l],
                           ssd_norm_w[l], w_proj_gdn[l], w_proj_ssd[l], w_proj_ret[l], mix_w_out[l],
                           cos, sin)
        x = layer_norm(DN_ALPHA * x + mix, ln_mix_g[l], ln_mix_b[l])
        xa = memory_cross_attention(x, mem, xa_w_q[l], xa_w_k[l], xa_w_v[l], xa_w_o[l])
        x = layer_norm(DN_ALPHA * x + xa, ln_xa_g[l], ln_xa_b[l])
        ff = moe_ffn(x, router_w, router_b, moe_w_gate[l], moe_w_up[l], moe_w_down[l])
        x = layer_norm(DN_ALPHA * x + ff, ln_moe_g[l], ln_moe_b[l])
    return x


_drawn_inputs = setup_inputs


def setup_inputs(seed=0):
    import zlib

    import numpy as np

    out = dict(_drawn_inputs(seed))
    spreads = {}
    factors = {'gdn_norm_w': 11.147,
     'ssd_d': 10.702,
     'ssd_norm_w': 8.765,
     'ln_moe_g': 21.318,
     'ln_moe_b': 22.303}
    for name, (base, spread) in spreads.items():
        noise = np.random.default_rng([zlib.crc32(name.encode()), seed]).standard_normal(out[name].shape)
        drawn = base * np.exp(spread * noise) if base else spread * noise
        out[name] = jnp.asarray(drawn.astype(out[name].dtype))
    for name, factor in factors.items():
        out[name] = (out[name] * factor).astype(out[name].dtype)
    return out
```

```python
import concourse.bass as bass
from concourse import mybir
from contextlib import ExitStack
import numpy as np

D = 1024
S = 512
P = 128
KT = D // P
NT = S // P
GH = 8
SG, SR = 4, 4
SH = SG * SR
RH = 4
NE = 16
F = 512
MEM = 256
XH = 4
ALPHA = 2.0 ** 0.25
LN_EPS, RMS_EPS = 1e-5, 1e-6
NOV = 7
NB = NE + NOV
LEVELS = 7
NEG = -1e30
C_GQKV, C_GZ, C_GA, C_GB = 0, 3072, 4096, 4104
C_SX, C_SB, C_SC, C_SZ, C_SDT = 4112, 5136, 5648, 6160, 7184
C_RQ, C_RK, C_RV, C_RG, C_GATE = 7200, 7712, 8224, 9248, 10272
K_ID, K_U, K_L, K_ONE, K_NEG, K_MASK = 0, 128, 256, 384, 512, 640
K_RDEC = K_MASK + LEVELS * 128
K_RKW = K_RDEC + RH * 128
K_RCUM = K_RKW + RH
K_COS = K_RCUM + RH
K_SIN = K_COS + NT * 64
K_RTOT = K_SIN + NT * 64
K_SLOT = K_RTOT + RH
K_TOK = K_SLOT + 128
K_END = K_TOK + NT


def shape_constants():
    f = np.float32
    i = np.arange(P)
    c = np.zeros((P, K_END), f)
    c[:, K_ID:K_ID + P] = np.eye(P)
    c[:, K_U:K_U + P] = i[:, None] <= i[None, :]
    c[:, K_L:K_L + P] = i[:, None] > i[None, :]
    c[:, K_ONE:K_ONE + P] = 1.0
    c[:, K_NEG:K_NEG + P] = np.where(i[None, :] >= i[:, None], 0.0, NEG)
    for l in range(LEVELS):
        b = 1 << l
        same = (i[:, None] // (2 * b)) == (i[None, :] // (2 * b))
        c[:, K_MASK + l * P:K_MASK + (l + 1) * P] = same & ((i[:, None] // b) % 2 == 0) & ((i[None, :] // b) % 2 == 1)
    for h in range(RH):
        lg = np.log1p(-np.exp2(f(-5.0 - h))).astype(f)
        d = (i[None, :] - i[:, None]).astype(f)
        c[:, K_RDEC + h * P:K_RDEC + (h + 1) * P] = np.where(d >= 0, np.exp(np.minimum(d, P) * lg * (d >= 0)), 0.0)
        c[:, K_RKW + h] = np.exp(lg * (P - 1 - i))
        c[:, K_RCUM + h] = np.exp(lg * (i + 1))
        c[:, K_RTOT + h] = np.exp(lg * P)
    inv = (f(10000.0) ** (-np.arange(0, P, 2, dtype=f) / f(P))).astype(f)
    ang = (np.arange(S, dtype=f)[:, None] * inv[None, :]).astype(f)
    for n in range(NT):
        c[:, K_COS + n * 64:K_COS + (n + 1) * 64] = np.cos(ang[n * P:(n + 1) * P])
        c[:, K_SIN + n * 64:K_SIN + (n + 1) * 64] = np.sin(ang[n * P:(n + 1) * P])
        c[:, K_TOK + n] = n * P + i
    c[:, K_SLOT:K_SLOT + P] = i[None, :]
    return c


class Count:

    def __init__(self, eng, sem, per, turn=0, base=0):
        self.eng, self.sem, self.n, self.per, self.turn, self.base = eng, sem, 0, per, turn, base

    def __call__(self, ins):
        self.n += 1
        ins.then_inc(self.sem, 1)
        self.eng.wait_ge(self.sem, self.turn * self.per + (self.base + self.n))

    def done(self):
        assert self.n == self.per, (self.n, self.per)


def program(nc, t, out, x2_dram, y_dram):
    f32, bf16, i32 = mybir.dt.float32, mybir.dt.bfloat16, mybir.dt.int32
    ALU, ACT, AX = mybir.AluOpType, mybir.ActivationFunctionType, mybir.AxisListType
    ds = bass.ds
    ctx = ExitStack()
    with ctx:
        def sb(name, shape, dt=f32):
            return ctx.enter_context(nc.sbuf_tensor(name, shape, dt))

        def sem(name):
            return ctx.enter_context(nc.semaphore(name))

        cst = sb("cst", [P, K_END])
        ident = cst[:, K_ID:K_ID + P]
        identb = sb("identb", [P, P], bf16)
        negb = sb("negb", [P, NT, P], bf16)
        xres = sb("xres", [P, NT, D])
        par = sb("par", [P, 64])
        cw_g = sb("cw_g", [P, 4, 24])
        cw_s = sb("cw_s", [P, 4, 16])
        cb_s = sb("cb_s", [P, 16])
        nw_g = sb("nw_g", [P, 1])
        nw_s = sb("nw_s", [P, KT])
        half = sb("half", [P, 40])
        la = sb("la", [P, NT, 24])
        sp = sb("sp", [P, NT, 24])
        beta = sb("beta", [P, NT, 8])
        ecum = sb("ecum", [P, NT, 24])
        ekw = sb("ekw", [P, NT, 24])
        etot = sb("etot", [P, NT, 24])
        becum = sb("becum", [P, NT, 8])
        r_g = sb("r_g", [P, 2, NT])
        r_slot = sb("r_slot", [P, 2, NT], i32)
        r_idx = sb("r_idx", [P, NB], i32)
        r_tab = sb("r_tab", [1, 8], i32)
        upper = ExitStack()

        def ub_(name, shape, dt=f32):
            return upper.enter_context(nc.sbuf_tensor(name, shape, dt))

        xT = ub_("xT", [P, KT, S])
        ring = ub_("ring", [P, 6, KT, P])
        yT = ub_("yT", [P, 3, KT, S])
        psum = [ctx.enter_context(nc.psum_tensor(f"bank{i}", [P, 512], f32)) for i in range(8)]

        w_loaded = [sem(f"w_loaded{i}") for i in range(6)]
        w_free = [sem(f"w_free{i}") for i in range(6)]
        uses = [0] * 6
        g_ready = [sem(f"gemm_ready{i}") for i in range(2)]
        g_free = [sem(f"gemm_free{i}") for i in range(2)]
        units = [0, 0]

        sp_turn = sem("sp_turn")
        phase_sems = []

        def sem(name):
            phase_sems.append(nc.alloc_semaphore(name=name))
            return phase_sems[-1]

        def end_phase():
            nc.clear_and_free_semaphores(phase_sems)
            nc.all_engine_barrier()
            phase_sems.clear()

        w_in = t["mix_w_in"][0]

        def w_cols(w, c0, n):
            return w[:, ds(c0, n)].rearrange("(k p) c -> p k c", p=P)

        def v3(ap, n=NT):
            return ap.rearrange("p (n c) -> p n c", n=n)

        with ExitStack() as c2:
            x_tok = xres
            wsm = c2.enter_context(nc.sbuf_tensor("wsm", [P, KT, 32], f32))
            sm = c2.enter_context(nc.sbuf_tensor("sm", [P, 12, NT, 24], f32))
            bsm = c2.enter_context(nc.sbuf_tensor("bsm", [P, 2, NT, 8], f32))
            nea = c2.enter_context(nc.sbuf_tensor("nea", [P, 24], f32))
            s_x, s_cst, s_par = sem("x_in"), sem("cst_in"), sem("par_in")
            s_xt, s_xtf, s_sm = sem("xT_psum"), sem("xT_done"), sem("small_psum")
            s_v, s_a, s_cum, s_half = sem("in_dve"), sem("in_act"), sem("cum_psum"), sem("half_set")
            with nc.Block() as block:
                @block.sync
                def _(sp_):
                    sp_.dma_start(cst[:, :], t["consts"]).then_inc(s_cst, 16)
                    for n in range(NT):
                        sp_.dma_start(x_tok[:, n, :], t["x"][0, n * P:(n + 1) * P, :]).then_inc(s_x, 16)
                    sp_.dma_start(wsm[:, :, 0:8], w_cols(w_in, C_GA, 8)).then_inc(s_par, 16)
                    sp_.dma_start(wsm[:, :, 8:24], w_cols(w_in, C_SDT, 16)).then_inc(s_par, 16)
                    sp_.dma_start(wsm[:, :, 24:32], w_cols(w_in, C_GB, 8)).then_inc(s_par, 16)
                    sp_.dma_start(par[:, :], t["par_rows"]).then_inc(s_par, 16)
                    sp_.dma_start(cw_g[:, :, :], t["conv_g"]).then_inc(s_par, 16)
                    sp_.dma_start(cw_s[:, :, :], t["conv_s"]).then_inc(s_par, 16)
                    sp_.dma_start(cb_s[:, :], t["convb_s"]).then_inc(s_par, 16)
                    sp_.dma_start(nw_g[:, :], t["norm_g"]).then_inc(s_par, 16)
                    sp_.dma_start(nw_s[:, :], t["norm_s"]).then_inc(s_par, 16)

                @block.gpsimd
                def _(pool):
                    nc.gpsimd.memset(half[:, :], -0.5).then_inc(s_half, 1)

                @block.tensor
                def _(pe):
                    pe.wait_ge(s_cst, 16)
                    pe.wait_ge(s_x, 16 * NT)
                    for k in range(KT):
                        if k >= 4:
                            pe.wait_ge(s_xtf, k - 3)
                        for n in range(NT):
                            ins = nc.tensor.transpose(psum[k % 4][:, n * P:(n + 1) * P], x_tok[:, n, k * P:(k + 1) * P], ident)
                        ins.then_inc(s_xt, 1)
                    pe.wait_ge(s_par, 16 * 9)
                    pe.wait_ge(s_xtf, KT)
                    for n in range(NT):
                        for k in range(KT):
                            ins = nc.tensor.matmul(psum[4][:, n * 32:(n + 1) * 32], xT[:, k, n * P:(n + 1) * P], wsm[:, k, :],
                                                   start=(k == 0), stop=(k == KT - 1))
                    ins.then_inc(s_sm, 1)
                    pe.wait_ge(s_cum, 1)
                    for n in range(NT):
                        nc.tensor.matmul(psum[5][:, n * 24:(n + 1) * 24], cst[:, K_U:K_U + P], la[:, n, :], start=True, stop=True)
                        ins = nc.tensor.matmul(psum[6][:, n * 24:(n + 1) * 24], cst[:, K_ONE:K_ONE + P], la[:, n, :], start=True, stop=True)
                    ins.then_inc(s_sm, 1)

                small = psum[4][:, 0:128].rearrange("p (n c) -> p n c", n=NT)
                cum_ps = psum[5][:, 0:96].rearrange("p (n c) -> p n c", n=NT)
                tot_ps = psum[6][:, 0:96].rearrange("p (n c) -> p n c", n=NT)

                @block.vector
                def _(dve):
                    link = Count(dve, s_v, 0)
                    for b in range(2):
                        dve.sem_inc(g_free[b], 1)
                    for k in range(KT):
                        dve.wait_ge(s_xt, k + 1)
                        nc.vector.tensor_copy(xT[:, k, :], psum[k % 4][:, :]).then_inc(s_xtf, 1)
                    dve.wait_ge(s_par, 16 * 9)
                    nc.vector.tensor_copy(identb[:, :], ident)
                    nc.vector.tensor_copy(negb[:, :, :], cst[:, K_NEG:K_NEG + P].unsqueeze(1).to_broadcast([P, NT, P]))
                    nc.vector.tensor_scalar(cw_g[:, :, :], cw_g[:, :, :], 0.5, None, ALU.mult)
                    nc.vector.tensor_scalar(cw_s[:, :, :], cw_s[:, :, :], 0.5, None, ALU.mult)
                    nc.vector.tensor_scalar(cb_s[:, :], cb_s[:, :], 0.5, None, ALU.mult)
                    dve.wait_ge(s_sm, 1)
                    z, m, neg, u, w, d, d0, dd, r, lnw, v, v2 = [sm[:, j] for j in range(12)]
                    nc.vector.tensor_scalar(bsm[:, 0], small[:, :, 24:32], -1.0, None, ALU.mult)
                    link(nc.vector.tensor_tensor(z, small[:, :, 0:24], par[:, 24:48].unsqueeze(1).to_broadcast([P, NT, 24]), ALU.add))
                    link(nc.vector.tensor_scalar(m, z, 0.0, None, ALU.max))
                    link(nc.vector.scalar_tensor_tensor(out=neg, in0=z, scalar=0.0, in1=m, op0=ALU.min, op1=ALU.subtract))
                    dve.wait_ge(s_a, 3)
                    link(nc.vector.tensor_scalar(w, u, 1.0, None, ALU.add))
                    link(nc.vector.tensor_scalar(d, w, -1.0, None, ALU.add))
                    link(nc.vector.tensor_scalar(d0, d, 0.0, None, ALU.is_equal))
                    link(nc.vector.tensor_tensor(dd, d, d0, ALU.add))
                    link(nc.vector.reciprocal(r, dd))
                    link(nc.vector.tensor_tensor(r, r, u, ALU.mult))
                    dve.wait_ge(s_a, 4)
                    link(nc.vector.tensor_tensor(v, lnw, r, ALU.mult))
                    link(nc.vector.tensor_tensor(v2, u, d0, ALU.mult))
                    link(nc.vector.tensor_tensor(v, v, v2, ALU.add))
                    link(nc.vector.tensor_tensor(sp[:, :, :], v, m, ALU.add))
                    link(nc.vector.tensor_tensor(la[:, :, :], sp[:, :, :], nea[:, :].unsqueeze(1).to_broadcast([P, NT, 24]), ALU.mult))
                    nc.vector.tensor_scalar(la[:, :, :], la[:, :, :], -1.0, None, ALU.mult).then_inc(s_cum, 1)
                    link(nc.vector.tensor_scalar(bsm[:, 0], bsm[:, 1], 1.0, None, ALU.add))
                    link(nc.vector.reciprocal(beta[:, :, :], bsm[:, 0]))
                    dve.wait_ge(s_sm, 2)
                    link(nc.vector.tensor_copy(z, cum_ps))
                    nc.vector.tensor_tensor(v, tot_ps, z, ALU.subtract).then_inc(s_cum, 1)
                    dve.wait_ge(s_a, 7)
                    nc.vector.tensor_tensor(becum[:, :, :], beta[:, :, :], ecum[:, :, 0:8], ALU.mult)

                @block.scalar
                def _(act):
                    act.wait_ge(s_v, 3)
                    nc.scalar.activation(sm[:, 3], sm[:, 2], ACT.Exp).then_inc(s_a, 1)
                    nc.scalar.activation(bsm[:, 1], bsm[:, 0], ACT.Exp).then_inc(s_a, 1)
                    nc.scalar.activation(nea[:, :], par[:, 0:24], ACT.Exp).then_inc(s_a, 1)
                    act.wait_ge(s_v, 4)
                    nc.scalar.activation(sm[:, 9], sm[:, 4], ACT.Ln).then_inc(s_a, 1)
                    act.wait_ge(s_cum, 2)
                    nc.scalar.activation(ekw[:, :, :], sm[:, 10], ACT.Exp).then_inc(s_a, 1)
                    nc.scalar.activation(ecum[:, :, :], cum_ps, ACT.Exp).then_inc(s_a, 1)
                    nc.scalar.activation(etot[:, :, :], tot_ps, ACT.Exp).then_inc(s_a, 1)

        end_phase()
        with ExitStack() as c2:
            def b2(name, shape, dt=f32):
                return c2.enter_context(nc.sbuf_tensor("r_" + name, shape, dt))

            t1, t2 = b2("t1", [P, NT, 2, 64]), b2("t2", [P, NT, 2, 64])
            qr, kr, qd, kd = [b2(n_, [P, NT, P]) for n_ in ("qr", "kr", "qd", "kd")]
            kT, qT, qdT, M = [b2(n_, [P, S]) for n_ in ("kT", "qT", "qdT", "M")]
            v = b2("v", [P, NT, 2, P])
            gh, gt, sg = b2("gh", [P, 2, S]), b2("gt", [P, 2, S]), b2("sg", [P, 2, S])
            St = b2("St", [P, 3, 2 * P])
            bn, mv = b2("bn", [P, NT, 6]), b2("mv", [P, NT, 2])
            var, rs = b2("var", [P, NT]), b2("rs", [P, NT])
            on = b2("on", [P, NT, 2, P])
            names = ("rot rot_done kd_done tokT_psum tokT_done score_psum m_done v_done gh_done gt_done sg_done kv_psum state o_psum "
                     "stat stat_all rs_in rs_out on_ready oT_psum y_done").split()
            q_ = {n_: sem("r_" + n_) for n_ in names}
            ub, us = list(units), list(uses)

            with nc.Block() as block:
                @block.sync
                def _(sp_):
                    with sp_.Fori(0, RH) as i:
                        for j in range(6):
                            col = (C_RQ + i * P, C_RK + i * P, C_RV + i * 256, C_RV + P + i * 256, C_RG + i * 256, C_RG + P + i * 256)[j]
                            sp_.wait_ge(w_free[j], i + us[j])
                            sp_.sem_inc(sp_turn, 1)
                            sp_.dma_start(ring[:, j], w_cols(w_in, col, P)).then_inc(w_loaded[j], 16)

                @block.tensor
                def _(pe):
                    with pe.Fori(0, RH) as i:
                        for j in range(6):
                            b = j % 2
                            pe.wait_ge(w_loaded[j], (i + (us[j] + 1)) * 16)
                            pe.wait_ge(g_free[b], i * 3 + (ub[b] + j // 2 + 1))
                            if j < 4:
                                for n in range(NT):
                                    for k in range(KT):
                                        ins = nc.tensor.matmul(psum[b][:, n * P:(n + 1) * P], xT[:, k, n * P:(n + 1) * P], ring[:, j, k, :],
                                                               start=(k == 0), stop=(k == KT - 1))
                            else:
                                for k in range(KT):
                                    ins = nc.tensor.matmul(psum[b][:, :], ring[:, j, k, :], xT[:, k, :], start=(k == 0), stop=(k == KT - 1))
                            ins.then_inc(g_ready[b], 1)
                            pe.wait_ge(g_ready[b], i * 3 + (ub[b] + j // 2 + 1))
                            pe.sem_inc(w_free[j], 1)
                        for j, src in enumerate((kr, qr, qd)):
                            pe.wait_ge(q_["rot_done"], i * 3 + (2, 1, 3)[j])
                            for n in range(NT):
                                ins = nc.tensor.transpose(psum[2 + j][:, n * P:(n + 1) * P], src[:, n, :], ident)
                            ins.then_inc(q_["tokT_psum"], 1)
                        pe.wait_ge(q_["tokT_done"], i * 3 + 3)
                        for n in range(NT):
                            c = slice(n * P, (n + 1) * P)
                            ins = nc.tensor.matmul(psum[2][:, c], kT[:, c], qT[:, c], start=True, stop=True)
                        ins.then_inc(q_["score_psum"], 1)
                        pe.wait_ge(q_["v_done"], i * 2 + 2)
                        pe.wait_ge(q_["kd_done"], i + 1)
                        for n in range(NT - 1):
                            bank, c0 = psum[3 + n // 2], (n % 2) * 256
                            ins = nc.tensor.matmul(bank[:, c0:c0 + 256], kd[:, n, :], v[:, n].rearrange("p a c -> p (a c)"), start=True, stop=True)
                        ins.then_inc(q_["kv_psum"], 1)
                        pe.wait_ge(q_["m_done"], i + 1)
                        pe.wait_ge(q_["state"], i * 3 + 3)
                        for n in range(NT):
                            c = slice(n * P, (n + 1) * P)
                            bank, c0 = psum[6 + n // 2], (n % 2) * 256
                            if n:
                                nc.tensor.matmul(bank[:, c0:c0 + 256], qdT[:, c], St[:, n - 1, :], start=True, stop=False)
                            ins = nc.tensor.matmul(bank[:, c0:c0 + 256], M[:, c], v[:, n].rearrange("p a c -> p (a c)"), start=(n == 0), stop=True)
                        ins.then_inc(q_["o_psum"], 1)
                        pe.wait_ge(q_["on_ready"], i + 1)
                        for a in range(2):
                            for n in range(NT):
                                ins = nc.tensor.transpose(psum[3 + a][:, n * P:(n + 1) * P], on[:, n, a, :], ident)
                            ins.then_inc(q_["oT_psum"], 1)
                        pe.wait_ge(q_["y_done"], i * 2 + 2)

                @block.scalar
                def _(act):
                    with act.Fori(0, RH) as i:
                        for a in range(2):
                            act.wait_ge(g_ready[a], i * 3 + (ub[a] + 2))
                            nc.scalar.activation(v[:, :, a, :], v3(psum[a][:, :]), ACT.Copy).then_inc(q_["v_done"], 1)
                            act.wait_ge(q_["v_done"], i * 2 + (a + 1))
                            act.sem_inc(g_free[a], 1)
                        for a in range(2):
                            act.wait_ge(g_ready[a], i * 3 + (ub[a] + 3))
                            nc.scalar.activation(gh[:, a, :], psum[a][:, :], ACT.Copy, scale=0.5).then_inc(q_["gh_done"], 1)
                            nc.scalar.activation(gt[:, a, :], psum[a][:, :], ACT.Tanh, scale=0.5).then_inc(q_["gt_done"], 1)
                            act.wait_ge(q_["gt_done"], i * 2 + (a + 1))
                            act.sem_inc(g_free[a], 1)
                        for j, (dst, sc) in enumerate(((kT, P ** -0.5), (qT, 1.0), (qdT, 1.0))):
                            act.wait_ge(q_["tokT_psum"], i * 3 + (j + 1))
                            nc.scalar.activation(dst[:, :], psum[2 + j][:, :], ACT.Copy, scale=sc).then_inc(q_["tokT_done"], 1)
                        act.wait_ge(q_["y_done"], i * 2 + 2)

                @block.gpsimd
                def _(pool):
                    with pool.Fori(0, RH) as i:
                        pool.wait_ge(q_["rs_in"], i + 1)
                        nc.gpsimd.tensor_tensor(rs[:, :], var[:, :], half[:, 0:NT], ALU.pow).then_inc(q_["rs_out"], 1)
                        pool.wait_ge(q_["y_done"], i * 2 + 2)

                @block.vector
                def _(dve):
                    cos = cst[:, K_COS:K_COS + NT * 64].rearrange("p (n c) -> p n c", n=NT).unsqueeze(2).to_broadcast([P, NT, 2, 64])
                    sin = cst[:, K_SIN:K_SIN + NT * 64].rearrange("p (n c) -> p n c", n=NT).unsqueeze(2).to_broadcast([P, NT, 2, 64])
                    with dve.Fori(0, RH) as i:
                        for j, dst in enumerate((qr, kr)):
                            dve.wait_ge(g_ready[j], i * 3 + (ub[j] + 1))
                            ps = psum[j][:, :].rearrange("p (n a c) -> p n a c", n=NT, a=2)
                            nc.vector.tensor_tensor(t1[:, :, :, :], ps, cos, ALU.mult).then_inc(q_["rot"], 1)
                            nc.vector.tensor_tensor(t2[:, :, :, :], ps, sin, ALU.mult).then_inc(q_["rot"], 1)
                            dve.wait_ge(q_["rot"], i * 6 + (3 * j + 2))
                            dve.sem_inc(g_free[j], 1)
                            nc.vector.tensor_tensor(dst[:, :, 0:64], t1[:, :, 0, :], t2[:, :, 1, :], ALU.subtract).then_inc(q_["rot"], 1)
                            nc.vector.tensor_tensor(dst[:, :, 64:128], t1[:, :, 1, :], t2[:, :, 0, :], ALU.add).then_inc(q_["rot_done"], 1)
                            dve.wait_ge(q_["rot_done"], i * 3 + (j + 1))
                            dve.wait_ge(q_["rot"], i * 6 + (3 * j + 3))
                        nc.vector.tensor_scalar(qd[:, :, :], qr[:, :, :], cst[:, ds(i + K_RCUM, 1)], None, ALU.mult).then_inc(q_["rot_done"], 1)
                        nc.vector.tensor_scalar(kd[:, :, :], kr[:, :, :], cst[:, ds(i + K_RKW, 1)], P ** -0.5, ALU.mult, ALU.mult).then_inc(q_["kd_done"], 1)
                        dve.wait_ge(q_["score_psum"], i + 1)
                        nc.vector.tensor_tensor(v3(M[:, :]), v3(psum[2][:, :]), cst[:, ds(i * P + K_RDEC, P)].unsqueeze(1).to_broadcast([P, NT, P]),
                                                ALU.mult).then_inc(q_["m_done"], 1)
                        dve.wait_ge(q_["kv_psum"], i + 1)
                        for n in range(NT - 1):
                            kv = psum[3 + n // 2][:, (n % 2) * 256:(n % 2) * 256 + 256]
                            if n == 0:
                                nc.vector.tensor_copy(St[:, 0, :], kv).then_inc(q_["state"], 1)
                            else:
                                dve.wait_ge(q_["state"], i * 3 + n)
                                nc.vector.scalar_tensor_tensor(out=St[:, n, :], in0=St[:, n - 1, :], scalar=cst[:, ds(i + K_RTOT, 1)], in1=kv,
                                                               op0=ALU.mult, op1=ALU.add).then_inc(q_["state"], 1)
                        dve.wait_ge(q_["o_psum"], i + 1)
                        for n in range(NT):
                            nc.vector.bn_stats(bn[:, n, :], psum[6 + n // 2][:, (n % 2) * 256:(n % 2) * 256 + 256]).then_inc(q_["stat"], 1)
                        dve.wait_ge(q_["stat"], i * 8 + 4)
                        dve.sem_inc(q_["stat_all"], 1)
                        for n in range(NT):
                            nc.vector.bn_aggr(mv[:, n, :], bn[:, n, :]).then_inc(q_["stat"], 1)
                        dve.wait_ge(q_["stat"], i * 8 + 8)
                        nc.vector.tensor_scalar(var[:, :], mv[:, :, 1], LN_EPS, None, ALU.add).then_inc(q_["rs_in"], 1)
                        dve.wait_ge(q_["rs_out"], i + 1)
                        for n in range(NT):
                            ins = nc.vector.tensor_scalar(on[:, n].rearrange("p a c -> p (a c)"), psum[6 + n // 2][:, (n % 2) * 256:(n % 2) * 256 + 256],
                                                          mv[:, n, 0:1], rs[:, n:n + 1], ALU.subtract, ALU.mult)
                        ins.then_inc(q_["on_ready"], 1)
                        for a in range(2):
                            dve.wait_ge(q_["gt_done"], i * 2 + (a + 1))
                            nc.vector.scalar_tensor_tensor(out=sg[:, a, :], in0=gt[:, a, :], scalar=1.0, in1=gh[:, a, :], op0=ALU.add, op1=ALU.mult).then_inc(q_["sg_done"], 1)
                        dve.wait_ge(q_["sg_done"], i * 2 + 2)
                        for a in range(2):
                            dve.wait_ge(q_["oT_psum"], i * 2 + (a + 1))
                            nc.vector.tensor_tensor(yT[:, 2, ds(i * 2 + a, 1), :].rearrange("p a c -> p (a c)"), psum[3 + a][:, :], sg[:, a, :], ALU.mult).then_inc(q_["y_done"], 1)
            for j in range(6):
                uses[j] += RH
            units[0] += 3 * RH
            units[1] += 3 * RH

        end_phase()
        with ExitStack() as c2:
            def b2(name, shape, dt=f32):
                return c2.enter_context(nc.sbuf_tensor("s_" + name, shape, dt))

            acc, th, fm = b2("acc", [P, 4, S]), b2("th", [P, 4, S]), b2("fm", [P, 4, S])
            zh, zt, sz = b2("zh", [P, NT, 2, P]), b2("zt", [P, NT, 2, P]), b2("sz", [P, NT, 2, P])
            xs, bt = b2("xs", [P, NT, 2, P]), b2("bt", [P, NT, P])
            v, vk, y = b2("v", [P, NT, 256]), b2("vk", [P, NT, 256]), b2("y", [P, NT, 256])
            lla, dec, M = b2("lla", [P, SR, NT, P]), b2("dec", [P, SR, S]), b2("M", [P, SR, S])
            St, ts = b2("St", [P, 3, 256]), b2("ts", [P, 2, 256])
            yi = b2("yi", [P, 3, 256])
            ssq, rs = b2("ssq", [P, NT]), b2("rs", [P, NT])
            names = ("conv_acc conv_th conv_fm fm_done cv zh_done zt_done sz_done tok_psum tok_done lla_ready dec_psum dec_ready score_psum m_done "
                     "v_done vk_done kv_psum st state y_psum yw sq_done rs_in rs_out on_ready oT_psum y_done").split()
            q_ = {n_: sem("s_" + n_) for n_ in names}
            ub, us = list(units), list(uses)

            with nc.Block() as block:
                @block.sync
                def _(sp_):
                    with sp_.Fori(0, SG) as i:
                        for j in range(6):
                            col = (C_SX + i * 256, C_SX + P + i * 256, C_SB + i * P, C_SC + i * P, C_SZ + i * 256, C_SZ + P + i * 256)[j]
                            sp_.wait_ge(w_free[j], i + us[j])
                            sp_.sem_inc(sp_turn, 1)
                            sp_.dma_start(ring[:, j], w_cols(w_in, col, P)).then_inc(w_loaded[j], 16)

                @block.tensor
                def _(pe):
                    with pe.Fori(0, SG) as i:
                        for j in range(6):
                            b = j % 2
                            pe.wait_ge(w_loaded[j], (i + (us[j] + 1)) * 16)
                            pe.wait_ge(g_free[b], i * 3 + (ub[b] + j // 2 + 1))
                            if j >= 4:
                                for n in range(NT):
                                    for k in range(KT):
                                        ins = nc.tensor.matmul(psum[b][:, n * P:(n + 1) * P], xT[:, k, n * P:(n + 1) * P], ring[:, j, k, :],
                                                               start=(k == 0), stop=(k == KT - 1))
                            else:
                                for k in range(KT):
                                    ins = nc.tensor.matmul(psum[b][:, :], ring[:, j, k, :], xT[:, k, :], start=(k == 0), stop=(k == KT - 1))
                            ins.then_inc(g_ready[b], 1)
                            pe.wait_ge(g_ready[b], i * 3 + (ub[b] + j // 2 + 1))
                            pe.sem_inc(w_free[j], 1)
                        for j in range(3):
                            pe.wait_ge(q_["fm_done"], i * 4 + (j + 1))
                            for n in range(NT):
                                ins = nc.tensor.transpose(psum[2 + j][:, n * P:(n + 1) * P], fm[:, j, n * P:(n + 1) * P], ident)
                            ins.then_inc(q_["tok_psum"], 1)
                        pe.wait_ge(q_["fm_done"], i * 4 + 4)
                        for n in range(NT):
                            c = slice(n * P, (n + 1) * P)
                            ins = nc.tensor.matmul(psum[5][:, c], fm[:, 2, c], fm[:, 3, c], start=True, stop=True)
                        ins.then_inc(q_["score_psum"], 1)
                        for r in range(SR):
                            pe.wait_ge(q_["lla_ready"], i * 4 + (r + 1))
                            if r >= 2:
                                pe.wait_ge(q_["dec_ready"], i * 4 + (r - 1))
                            b = psum[6 + r % 2]
                            for n in range(NT):
                                nc.tensor.matmul(b[:, n * P:(n + 1) * P], lla[:, r, n, :], cst[:, K_U:K_U + P], start=(n == 0), stop=False, skip_group_check=True)
                            nc.tensor.matmul(b[:, :], identb[:, :], negb[:, :, :].rearrange("p n c -> p (n c)"), start=False, stop=True,
                                             skip_group_check=True).then_inc(q_["dec_psum"], 1)
                        pe.wait_ge(q_["tok_done"], i * 3 + 3)
                        pe.wait_ge(q_["vk_done"], i + 1)
                        for n in range(NT - 1):
                            bank, c0 = psum[2 + n // 2], (n % 2) * 256
                            ins = nc.tensor.matmul(bank[:, c0:c0 + 256], bt[:, n, :], vk[:, n, :], start=True, stop=True)
                        ins.then_inc(q_["kv_psum"], 1)
                        pe.wait_ge(q_["m_done"], i * 4 + 4)
                        for n in range(NT):
                            for r in range(SR):
                                c0 = (n % 2) * 256 + r * 64
                                ins = nc.tensor.matmul(psum[6 + n // 2][:, c0:c0 + 64], M[:, r, n * P:(n + 1) * P], v[:, n, r * 64:(r + 1) * 64], start=True, stop=True)
                        ins.then_inc(q_["y_psum"], 1)
                        pe.wait_ge(q_["state"], i * 3 + 3)
                        for n in range(1, NT):
                            c0 = (n % 2) * 256
                            ins = nc.tensor.matmul(psum[4 + n // 2][:, c0:c0 + 256], fm[:, 3, n * P:(n + 1) * P], St[:, n - 1, :], start=True, stop=True)
                        ins.then_inc(q_["y_psum"], 1)
                        pe.wait_ge(q_["on_ready"], i + 1)
                        for a in range(2):
                            for n in range(NT):
                                ins = nc.tensor.transpose(psum[2 + a][:, n * P:(n + 1) * P], vk[:, n, a * P:(a + 1) * P], ident)
                            ins.then_inc(q_["oT_psum"], 1)
                        pe.wait_ge(q_["y_done"], i * 2 + 2)

                @block.scalar
                def _(act):
                    with act.Fori(0, SG) as i:
                        for j in range(4):
                            ch = (i * 2, i * 2 + 1, i + 8, i + 12)[j]
                            act.wait_ge(g_ready[j % 2], i * 3 + (ub[j % 2] + j // 2 + 1))
                            nc.scalar.activation(acc[:, j, :], psum[j % 2][:, :], ACT.Identity, scale=cw_s[:, 3, ds(ch, 1)], bias=cb_s[:, ds(ch, 1)]).then_inc(q_["conv_acc"], 1)
                            act.wait_ge(q_["conv_fm"], i * 4 + (j + 1))
                            nc.scalar.activation(th[:, j, :], acc[:, j, :], ACT.Tanh).then_inc(q_["conv_th"], 1)
                        for a in range(2):
                            act.wait_ge(g_ready[a], i * 3 + (ub[a] + 3))
                            nc.scalar.activation(zh[:, :, a, :], v3(psum[a][:, :]), ACT.Copy, scale=0.5).then_inc(q_["zh_done"], 1)
                            nc.scalar.activation(zt[:, :, a, :], v3(psum[a][:, :]), ACT.Tanh, scale=0.5).then_inc(q_["zt_done"], 1)
                            act.wait_ge(q_["zt_done"], i * 2 + (a + 1))
                            act.sem_inc(g_free[a], 1)
                        for j, dst in enumerate((xs[:, :, 0, :], xs[:, :, 1, :], bt[:, :, :])):
                            act.wait_ge(q_["tok_psum"], i * 3 + (j + 1))
                            nc.scalar.activation(dst, v3(psum[2 + j][:, :]), ACT.Copy).then_inc(q_["tok_done"], 1)
                        for r in range(SR):
                            act.wait_ge(q_["dec_psum"], i * 4 + (r + 1))
                            nc.scalar.activation(dec[:, r, :], psum[6 + r % 2][:, :], ACT.Exp).then_inc(q_["dec_ready"], 1)
                        act.wait_ge(q_["yw"], i * 7 + 7)
                        nc.scalar.activation(v[:, :, :], y[:, :, :], ACT.Square).then_inc(q_["sq_done"], 1)
                        for a in range(2):
                            act.wait_ge(q_["oT_psum"], i * 2 + (a + 1))
                            nc.scalar.activation(yT[:, 1, ds(i * 2 + a, 1), :].rearrange("p a c -> p (a c)"), psum[2 + a][:, :], ACT.Copy,
                                                 scale=nw_s[:, ds(i * 2 + a, 1)]).then_inc(q_["y_done"], 1)
                        act.wait_ge(q_["y_done"], i * 2 + 2)

                @block.gpsimd
                def _(pool):
                    with pool.Fori(0, SG) as i:
                        for r in range(SR):
                            nc.gpsimd.tensor_tensor(lla[:, r], cst[:, K_L:K_L + P].unsqueeze(1).to_broadcast([P, NT, P]),
                                                    la[:, :, ds(i * 4 + (8 + r), 1)].to_broadcast([P, NT, P]), ALU.mult).then_inc(q_["lla_ready"], 1)
                        pool.wait_ge(q_["rs_in"], i + 1)
                        nc.gpsimd.tensor_tensor(rs[:, :], ssq[:, :], half[:, 0:NT], ALU.pow).then_inc(q_["rs_out"], 1)
                        pool.wait_ge(q_["y_done"], i * 2 + 2)

                def heads(ap):
                    return ap.unsqueeze(3).to_broadcast([P, ap.shape[1], 4, 64])

                def r4(ap):
                    return ap.rearrange("p n (r c) -> p n r c", r=4)

                @block.vector
                def _(dve):
                    with dve.Fori(0, SG) as i:
                        link = Count(dve, q_["cv"], 13, i)
                        for j in range(4):
                            ch = (i * 2, i * 2 + 1, i + 8, i + 12)[j]
                            dve.wait_ge(q_["conv_acc"], i * 4 + (j + 1))
                            p = psum[j % 2]
                            for m in (1, 2):
                                link(nc.vector.scalar_tensor_tensor(out=acc[:, j, m:S], in0=p[:, 0:S - m], scalar=cw_s[:, 3 - m, ds(ch, 1)],
                                                                    in1=acc[:, j, m:S], op0=ALU.mult, op1=ALU.add))
                            nc.vector.scalar_tensor_tensor(out=acc[:, j, 3:S], in0=p[:, 0:S - 3], scalar=cw_s[:, 0, ds(ch, 1)],
                                                           in1=acc[:, j, 3:S], op0=ALU.mult, op1=ALU.add).then_inc(q_["conv_fm"], 1)
                            dve.wait_ge(q_["conv_fm"], i * 4 + (j + 1))
                            dve.sem_inc(g_free[j % 2], 1)
                            dve.wait_ge(q_["conv_th"], i * 4 + (j + 1))
                            nc.vector.scalar_tensor_tensor(out=fm[:, j, :], in0=th[:, j, :], scalar=1.0, in1=acc[:, j, :], op0=ALU.add, op1=ALU.mult).then_inc(q_["fm_done"], 1)
                        dve.wait_ge(q_["tok_done"], i * 3 + 3)
                        xs4 = xs[:, :, :, :].rearrange("p n a (b c) -> p n (a b) c", b=2)
                        nc.vector.tensor_tensor(r4(v[:, :, :]), xs4, heads(sp[:, :, ds(i * 4 + 8, 4)]), ALU.mult).then_inc(q_["v_done"], 1)
                        dve.wait_ge(q_["v_done"], i + 1)
                        nc.vector.tensor_tensor(r4(vk[:, :, :]), r4(v[:, :, :]), heads(ekw[:, :, ds(i * 4 + 8, 4)]), ALU.mult).then_inc(q_["vk_done"], 1)
                        dve.wait_ge(q_["score_psum"], i + 1)
                        for r in range(SR):
                            dve.wait_ge(q_["dec_ready"], i * 4 + (r + 1))
                            nc.vector.tensor_tensor(M[:, r, :], psum[5][:, :], dec[:, r, :], ALU.mult).then_inc(q_["m_done"], 1)
                        dve.wait_ge(q_["kv_psum"], i + 1)
                        for n in range(NT - 1):
                            kv = psum[2 + n // 2][:, (n % 2) * 256:(n % 2) * 256 + 256]
                            if n == 0:
                                nc.vector.tensor_copy(St[:, 0, :], kv).then_inc(q_["state"], 1)
                            else:
                                dve.wait_ge(q_["state"], i * 3 + n)
                                link(nc.vector.tensor_tensor(ts[:, n - 1, :].rearrange("p (r c) -> p r c", r=4), St[:, n - 1, :].rearrange("p (r c) -> p r c", r=4),
                                                             etot[:, n, ds(i * 4 + 8, 4)].unsqueeze(2).to_broadcast([P, 4, 64]), ALU.mult))
                                nc.vector.tensor_tensor(St[:, n, :], ts[:, n - 1, :], kv, ALU.add).then_inc(q_["state"], 1)
                        link(nc.vector.tensor_tensor(r4(y[:, :, :]), xs4, heads(par[:, ds(i * 4 + 48, 4)].unsqueeze(1).to_broadcast([P, NT, 4])), ALU.mult))
                        link(nc.vector.scalar_tensor_tensor(out=sz[:, :, :, :].rearrange("p n a c -> p (n a c)"), in0=zt[:, :, :, :].rearrange("p n a c -> p (n a c)"),
                                                            scalar=1.0, in1=zh[:, :, :, :].rearrange("p n a c -> p (n a c)"), op0=ALU.add, op1=ALU.mult))
                        dve.wait_ge(q_["y_psum"], i * 2 + 2)
                        for b in range(2):
                            nc.vector.tensor_tensor(y[:, 2 * b:2 * b + 2, :].rearrange("p n c -> p (n c)"), y[:, 2 * b:2 * b + 2, :].rearrange("p n c -> p (n c)"),
                                                    psum[6 + b][:, :], ALU.add).then_inc(q_["yw"], 1)
                        for n in range(1, NT):
                            nc.vector.tensor_tensor(yi[:, n - 1, :].rearrange("p (r c) -> p r c", r=4), psum[4 + n // 2][:, (n % 2) * 256:(n % 2) * 256 + 256].rearrange("p (r c) -> p r c", r=4),
                                                    ecum[:, n, ds(i * 4 + 8, 4)].unsqueeze(2).to_broadcast([P, 4, 64]), ALU.mult).then_inc(q_["yw"], 1)
                        dve.wait_ge(q_["yw"], i * 7 + 5)
                        nc.vector.tensor_tensor(y[:, 1:NT, :], y[:, 1:NT, :], yi[:, :, :], ALU.add).then_inc(q_["yw"], 1)
                        dve.wait_ge(q_["yw"], i * 7 + 6)
                        nc.vector.tensor_tensor(y[:, :, :], y[:, :, :], sz[:, :, :, :].rearrange("p n a c -> p n (a c)"), ALU.mult).then_inc(q_["yw"], 1)
                        dve.wait_ge(q_["sq_done"], i + 1)
                        link(nc.vector.tensor_reduce(ssq[:, :], v[:, :, :], AX.X, ALU.add))
                        nc.vector.tensor_scalar(ssq[:, :], ssq[:, :], 1.0 / 256, RMS_EPS, ALU.mult, ALU.add).then_inc(q_["rs_in"], 1)
                        dve.wait_ge(q_["rs_out"], i + 1)
                        nc.vector.tensor_tensor(vk[:, :, :], y[:, :, :], rs[:, :].unsqueeze(2).to_broadcast([P, NT, 256]), ALU.mult).then_inc(q_["on_ready"], 1)
                        link.done()
            for j in range(6):
                uses[j] += SG
            units[0] += 3 * SG
            units[1] += 3 * SG

        end_phase()
        with ExitStack() as c2:
            def b2(name, shape, dt=f32):
                return c2.enter_context(nc.sbuf_tensor("g_" + name, shape, dt))

            acc, th = b2("acc", [P, 4, S]), b2("th", [P, 4, S])
            fm = b2("fm", [P, 4, S])
            sq = b2("sq", [P, 3, NT, P])
            ssq, rs = b2("ssq", [P, 12]), b2("rs", [P, 12])
            kn, kb, kbe, kd = [b2(n_, [P, NT, P]) for n_ in ("kn", "kb", "kbe", "kd")]
            qn, qd, vb = [b2(n_, [P, NT, P]) for n_ in ("qn", "qd", "vb")]
            knT, kbT, qnT, qdT = [b2(n_, [P, S]) for n_ in ("knT", "kbT", "qnT", "qdT")]
            lla, dec = b2("lla", [P, NT, P]), b2("dec", [P, S])
            AT, atT = b2("AT", [P, S]), b2("atT", [P, S])
            Cl = b2("Cl", [P, LEVELS, S])
            T, TT, X = b2("T", [P, S]), b2("TT", [P, S]), b2("X", [P, S])
            nwT, vn = b2("nwT", [P, S]), b2("vn", [P, S])
            St = b2("St", [P, 3, P])
            on = b2("on", [P, S])

            names = ("conv_acc conv_th conv_fm fm_done tok_psum tok_norm rs_in rs_out tokT_psum tokT_done lla_ready dec_psum dec_ready "
                     "score_psum score_done cl_ready t0_psum lev_x_psum lev_x lev_y_psum lev_t wT_psum wT_ready vn_psum vn_ready kv_psum state "
                     "o_psum on_ready oT_psum y_done tok_sq g_dve g_lv").split()
            q_ = {n_: sem("g_" + n_) for n_ in names}
            ub = list(units)
            us = list(uses)

            with nc.Block() as block:
                @block.sync
                def _(sp_):
                    with sp_.Fori(0, GH) as i:
                        for j in range(4):
                            sp_.wait_ge(w_free[j], i + us[j])
                            sp_.sem_inc(sp_turn, 1)
                            sp_.dma_start(ring[:, j], w_cols(w_in, (C_GQKV, C_GQKV + 1024, C_GQKV + 2048, C_GZ)[j] + i * P, P)).then_inc(w_loaded[j], 16)

                @block.tensor
                def _(pe):
                    with pe.Fori(0, GH) as i:
                        for j in range(4):
                            pe.wait_ge(w_loaded[j], (i + (us[j] + 1)) * 16)
                            if j < 2:
                                pe.wait_ge(g_free[j % 2], i * 2 + (ub[j % 2] + 1))
                            else:
                                pe.wait_ge(g_free[j % 2], i * 2 + (ub[j % 2] + 2))
                            for k in range(KT):
                                ins = nc.tensor.matmul(psum[j % 2][:, :], ring[:, j, k, :], xT[:, k, :], start=(k == 0), stop=(k == KT - 1))
                            ins.then_inc(g_ready[j % 2], 1)
                            pe.wait_ge(g_ready[j % 2], i * 2 + (ub[j % 2] + j // 2 + 1))
                            pe.sem_inc(w_free[j], 1)
                        for j in range(3):
                            pe.wait_ge(q_["fm_done"], i * 4 + (j + 1))
                            for n in range(NT):
                                ins = nc.tensor.transpose(psum[2 + j][:, n * P:(n + 1) * P], fm[:, j, n * P:(n + 1) * P], ident)
                            ins.then_inc(q_["tok_psum"], 1)
                        pe.wait_ge(q_["lla_ready"], i + 1)
                        for n in range(NT):
                            nc.tensor.matmul(psum[5][:, n * P:(n + 1) * P], lla[:, n, :], cst[:, K_U:K_U + P], start=(n == 0), stop=False, skip_group_check=True)
                        nc.tensor.matmul(psum[5][:, :], identb[:, :], negb[:, :, :].rearrange("p n c -> p (n c)"), start=False, stop=True,
                                         skip_group_check=True).then_inc(q_["dec_psum"], 1)
                        for j, src in enumerate((kn, kb, qn, qd)):
                            pe.wait_ge(q_["tok_norm"], i * 7 + (1, 2, 5, 6)[j])
                            bank = psum[(6, 7, 2, 3)[j]]
                            for n in range(NT):
                                ins = nc.tensor.transpose(bank[:, n * P:(n + 1) * P], src[:, n, :], ident)
                            ins.then_inc(q_["tokT_psum"], 1)
                        pe.wait_ge(q_["tokT_done"], i * 4 + 4)
                        for j, (rhs, bank) in enumerate(((kbT, psum[6]), (qnT, psum[7]))):
                            for n in range(NT):
                                c = slice(n * P, (n + 1) * P)
                                ins = nc.tensor.matmul(bank[:, c], knT[:, c], rhs[:, c], start=True, stop=True)
                            ins.then_inc(q_["score_psum"], 1)
                        pe.wait_ge(q_["lev_t"], i * 13 + 1)
                        for n in range(NT):
                            c = slice(n * P, (n + 1) * P)
                            ins = nc.tensor.transpose(psum[4][:, c], TT[:, c], ident)
                        ins.then_inc(q_["t0_psum"], 1)
                        for l in range(1, LEVELS):
                            pe.wait_ge(q_["cl_ready"], i * 6 + l)
                            pe.wait_ge(q_["lev_t"], i * 13 + 2 * l)
                            for n in range(NT):
                                c = slice(n * P, (n + 1) * P)
                                ins = nc.tensor.matmul(psum[5][:, c], Cl[:, l, c], T[:, c], start=True, stop=True)
                            ins.then_inc(q_["lev_x_psum"], 1)
                            pe.wait_ge(q_["lev_x"], i * 6 + l)
                            for n in range(NT):
                                c = slice(n * P, (n + 1) * P)
                                ins = nc.tensor.matmul(psum[6][:, c], X[:, c], TT[:, c], start=True, stop=True)
                            ins.then_inc(q_["lev_y_psum"], 1)
                            if l < LEVELS - 1:
                                for n in range(NT):
                                    c = slice(n * P, (n + 1) * P)
                                    ins = nc.tensor.matmul(psum[7][:, c], TT[:, c], X[:, c], start=True, stop=True)
                                ins.then_inc(q_["lev_y_psum"], 1)
                        pe.wait_ge(q_["lev_t"], i * 13 + 13)
                        for n in range(NT):
                            c = slice(n * P, (n + 1) * P)
                            ins = nc.tensor.matmul(psum[4][:, c], kbe[:, n, :], TT[:, c], start=True, stop=True)
                        ins.then_inc(q_["wT_psum"], 1)
                        pe.wait_ge(q_["score_done"], i * 2 + 2)
                        for n in range(NT):
                            c = slice(n * P, (n + 1) * P)
                            ins = nc.tensor.matmul(psum[5][:, c], TT[:, c], vb[:, n, :], start=True, stop=(n == 0))
                            if n:
                                pe.wait_ge(q_["wT_ready"], i + 1)
                                pe.wait_ge(q_["state"], i * 3 + n)
                                ins = nc.tensor.matmul(psum[5][:, c], nwT[:, c], St[:, n - 1, :], start=False, stop=True)
                            ins.then_inc(q_["vn_psum"], 1)
                            pe.wait_ge(q_["vn_ready"], i * 4 + (n + 1))
                            if n < NT - 1:
                                nc.tensor.matmul(psum[6][:, c], kd[:, n, :], vn[:, c], start=True, stop=True).then_inc(q_["kv_psum"], 1)
                            if n:
                                nc.tensor.matmul(psum[7][:, c], qdT[:, c], St[:, n - 1, :], start=True, stop=False)
                            ins = nc.tensor.matmul(psum[7][:, c], atT[:, c], vn[:, c], start=(n == 0), stop=True)
                        ins.then_inc(q_["o_psum"], 1)
                        pe.wait_ge(q_["on_ready"], i + 1)
                        for n in range(NT):
                            c = slice(n * P, (n + 1) * P)
                            ins = nc.tensor.transpose(psum[2][:, c], on[:, c], ident)
                        ins.then_inc(q_["oT_psum"], 1)
                        pe.wait_ge(q_["y_done"], i + 1)

                @block.scalar
                def _(act):
                    with act.Fori(0, GH) as i:
                        for j in range(4):
                            act.wait_ge(g_ready[j % 2], i * 2 + (ub[j % 2] + j // 2 + 1))
                            if j < 3:
                                nc.scalar.activation(acc[:, j, :], psum[j % 2][:, :], ACT.Copy, scale=cw_g[:, 3, ds(i + 8 * j, 1)]).then_inc(q_["conv_acc"], 1)
                                act.wait_ge(q_["conv_fm"], i * 3 + (j + 1))
                                nc.scalar.activation(th[:, j, :], acc[:, j, :], ACT.Tanh).then_inc(q_["conv_th"], 1)
                            else:
                                nc.scalar.activation(acc[:, 3, :], psum[1][:, :], ACT.Copy, scale=0.5).then_inc(q_["conv_acc"], 1)
                                nc.scalar.activation(th[:, 3, :], psum[1][:, :], ACT.Tanh, scale=0.5).then_inc(q_["conv_th"], 1)
                                act.wait_ge(q_["conv_th"], i * 4 + 4)
                                act.sem_inc(g_free[1], 1)
                        for j in range(3 - 1):
                            act.wait_ge(q_["tok_psum"], i * 3 + (j + 1))
                            nc.scalar.activation(sq[:, j], v3(psum[2 + j][:, :]), ACT.Square).then_inc(q_["tok_sq"], 1)
                        act.wait_ge(q_["dec_psum"], i + 1)
                        nc.scalar.activation(dec[:, :], psum[5][:, :], ACT.Exp).then_inc(q_["dec_ready"], 1)
                        for j, (dst, b) in enumerate(((knT, 6), (kbT, 7), (qnT, 2), (qdT, 3))):
                            act.wait_ge(q_["tokT_psum"], i * 4 + (j + 1))
                            nc.scalar.activation(dst[:, :], psum[b][:, :], ACT.Copy).then_inc(q_["tokT_done"], 1)
                        for l in range(1, LEVELS):
                            act.wait_ge(q_["lev_x_psum"], i * 6 + l)
                            nc.scalar.activation(X[:, :], psum[5][:, :], ACT.Copy).then_inc(q_["lev_x"], 1)
                        act.wait_ge(q_["wT_psum"], i + 1)
                        nc.scalar.activation(nwT[:, :], psum[4][:, :], ACT.Copy, scale=-1.0).then_inc(q_["wT_ready"], 1)
                        for n in range(NT):
                            c = slice(n * P, (n + 1) * P)
                            act.wait_ge(q_["vn_psum"], i * 4 + (n + 1))
                            nc.scalar.activation(vn[:, c], psum[5][:, c], ACT.Copy).then_inc(q_["vn_ready"], 1)
                        act.wait_ge(q_["o_psum"], i + 1)
                        nc.scalar.activation(sq[:, 2], v3(psum[7][:, :]), ACT.Square).then_inc(q_["tok_sq"], 1)
                        act.wait_ge(q_["y_done"], i + 1)

                @block.gpsimd
                def _(pool):
                    with pool.Fori(0, GH) as i:
                        nc.gpsimd.tensor_tensor(lla[:, :, :], cst[:, K_L:K_L + P].unsqueeze(1).to_broadcast([P, NT, P]),
                                                la[:, :, ds(i, 1)].to_broadcast([P, NT, P]), ALU.mult).then_inc(q_["lla_ready"], 1)
                        pool.wait_ge(q_["rs_in"], i * 2 + 1)
                        nc.gpsimd.tensor_tensor(rs[:, 0:8], ssq[:, 0:8], half[:, 0:8], ALU.pow).then_inc(q_["rs_out"], 1)
                        pool.wait_ge(q_["score_done"], i * 2 + 1)
                        for l in range(1, LEVELS):
                            nc.gpsimd.tensor_tensor(v3(Cl[:, l, :]), v3(AT[:, :]), cst[:, K_MASK + l * P:K_MASK + (l + 1) * P].unsqueeze(1).to_broadcast([P, NT, P]),
                                                    ALU.mult).then_inc(q_["cl_ready"], 1)
                        pool.wait_ge(q_["rs_in"], i * 2 + 2)
                        nc.gpsimd.tensor_tensor(rs[:, 8:12], ssq[:, 8:12], half[:, 0:4], ALU.pow).then_inc(q_["rs_out"], 1)
                        pool.wait_ge(q_["y_done"], i + 1)

                @block.vector
                def _(dve):
                    with dve.Fori(0, GH) as i:
                        link = Count(dve, q_["g_dve"], 9, i)
                        lv = Count(dve, q_["g_lv"], 11, i)
                        for j in range(4):
                            dve.wait_ge(q_["conv_acc"], i * 4 + (j + 1))
                            if j < 3:
                                p = psum[j % 2]
                                for m in (1, 2):
                                    link(nc.vector.scalar_tensor_tensor(out=acc[:, j, m:S], in0=p[:, 0:S - m], scalar=cw_g[:, 3 - m, ds(i + 8 * j, 1)],
                                                                        in1=acc[:, j, m:S], op0=ALU.mult, op1=ALU.add))
                                nc.vector.scalar_tensor_tensor(out=acc[:, j, 3:S], in0=p[:, 0:S - 3], scalar=cw_g[:, 0, ds(i + 8 * j, 1)],
                                                               in1=acc[:, j, 3:S], op0=ALU.mult, op1=ALU.add).then_inc(q_["conv_fm"], 1)
                                dve.wait_ge(q_["conv_fm"], i * 3 + (j + 1))
                                dve.sem_inc(g_free[j % 2], 1)
                            dve.wait_ge(q_["conv_th"], i * 4 + (j + 1))
                            nc.vector.scalar_tensor_tensor(out=fm[:, j, :], in0=th[:, j, :], scalar=1.0, in1=acc[:, j, :], op0=ALU.add, op1=ALU.mult).then_inc(q_["fm_done"], 1)
                        dve.wait_ge(q_["tok_sq"], i * 3 + 2)
                        link(nc.vector.tensor_reduce(ssq[:, 0:8], sq[:, 0:2].rearrange("p a n c -> p (a n) c"), AX.X, ALU.add))
                        link(nc.vector.tensor_scalar(ssq[:, 0:4], ssq[:, 0:4], RMS_EPS, float(P), ALU.add, ALU.mult))
                        nc.vector.tensor_scalar(ssq[:, 4:8], ssq[:, 4:8], RMS_EPS, None, ALU.add).then_inc(q_["rs_in"], 1)
                        dve.wait_ge(q_["tok_psum"], i * 3 + 3)
                        dve.wait_ge(q_["rs_out"], i * 2 + 1)

                        def by(dst, src, scale, w):
                            nc.vector.tensor_tensor(dst[:, :, :], src, scale.to_broadcast([P, NT, P]), ALU.mult).then_inc(q_["tok_norm"], 1)
                            dve.wait_ge(q_["tok_norm"], i * 7 + w)

                        by(kn, v3(psum[3][:, :]), rs[:, 4:8].unsqueeze(2), 1)
                        by(kb, kn[:, :, :], beta[:, :, ds(i, 1)], 2)
                        by(kbe, kn[:, :, :], becum[:, :, ds(i, 1)], 3)
                        by(kd, kn[:, :, :], ekw[:, :, ds(i, 1)], 4)
                        by(qn, v3(psum[2][:, :]), rs[:, 0:4].unsqueeze(2), 5)
                        by(qd, qn[:, :, :], ecum[:, :, ds(i, 1)], 6)
                        by(vb, v3(psum[4][:, :]), beta[:, :, ds(i, 1)], 7)
                        dve.wait_ge(q_["dec_ready"], i + 1)
                        for j, (dst, b) in enumerate(((AT, 6), (atT, 7))):
                            dve.wait_ge(q_["score_psum"], i * 2 + (j + 1))
                            nc.vector.tensor_tensor(dst[:, :], psum[b][:, :], dec[:, :], ALU.mult).then_inc(q_["score_done"], 1)
                        dve.wait_ge(q_["score_done"], i * 2 + 2)
                        lv(nc.vector.tensor_tensor(v3(X[:, :]), v3(AT[:, :]), cst[:, K_MASK:K_MASK + P].unsqueeze(1).to_broadcast([P, NT, P]), ALU.mult))
                        nc.vector.tensor_tensor(v3(TT[:, :]), ident.unsqueeze(1).to_broadcast([P, NT, P]), v3(X[:, :]), ALU.subtract).then_inc(q_["lev_t"], 1)
                        dve.wait_ge(q_["t0_psum"], i + 1)
                        nc.vector.tensor_copy(T[:, :], psum[4][:, :]).then_inc(q_["lev_t"], 1)
                        for l in range(1, LEVELS):
                            dve.wait_ge(q_["lev_y_psum"], i * 11 + 2 * l)if l < LEVELS - 1 else dve.wait_ge(q_["lev_y_psum"], i * 11 + 11)
                            nc.vector.tensor_tensor(TT[:, :], TT[:, :], psum[6][:, :], ALU.subtract).then_inc(q_["lev_t"], 1) if l == LEVELS - 1 else \
                                lv(nc.vector.tensor_tensor(TT[:, :], TT[:, :], psum[6][:, :], ALU.subtract))
                            if l < LEVELS - 1:
                                lv(nc.vector.tensor_tensor(T[:, :], T[:, :], psum[7][:, :], ALU.subtract))
                                dve.sem_inc(q_["lev_t"], 2)
                        for n in range(NT - 1):
                            c = slice(n * P, (n + 1) * P)
                            dve.wait_ge(q_["kv_psum"], i * 3 + (n + 1))
                            if n == 0:
                                nc.vector.tensor_copy(St[:, 0, :], psum[6][:, c]).then_inc(q_["state"], 1)
                            else:
                                dve.wait_ge(q_["state"], i * 3 + n)
                                nc.vector.scalar_tensor_tensor(out=St[:, n, :], in0=St[:, n - 1, :], scalar=etot[:, n, ds(i, 1)], in1=psum[6][:, c],
                                                               op0=ALU.mult, op1=ALU.add).then_inc(q_["state"], 1)
                        dve.wait_ge(q_["tok_sq"], i * 3 + 3)
                        link(nc.vector.tensor_reduce(ssq[:, 8:12], sq[:, 2], AX.X, ALU.add))
                        nc.vector.tensor_scalar(ssq[:, 8:12], ssq[:, 8:12], 1.0 / P, RMS_EPS, ALU.mult, ALU.add).then_inc(q_["rs_in"], 1)
                        dve.wait_ge(q_["rs_out"], i * 2 + 2)
                        nc.vector.tensor_tensor(v3(on[:, :]), v3(psum[7][:, :]), rs[:, 8:12].unsqueeze(2).to_broadcast([P, NT, P]), ALU.mult).then_inc(q_["on_ready"], 1)
                        dve.wait_ge(q_["oT_psum"], i + 1)
                        nc.vector.scalar_tensor_tensor(out=yT[:, 0, ds(i, 1), :].rearrange("p a c -> p (a c)"), in0=psum[2][:, :], scalar=nw_g[:, 0:1], in1=fm[:, 3, :],
                                                       op0=ALU.mult, op1=ALU.mult).then_inc(q_["y_done"], 1)
                        link.done(), lv.done()
            for j in range(4):
                uses[j] += GH
            units[0] += 2 * GH
            units[1] += 2 * GH
        end_phase()
        mT = ub_("mT", [P, KT, S])
        with ExitStack() as c2:
            def b2(name, shape, dt=f32):
                return c2.enter_context(nc.sbuf_tensor("m_" + name, shape, dt))

            gt, pr, s01 = b2("gt", [P, 3, S]), b2("pr", [P, 3, S]), b2("s01", [P, S])
            names = "gate_done pr_done s01_done m_done".split()
            q_ = {n_: sem("m_" + n_) for n_ in names}
            ub, us = list(units), list(uses)
            projs = [t["w_proj_gdn"][0], t["w_proj_ssd"][0], t["w_proj_ret"][0]]

            with nc.Block() as block:
                @block.sync
                def _(sp_):
                    with sp_.Fori(0, KT) as i:
                        for j in range(6):
                            src = w_cols(projs[j // 2], i * P, P) if j % 2 else w_cols(w_in, C_GATE + (j // 2) * D + i * P, P)
                            sp_.wait_ge(w_free[j], i + us[j])
                            sp_.sem_inc(sp_turn, 1)
                            sp_.dma_start(ring[:, j], src).then_inc(w_loaded[j], 16)

                @block.tensor
                def _(pe):
                    with pe.Fori(0, KT) as i:
                        for j in range(6):
                            b = j % 2
                            pe.wait_ge(w_loaded[j], (i + (us[j] + 1)) * 16)
                            pe.wait_ge(g_free[b], i * 3 + (ub[b] + j // 2 + 1))
                            for k in range(KT):
                                rhs = yT[:, j // 2, k, :] if b else xT[:, k, :]
                                ins = nc.tensor.matmul(psum[b][:, :], ring[:, j, k, :], rhs, start=(k == 0), stop=(k == KT - 1))
                            ins.then_inc(g_ready[b], 1)
                            pe.wait_ge(g_ready[b], i * 3 + (ub[b] + j // 2 + 1))
                            pe.sem_inc(w_free[j], 1)

                @block.scalar
                def _(act):
                    with act.Fori(0, KT) as i:
                        for j in range(3):
                            act.wait_ge(g_ready[0], i * 3 + (ub[0] + j + 1))
                            act.wait_ge(q_["pr_done"], i * 3 + (j + 1))
                            nc.scalar.activation(gt[:, j, :], psum[0][:, :], ACT.Tanh, scale=0.5).then_inc(q_["gate_done"], 1)
                            act.wait_ge(q_["gate_done"], i * 3 + (j + 1))
                            act.sem_inc(g_free[0], 1)

                @block.vector
                def _(dve):
                    dve.sem_inc(q_["pr_done"], 3)
                    with dve.Fori(0, KT) as i:
                        for j in range(3):
                            dve.wait_ge(g_ready[1], i * 3 + (ub[1] + j + 1))
                            dve.wait_ge(q_["gate_done"], i * 3 + (j + 1))
                            nc.vector.scalar_tensor_tensor(out=pr[:, j, :], in0=gt[:, j, :], scalar=1.0, in1=psum[1][:, :], op0=ALU.add, op1=ALU.mult).then_inc(q_["pr_done"], 1)
                            dve.wait_ge(q_["pr_done"], i * 3 + (j + 4))
                            dve.sem_inc(g_free[1], 1)
                        nc.vector.tensor_tensor(s01[:, :], pr[:, 0, :], pr[:, 1, :], ALU.add).then_inc(q_["s01_done"], 1)
                        dve.wait_ge(q_["s01_done"], i + 1)
                        nc.vector.tensor_tensor(mT[:, ds(i, 1), :].rearrange("p a c -> p (a c)"), s01[:, :], pr[:, 2, :], ALU.add).then_inc(q_["m_done"], 1)
                        dve.wait_ge(q_["m_done"], i + 1)
            for j in range(6):
                uses[j] += KT
            units[0] += 3 * KT
            units[1] += 3 * KT


        def norm_rows(dve, stats, mv, var, rs, n, rs_in, rs_out, nsem, grow, brow, ready, done):
            for h in range(2):
                nc.vector.bn_stats(stats[:, n, h, :], xres[:, n, h * F:(h + 1) * F]).then_inc(nsem, 1)
            dve.wait_ge(nsem, n * 5 + 2)
            nc.vector.bn_aggr(mv[:, n, :], stats[:, n, :, :].rearrange("p h c -> p (h c)")).then_inc(nsem, 1)
            dve.wait_ge(nsem, n * 5 + 3)
            nc.vector.tensor_scalar(var[:, n:n + 1], mv[:, n, 1:2], LN_EPS, None, ALU.add).then_inc(rs_in, 1)
            dve.wait_ge(rs_out, n + 1)
            nc.vector.tensor_scalar(xres[:, n, :], xres[:, n, :], mv[:, n, 0:1], rs[:, n:n + 1], ALU.subtract, ALU.mult).then_inc(nsem, 1)
            dve.wait_ge(nsem, n * 5 + 4)
            nc.vector.tensor_tensor(xres[:, n, :], xres[:, n, :], grow, ALU.mult).then_inc(nsem, 1)
            dve.wait_ge(nsem, n * 5 + 5)
            nc.vector.tensor_tensor(xres[:, n, :], xres[:, n, :], brow, ALU.add).then_inc(done, 1)

        def dense_and_norm(tag, srcT, w, scale, g_dram, b_dram):
            with ExitStack() as c2:
                def b2(name, shape, dt=f32):
                    return c2.enter_context(nc.sbuf_tensor(f"{tag}_{name}", shape, dt))

                rows = b2("rows", [P, 2, D])
                wide = [b2(f"w{h}", [P, KT, F]) for h in range(2)]
                stats, mv, var, rs = b2("stats", [P, NT, 2, 6]), b2("mv", [P, NT, 2]), b2("var", [P, NT]), b2("rs", [P, NT])
                w_in_, rows_in = sem(tag + "_w_in"), sem(tag + "_rows_in")
                ax, prod, z_done, nsem = sem(tag + "_alpha_x"), sem(tag + "_prod"), sem(tag + "_z_done"), sem(tag + "_norm")
                rs_in, rs_out, x_done, t_psum, t_done = [sem(f"{tag}_{n_}") for n_ in ("rs_in", "rs_out", "x_done", "t_psum", "t_done")]
                with nc.Block() as block:
                    @block.sync
                    def _(sp_):
                        for h in range(2):
                            sp_.dma_start(wide[h][:, :, :], w_cols(w, h * F, F)).then_inc(w_in_, 16)
                        sp_.dma_start(rows[:, 0, :], g_dram).then_inc(rows_in, 16)
                        sp_.dma_start(rows[:, 1, :], b_dram).then_inc(rows_in, 16)

                    @block.tensor
                    def _(pe):
                        pe.wait_ge(w_in_, 32)
                        for n in range(NT):
                            for h in range(2):
                                u = 2 * n + h
                                if u >= 4:
                                    pe.wait_ge(z_done, u - 3)
                                for k in range(KT):
                                    ins = nc.tensor.matmul(psum[u % 4][:, :], srcT[:, k, n * P:(n + 1) * P], wide[h][:, k, :], start=(k == 0), stop=(k == KT - 1))
                                ins.then_inc(prod, 1)
                        for n in range(NT):
                            pe.wait_ge(x_done, n + 1)
                            for a in range(2):
                                u = 2 * n + a
                                if u >= 4:
                                    pe.wait_ge(t_done, u - 3)
                                for k in range(4):
                                    ins = nc.tensor.transpose(psum[4 + u % 4][:, k * P:(k + 1) * P], xres[:, n, (4 * a + k) * P:(4 * a + k + 1) * P], ident)
                                ins.then_inc(t_psum, 1)

                    @block.scalar
                    def _(act):
                        for n in range(NT):
                            nc.scalar.activation(xres[:, n, :], xres[:, n, :], ACT.Copy, scale=ALPHA).then_inc(ax, 1)
                        for u in range(2 * NT):
                            n, a = u // 2, u % 2
                            act.wait_ge(t_psum, u + 1)
                            nc.scalar.activation(xT[:, 4 * a:4 * a + 4, n * P:(n + 1) * P], v3(psum[4 + u % 4][:, :]), ACT.Copy).then_inc(t_done, 1)

                    @block.gpsimd
                    def _(pool):
                        for n in range(NT):
                            pool.wait_ge(rs_in, n + 1)
                            nc.gpsimd.tensor_tensor(rs[:, n:n + 1], var[:, n:n + 1], half[:, 0:1], ALU.pow).then_inc(rs_out, 1)

                    @block.vector
                    def _(dve):
                        dve.wait_ge(rows_in, 32)
                        for n in range(NT):
                            dve.wait_ge(ax, n + 1)
                            for h in range(2):
                                u = 2 * n + h
                                dve.wait_ge(prod, u + 1)
                                c = slice(h * F, (h + 1) * F)
                                nc.vector.scalar_tensor_tensor(out=xres[:, n, c], in0=psum[u % 4][:, :], scalar=scale, in1=xres[:, n, c], op0=ALU.mult, op1=ALU.add).then_inc(z_done, 1)
                            dve.wait_ge(z_done, 2 * n + 2)
                            norm_rows(dve, stats, mv, var, rs, n, rs_in, rs_out, nsem, rows[:, 0, :], rows[:, 1, :], None, x_done)

        end_phase()
        dense_and_norm("mix", mT, t["mix_w_out"][0], 0.5, t["ln_mix_g"], t["ln_mix_b"])

        end_phase()
        with ExitStack() as c2:
            def b2(name, shape, dt=f32):
                return c2.enter_context(nc.sbuf_tensor("x_" + name, shape, dt))

            mem_tok, memT = b2("mem_tok", [P, 2, D]), b2("memT", [P, KT, MEM])
            qT, kT, v = b2("qT", [P, 2, S]), b2("kT", [P, 2, MEM]), b2("v", [P, 2, 2, P])
            mx, nb, sm_, ri = b2("mx", [P, NT]), b2("nb", [P, NT]), b2("sm", [P, NT]), b2("ri", [P, NT])
            pe_, pn = b2("pexp", [P, NT, MEM]), b2("pn", [P, NT, MEM])
            pT = b2("pT", [P, 2, S])
            names = ("mem_in mem_psum mem_done q_done k_done v_done s_psum mx_done nb_done e_done ri_done pn_done pT_psum pT_done o_psum o_done").split()
            q_ = {n_: sem("x_" + n_) for n_ in names}
            ub, us = list(units), list(uses)
            xw = [t["xa_w_q"][0], t["xa_w_k"][0], t["xa_w_v"][0]]
            SC = (D // XH) ** -0.5

            with nc.Block() as block:
                @block.sync
                def _(sp_):
                    for m in range(2):
                        sp_.dma_start(mem_tok[:, m, :], t["mem"][0, m * P:(m + 1) * P, :]).then_inc(q_["mem_in"], 16)
                    with sp_.Fori(0, XH) as i:
                        for j in range(6):
                            src = w_cols(xw[j // 2], i * 256 + (j % 2) * P, P)
                            sp_.wait_ge(w_free[j], i + us[j])
                            sp_.sem_inc(sp_turn, 1)
                            sp_.dma_start(ring[:, j], src).then_inc(w_loaded[j], 16)

                @block.tensor
                def _(pe):
                    pe.wait_ge(q_["mem_in"], 32)
                    for k2 in range(4):
                        for kk in range(2):
                            for m in range(2):
                                ins = nc.tensor.transpose(psum[2 + k2][:, (2 * kk + m) * P:(2 * kk + m + 1) * P], mem_tok[:, m, (2 * k2 + kk) * P:(2 * k2 + kk + 1) * P], ident)
                        ins.then_inc(q_["mem_psum"], 1)
                    pe.wait_ge(q_["mem_done"], 4)
                    with pe.Fori(0, XH) as i:
                        for j in range(6):
                            b = j % 2
                            pe.wait_ge(w_loaded[j], (i + (us[j] + 1)) * 16)
                            pe.wait_ge(g_free[b], i * 3 + (ub[b] + j // 2 + 1))
                            if j < 4:
                                for k in range(KT):
                                    ins = nc.tensor.matmul(psum[b][:, 0:(S, MEM)[j // 2]], ring[:, j, k, :], (xT, memT)[j // 2][:, k, :], start=(k == 0), stop=(k == KT - 1))
                            else:
                                for m in range(2):
                                    for k in range(KT):
                                        ins = nc.tensor.matmul(psum[b][:, m * P:(m + 1) * P], memT[:, k, m * P:(m + 1) * P], ring[:, j, k, :], start=(k == 0), stop=(k == KT - 1))
                            ins.then_inc(g_ready[b], 1)
                            pe.wait_ge(g_ready[b], i * 3 + (ub[b] + j // 2 + 1))
                            pe.sem_inc(w_free[j], 1)
                        pe.wait_ge(q_["q_done"], i * 2 + 2)
                        pe.wait_ge(q_["k_done"], i * 2 + 2)
                        for n in range(NT):
                            for c in range(2):
                                ins = nc.tensor.matmul(psum[2 + n // 2][:, (n % 2) * MEM:(n % 2 + 1) * MEM], qT[:, c, n * P:(n + 1) * P], kT[:, c, :], start=(c == 0), stop=(c == 1))
                        ins.then_inc(q_["s_psum"], 1)
                        pe.wait_ge(q_["pn_done"], i + 1)
                        for m in range(2):
                            for n in range(NT):
                                ins = nc.tensor.transpose(psum[4 + m][:, n * P:(n + 1) * P], pn[:, n, m * P:(m + 1) * P], ident)
                            ins.then_inc(q_["pT_psum"], 1)
                        pe.wait_ge(q_["pT_done"], i * 2 + 2)
                        pe.wait_ge(q_["v_done"], i * 2 + 2)
                        for c in range(2):
                            for m in range(2):
                                ins = nc.tensor.matmul(psum[6 + c][:, :], v[:, m, c, :], pT[:, m, :], start=(m == 0), stop=(m == 1))
                            ins.then_inc(q_["o_psum"], 1)
                        pe.wait_ge(q_["o_done"], i * 2 + 2)

                @block.scalar
                def _(act):
                    for k2 in range(4):
                        act.wait_ge(q_["mem_psum"], k2 + 1)
                        nc.scalar.activation(memT[:, 2 * k2:2 * k2 + 2, :].rearrange("p k m -> p (k m)"), psum[2 + k2][:, :], ACT.Copy).then_inc(q_["mem_done"], 1)
                    with act.Fori(0, XH) as i:
                        for j in range(6):
                            b = j % 2
                            act.wait_ge(g_ready[b], i * 3 + (ub[b] + j // 2 + 1))
                            key = ("q_done", "k_done", "v_done")[j // 2]
                            if j < 2:
                                nc.scalar.activation(qT[:, b, :], psum[b][:, :], ACT.Copy).then_inc(q_[key], 1)
                            elif j < 4:
                                nc.scalar.activation(kT[:, b, :], psum[b][:, 0:MEM], ACT.Copy).then_inc(q_[key], 1)
                            else:
                                nc.scalar.activation(v[:, :, b, :], psum[b][:, 0:MEM].rearrange("p (m c) -> p m c", m=2), ACT.Copy).then_inc(q_[key], 1)
                            act.wait_ge(q_[key], i * 2 + (b + 1))
                            act.sem_inc(g_free[b], 1)
                        act.wait_ge(q_["nb_done"], i + 1)
                        for n in range(NT):
                            nc.scalar.activation(pe_[:, n, :], psum[2 + n // 2][:, (n % 2) * MEM:(n % 2 + 1) * MEM], ACT.Exp, bias=nb[:, n:n + 1], scale=SC,
                                                 accum_out=sm_[:, n:n + 1]).then_inc(q_["e_done"], 1)
                        for m in range(2):
                            act.wait_ge(q_["pT_psum"], i * 2 + (m + 1))
                            nc.scalar.activation(pT[:, m, :], psum[4 + m][:, :], ACT.Copy).then_inc(q_["pT_done"], 1)
                        for c in range(2):
                            act.wait_ge(q_["o_psum"], i * 2 + (c + 1))
                            nc.scalar.activation(mT[:, ds(i * 2 + c, 1), :].rearrange("p a c -> p (a c)"), psum[6 + c][:, :], ACT.Copy).then_inc(q_["o_done"], 1)
                        act.wait_ge(q_["o_done"], i * 2 + 2)

                @block.vector
                def _(dve):
                    with dve.Fori(0, XH) as i:
                        dve.wait_ge(q_["s_psum"], i + 1)
                        for b in range(2):
                            nc.vector.tensor_reduce(mx[:, 2 * b:2 * b + 2], psum[2 + b][:, :].rearrange("p (n c) -> p n c", n=2), AX.X, ALU.max).then_inc(q_["mx_done"], 1)
                        dve.wait_ge(q_["mx_done"], i * 2 + 2)
                        nc.vector.tensor_scalar(nb[:, :], mx[:, :], -SC, None, ALU.mult).then_inc(q_["nb_done"], 1)
                        dve.wait_ge(q_["e_done"], i * 4 + 4)
                        nc.vector.reciprocal(ri[:, :], sm_[:, :]).then_inc(q_["ri_done"], 1)
                        dve.wait_ge(q_["ri_done"], i + 1)
                        nc.vector.tensor_tensor(pn[:, :, :], pe_[:, :, :], ri[:, :].unsqueeze(2).to_broadcast([P, NT, MEM]), ALU.mult).then_inc(q_["pn_done"], 1)
                        dve.wait_ge(q_["o_done"], i * 2 + 2)
            for j in range(6):
                uses[j] += XH
            units[0] += 3 * XH
            units[1] += 3 * XH

        end_phase()
        dense_and_norm("xa", mT, t["xa_w_o"][0], 1.0, t["ln_xa_g"], t["ln_xa_b"])
        end_phase()
        BIG = 1e9
        with ExitStack() as c2:
            def b2(name, shape, dt=f32):
                return c2.enter_context(nc.sbuf_tensor("q_" + name, shape, dt))

            rw, rb = b2("rw", [P, KT, NE]), b2("rb", [P, NE])
            R = b2("R", [P, 24, NT, NE])
            G = b2("G", [P, 12, NT, 4])
            one = b2("one", [P, 10, NT])
            E16 = b2("E16", [P, 8, NE])
            ge, ohh = b2("ge", [P, 2, NT, NB + 1]), b2("ohh", [P, 2, NT, NB])
            ohl = b2("ohl", [P, 2, NT, P])
            lo = b2("lo", [P, 2, NT])
            thr = b2("thr", [P, NB + 1])
            eo = b2("eo", [P, 8, NE])
            tab = b2("tab", [P, 8])
            zero, zero_set = b2("zero", [P, D]), sem("q_zero_set")
            r_in, lg_psum, e_done, oh_done, rk_psum, list_in, list_psum, chain, x2_st = [sem("q_" + n_) for n_ in
                ("in", "logit_psum", "e_done", "oh_done", "rank_psum", "list_in", "list_psum", "chain", "x2_stored")]
            with nc.Block() as block:
                @block.sync
                def _(sp_):
                    sp_.dma_start(rw[:, :, :], t["router_w"].rearrange("(k p) e -> p k e", p=P)).then_inc(r_in, 16)
                    sp_.dma_start(rb[:, :], t["router_rows"]).then_inc(r_in, 16)
                    for n in range(NT):
                        sp_.dma_start(x2_dram[n * P:(n + 1) * P, :], xres[:, n, :]).then_inc(x2_st, 16)
                    sp_.wait_ge(zero_set, 1)
                    for j in range(NOV):
                        sp_.dma_start(y_dram[(NE + j) * P:(NE + j + 1) * P, :], zero[:, :]).then_inc(x2_st, 16)
                    sp_.wait_ge(x2_st, 16 * (NT + NOV))

                @block.gpsimd
                def _(pool):
                    nc.gpsimd.memset(zero[:, :], 0.0).then_inc(zero_set, 1)

                @block.tensor
                def _(pe):
                    pe.wait_ge(r_in, 32)
                    for n in range(NT):
                        for k in range(KT):
                            ins = nc.tensor.matmul(psum[0][:, n * NE:(n + 1) * NE], xT[:, k, n * P:(n + 1) * P], rw[:, k, :], start=(k == 0), stop=(k == KT - 1))
                    ins.then_inc(lg_psum, 1)
                    pe.wait_ge(oh_done, 1)
                    for n in range(NT):
                        for m in range(n + 1):
                            ins = nc.tensor.matmul(psum[1][:, n * NE:(n + 1) * NE], cst[:, K_U:K_U + P] if m == n else cst[:, K_ONE:K_ONE + P], R[:, 12, m, :], start=(m == 0), stop=(m == n))
                    for m in range(NT):
                        ins = nc.tensor.matmul(psum[1][:, NT * NE:(NT + 1) * NE], cst[:, K_ONE:K_ONE + P], R[:, 12, m, :], start=(m == 0), stop=(m == NT - 1))
                    ins.then_inc(rk_psum, 1)
                    pe.wait_ge(list_in, 1)
                    for c in range(2):
                        for n in range(NT):
                            ins = nc.tensor.matmul(psum[2][:, 0:NB], ohl[:, c, n, :], ohh[:, c, n, :], start=(c + n == 0), stop=(c == 1 and n == NT - 1))
                    ins.then_inc(list_psum, 1)

                @block.scalar
                def _(act):
                    act.wait_ge(lg_psum, 1)
                    nc.scalar.activation(R[:, 0], psum[0][:, 0:NT * NE].rearrange("p (n e) -> p n e", n=NT), ACT.Exp, scale=-1.0).then_inc(e_done, 1)

                iota = cst[:, K_SLOT:K_SLOT + NE].unsqueeze(1).to_broadcast([P, NT, NE])
                iota4 = cst[:, K_SLOT:K_SLOT + 4].unsqueeze(1).to_broadcast([P, NT, 4])

                @block.vector
                def _(dve):
                    link = Count(dve, chain, 0)
                    V = nc.vector

                    def first_max(vals, io, mxv, eq, cand, idx, oh, n_):
                        link(V.tensor_reduce(mxv, vals, AX.X, ALU.max))
                        link(V.tensor_tensor(eq, vals, mxv.unsqueeze(2).to_broadcast([P, NT, n_]), ALU.is_equal))
                        link(V.scalar_tensor_tensor(out=cand, in0=eq, scalar=-64.0, in1=io, op0=ALU.mult, op1=ALU.add))
                        link(V.tensor_reduce(idx, cand, AX.X, ALU.min))
                        link(V.tensor_scalar(idx, idx, 64.0, None, ALU.add))
                        link(V.tensor_tensor(oh, io, idx.unsqueeze(2).to_broadcast([P, NT, n_]), ALU.is_equal))

                    dve.wait_ge(e_done, 1)
                    link(V.tensor_scalar(R[:, 1], R[:, 0], 1.0, None, ALU.add))
                    link(V.reciprocal(R[:, 2], R[:, 1]))
                    link(V.tensor_tensor(R[:, 3], R[:, 2], rb[:, :].unsqueeze(1).to_broadcast([P, NT, NE]), ALU.add))
                    s4 = R[:, 3].rearrange("p n (g e) -> p n g e", g=4)
                    a_, b_, c_, d_ = [s4[:, :, :, j] for j in range(4)]
                    link(V.tensor_tensor(G[:, 0], a_, b_, ALU.max))
                    link(V.tensor_tensor(G[:, 1], a_, b_, ALU.min))
                    link(V.tensor_tensor(G[:, 2], c_, d_, ALU.max))
                    link(V.tensor_tensor(G[:, 3], c_, d_, ALU.min))
                    link(V.tensor_tensor(G[:, 4], G[:, 0], G[:, 2], ALU.max))
                    link(V.tensor_tensor(G[:, 5], G[:, 0], G[:, 2], ALU.min))
                    link(V.tensor_tensor(G[:, 6], G[:, 1], G[:, 3], ALU.max))
                    link(V.tensor_tensor(G[:, 5], G[:, 5], G[:, 6], ALU.max))
                    link(V.tensor_tensor(G[:, 7], G[:, 4], G[:, 5], ALU.add))
                    first_max(G[:, 7], iota4, one[:, 0], G[:, 8], G[:, 9], one[:, 1], G[:, 10], 4)
                    link(V.tensor_scalar(G[:, 11], G[:, 10], -1.0, BIG, ALU.add, ALU.mult))
                    link(V.tensor_tensor(R[:, 4].rearrange("p n (g e) -> p n g e", g=4), s4, G[:, 11].unsqueeze(3).to_broadcast([P, NT, 4, 4]), ALU.add))
                    first_max(R[:, 4], iota, one[:, 0], R[:, 5], R[:, 6], one[:, 1], R[:, 7], NE)
                    link(V.scalar_tensor_tensor(out=R[:, 8], in0=R[:, 7], scalar=-4 * BIG, in1=R[:, 4], op0=ALU.mult, op1=ALU.add))
                    first_max(R[:, 8], iota, one[:, 0], R[:, 5], R[:, 6], one[:, 1], R[:, 11], NE)
                    link(V.tensor_tensor(R[:, 12], R[:, 7], R[:, 11], ALU.add))
                    dve.sem_inc(oh_done, 1)
                    for c, oh in enumerate((7, 11)):
                        link(V.tensor_tensor(R[:, 13], R[:, 2], R[:, oh], ALU.mult))
                        link(V.tensor_reduce(one[:, 2 + c], R[:, 13], AX.X, ALU.add))
                    link(V.tensor_tensor(one[:, 4], one[:, 2], one[:, 3], ALU.add))
                    link(V.reciprocal(one[:, 5], one[:, 4]))
                    for c in range(2):
                        link(V.tensor_tensor(r_g[:, c, :], one[:, 2 + c], one[:, 5], ALU.mult))
                    dve.wait_ge(rk_psum, 1)
                    cnt = psum[1][:, NT * NE:(NT + 1) * NE]
                    link(V.tensor_scalar(E16[:, 0], cnt, float(P), None, ALU.is_gt))
                    link(V.tensor_scalar(E16[:, 1], cnt, 2.0 * P, None, ALU.is_gt))
                    link(V.tensor_scalar(E16[:, 2], cnt, 3.0 * P, None, ALU.is_gt))
                    link(V.tensor_tensor(E16[:, 0], E16[:, 0], E16[:, 1], ALU.add))
                    link(V.tensor_tensor(E16[:, 0], E16[:, 0], E16[:, 2], ALU.add))
                    link(V.tensor_copy(E16[:, 3], E16[:, 0]))
                    src, dst = 3, 4
                    for sh in (1, 2, 4, 8):
                        link(V.tensor_copy(E16[:, dst, 0:sh], E16[:, src, 0:sh]))
                        link(V.tensor_tensor(E16[:, dst, sh:NE], E16[:, src, sh:NE], E16[:, src, 0:NE - sh], ALU.add))
                        src, dst = dst, src
                    inc = E16[:, src]
                    link(V.tensor_tensor(E16[:, 5], inc, E16[:, 0], ALU.subtract))
                    link(V.tensor_tensor(R[:, 14], psum[1][:, 0:NT * NE].rearrange("p (n e) -> p n e", n=NT), R[:, 12], ALU.subtract))
                    link(V.tensor_scalar(R[:, 15], R[:, 14], float(P), None, ALU.is_ge))
                    link(V.tensor_scalar(E16[:, 6], cst[:, K_SLOT:K_SLOT + NE], float(P), None, ALU.mult))
                    link(V.tensor_scalar(E16[:, 7], E16[:, 5], float(P), float((NE - 1) * P), ALU.mult, ALU.add))
                    link(V.tensor_tensor(E16[:, 7], E16[:, 7], E16[:, 6], ALU.subtract))
                    link(V.tensor_tensor(R[:, 16], R[:, 15], E16[:, 7].unsqueeze(1).to_broadcast([P, NT, NE]), ALU.mult))
                    link(V.tensor_tensor(R[:, 16], R[:, 16], E16[:, 6].unsqueeze(1).to_broadcast([P, NT, NE]), ALU.add))
                    link(V.tensor_tensor(R[:, 16], R[:, 16], R[:, 14], ALU.add))
                    link(V.tensor_scalar(thr[:, :], cst[:, K_SLOT:K_SLOT + NB + 1], float(P), None, ALU.mult))
                    for c, oh in enumerate((7, 11)):
                        link(V.tensor_tensor(R[:, 13], R[:, 16], R[:, oh], ALU.mult))
                        link(V.tensor_reduce(one[:, 6 + c], R[:, 13], AX.X, ALU.add))
                        link(V.tensor_copy(r_slot[:, c, :], one[:, 6 + c]))
                        link(V.tensor_tensor(ge[:, c], one[:, 6 + c].unsqueeze(2).to_broadcast([P, NT, NB + 1]), thr[:, :].unsqueeze(1).to_broadcast([P, NT, NB + 1]), ALU.is_ge))
                        link(V.tensor_tensor(ohh[:, c], ge[:, c, :, 0:NB], ge[:, c, :, 1:NB + 1], ALU.subtract))
                        link(V.tensor_reduce(lo[:, c], ge[:, c, :, 1:NB + 1], AX.X, ALU.add))
                        link(V.scalar_tensor_tensor(out=lo[:, c], in0=lo[:, c], scalar=-float(P), in1=one[:, 6 + c], op0=ALU.mult, op1=ALU.add))
                        link(V.tensor_tensor(ohl[:, c], lo[:, c].unsqueeze(2).to_broadcast([P, NT, P]), cst[:, K_SLOT:K_SLOT + P].unsqueeze(1).to_broadcast([P, NT, P]), ALU.is_equal))
                        link(V.tensor_tensor(ohh[:, c], ohh[:, c], cst[:, K_TOK:K_TOK + NT].unsqueeze(2).to_broadcast([P, NT, NB]), ALU.mult))
                    dve.sem_inc(list_in, 1)
                    link(V.tensor_tensor(eo[:, :, :], inc.unsqueeze(1).to_broadcast([P, 8, NE]), cst[:, K_SLOT:K_SLOT + 8].unsqueeze(2).to_broadcast([P, 8, NE]), ALU.is_le))
                    link(V.tensor_reduce(tab[:, :], eo[:, :, :], AX.X, ALU.add))
                    link(V.tensor_copy(tab[:, 7:8], inc[:, NE - 1:NE]))
                    link(V.tensor_copy(r_tab[0:1, :], tab[0:1, :]))
                    dve.wait_ge(list_psum, 1)
                    link(V.tensor_copy(r_idx[:, :], psum[2][:, 0:NB]))

        end_phase()
        upper.close()
        with ExitStack() as c2:
            def b2(name, shape, dt=f32):
                return c2.enter_context(nc.sbuf_tensor("e_" + name, shape, dt))

            wg, wu, wd = b2("wg", [P, 2, KT, F]), b2("wu", [P, 2, KT, F]), b2("wd", [P, 2, 4, D])
            idx = b2("idx", [P, 2], i32)
            xg, xgT = b2("xg", [P, 2, D]), b2("xgT", [P, 2, KT, P])
            gt, sg, hid = b2("gt", [P, F]), b2("sg", [P, F]), b2("hid", [P, F])
            hT, ye = b2("hT", [P, 4, P]), b2("ye", [P, 2, D])
            w_sets = [t["moe_w_gate"][0], t["moe_w_up"][0], t["moe_w_down"][0]]

            def expert_sems(tag):
                return {n_: sem(f"{tag}_{n_}") for n_ in
                        "turn w_in0 w_in1 idx xg_in xT_psum xT_done up_psum gt sg hid hT_psum hT_done y_psum ye stored".split()}

            main, over = expert_sems("e"), expert_sems("o")

            def load_expert(sp_, e, u, s, part):
                w = (wg, wu, wd)[part]
                src = w_sets[part][ds(e, 1)].rearrange("a (k p) f -> p (a k) f", p=P)
                sp_.dma_start(w[:, u], src).then_inc(s[f"w_in{u}"], 16)

            def pe_block(pe, s, m, q, u):
                pe.wait_ge(s["xg_in"], (m + 1) * 16)
                for a in range(2):
                    for k in range(4):
                        ins = nc.tensor.transpose(psum[a][:, k * P:(k + 1) * P], xg[:, u, (4 * a + k) * P:(4 * a + k + 1) * P], ident)
                    ins.then_inc(s["xT_psum"], 1)
                pe.wait_ge(s[f"w_in{u}"], (q + 1) * 48)
                pe.wait_ge(s["xT_done"], m * 2 + 2)
                for w, b in ((wg, 2), (wu, 3)):
                    for k in range(KT):
                        ins = nc.tensor.matmul(psum[b][:, :], xgT[:, u, k, :], w[:, u, k, :], start=(k == 0), stop=(k == KT - 1))
                    ins.then_inc(s["up_psum"], 1)
                pe.wait_ge(s["hid"], m + 1)
                for f in range(4):
                    ins = nc.tensor.transpose(psum[4][:, f * P:(f + 1) * P], hid[:, f * P:(f + 1) * P], ident)
                ins.then_inc(s["hT_psum"], 1)
                pe.wait_ge(s["hT_done"], m + 1)
                for h in range(2):
                    for f in range(4):
                        ins = nc.tensor.matmul(psum[6 + h][:, :], hT[:, f, :], wd[:, u, f, h * F:(h + 1) * F], start=(f == 0), stop=(f == 3))
                    ins.then_inc(s["y_psum"], 1)
                pe.wait_ge(s["ye"], m * 2 + 2)

            def act_block(act, s, m, u):
                for a in range(2):
                    act.wait_ge(s["xT_psum"], m * 2 + (a + 1))
                    nc.scalar.activation(xgT[:, u, 4 * a:4 * a + 4, :], v3(psum[a][:, :]), ACT.Copy).then_inc(s["xT_done"], 1)
                act.wait_ge(s["up_psum"], m * 2 + 1)
                nc.scalar.activation(gt[:, :], psum[2][:, :], ACT.Tanh, scale=0.5).then_inc(s["gt"], 1)
                act.wait_ge(s["hT_psum"], m + 1)
                nc.scalar.activation(hT[:, :, :], v3(psum[4][:, :]), ACT.Copy).then_inc(s["hT_done"], 1)

            def dve_block(dve, s, m, u):
                dve.wait_ge(s["gt"], m + 1)
                nc.vector.scalar_tensor_tensor(out=sg[:, :], in0=gt[:, :], scalar=1.0, in1=psum[2][:, :], op0=ALU.add, op1=ALU.mult).then_inc(s["sg"], 1)
                dve.wait_ge(s["sg"], m + 1)
                dve.wait_ge(s["up_psum"], m * 2 + 2)
                nc.vector.scalar_tensor_tensor(out=hid[:, :], in0=sg[:, :], scalar=0.5, in1=psum[3][:, :], op0=ALU.mult, op1=ALU.mult).then_inc(s["hid"], 1)
                for h in range(2):
                    dve.wait_ge(s["y_psum"], m * 2 + (h + 1))
                    nc.vector.tensor_copy(ye[:, u, h * F:(h + 1) * F], psum[6 + h][:, :]).then_inc(s["ye"], 1)

            with nc.Block() as block:
                @block.sync
                def _(sp_):
                    for u in range(2):
                        for part in range(3):
                            load_expert(sp_, u, u, main, part)
                    def store(i, u):
                        sp_.wait_ge(main["ye"], i * 4 + (2 * u + 2))
                        sp_.sem_inc(main["turn"], 1)
                        sp_.dma_start(y_dram[ds(i * 256 + u * P, P), :], ye[:, u, :]).then_inc(main["stored"], 16)

                    with sp_.Fori(0, NE // 2 - 1) as i:
                        for u in range(2):
                            store(i, u)
                            for part in range(3):
                                load_expert(sp_, i * 2 + (u + 2), u, main, part)
                    for u in range(2):
                        store(NE // 2 - 1, u)
                    sp_.wait_ge(main["stored"], 16 * NE)
                    nov = sp_.value_load(r_tab[0:1, 7:8], min_val=0, max_val=NOV)
                    with sp_.Fori(0, NOV) as j:
                        with sp_.If(nov > j):
                            e = sp_.value_load(r_tab[0:1, ds(j, 1)], min_val=0, max_val=NE - 1)
                            for part in range(3):
                                load_expert(sp_, e, 0, over, part)
                            sp_.wait_ge(over["ye"], j * 2 + 2)
                            sp_.sem_inc(over["turn"], 1)
                            sp_.dma_start(y_dram[ds(j * P + NE * P, P), :], ye[:, 0, :]).then_inc(over["stored"], 16)
                            sp_.wait_ge(over["stored"], (j + 1) * 16)
                            sp_.sem_inc(over["turn"], 1)

                @block.gpsimd
                def _(pool):
                    with pool.Fori(0, NE // 2) as i:
                        for u in range(2):
                            pool.wait_ge(main["idx"], i * 2 + (u + 1))
                            pool.sem_inc(main["turn"], 1)
                            nc.gpsimd.indirect_dma_start(xg[:, u, :], None, x2_dram, bass.IndirectOffsetOnAxis(ap=idx[:, u:u + 1], axis=0)).then_inc(main["xg_in"], 16)
                            pool.wait_ge(main["xg_in"], (i * 2 + (u + 1)) * 16)
                            pool.sem_inc(main["turn"], 1)
                    nov = pool.value_load(r_tab[0:1, 7:8], min_val=0, max_val=NOV)
                    with pool.Fori(0, NOV) as j:
                        with pool.If(nov > j):
                            pool.wait_ge(over["idx"], j + 1)
                            pool.sem_inc(over["turn"], 1)
                            nc.gpsimd.indirect_dma_start(xg[:, 0, :], None, x2_dram, bass.IndirectOffsetOnAxis(ap=idx[:, 0:1], axis=0)).then_inc(over["xg_in"], 16)
                            pool.wait_ge(over["xg_in"], (j + 1) * 16)
                            pool.sem_inc(over["turn"], 1)

                @block.tensor
                def _(pe):
                    with pe.Fori(0, NE // 2) as i:
                        for u in range(2):
                            pe_block(pe, main, i * 2 + u, i, u)
                    nov = pe.value_load(r_tab[0:1, 7:8], min_val=0, max_val=NOV)
                    with pe.Fori(0, NOV) as j:
                        with pe.If(nov > j):
                            pe_block(pe, over, j, j, 0)

                @block.scalar
                def _(act):
                    with act.Fori(0, NE // 2) as i:
                        for u in range(2):
                            act_block(act, main, i * 2 + u, u)
                    nov = act.value_load(r_tab[0:1, 7:8], min_val=0, max_val=NOV)
                    with act.Fori(0, NOV) as j:
                        with act.If(nov > j):
                            act_block(act, over, j, 0)

                @block.vector
                def _(dve):
                    for u in range(2):
                        nc.vector.tensor_copy(idx[:, u:u + 1], r_idx[:, u:u + 1]).then_inc(main["idx"], 1)
                    with dve.Fori(0, NE // 2) as i:
                        for u in range(2):
                            if u == 0:
                                dve.wait_ge(main["stored"], i * 32)
                            dve_block(dve, main, i * 2 + u, u)
                            dve.wait_ge(main["xg_in"], (i * 2 + (u + 1)) * 16)
                            nc.vector.tensor_copy(idx[:, u:u + 1], r_idx[:, ds(i * 2 + (u + 2), 1)]).then_inc(main["idx"], 1)
                    nov = dve.value_load(r_tab[0:1, 7:8], min_val=0, max_val=NOV)
                    dve.wait_ge(main["stored"], 16 * NE)
                    dve.wait_ge(main["xg_in"], 16 * NE)
                    with dve.Fori(0, NOV) as j:
                        with dve.If(nov > j):
                            nc.vector.tensor_copy(idx[:, 0:1], r_idx[:, ds(j + NE, 1)]).then_inc(over["idx"], 1)
                            dve_block(dve, over, j, 0)
                            dve.wait_ge(over["stored"], (j + 1) * 16)
                            dve.sem_inc(over["turn"], 1)

        end_phase()
        with ExitStack() as c2:
            def b2(name, shape, dt=f32):
                return c2.enter_context(nc.sbuf_tensor("c_" + name, shape, dt))

            rows = b2("rows", [P, 2, D])
            stats, mv, var, rs = b2("stats", [P, NT, 2, 6]), b2("mv", [P, NT, 2]), b2("var", [P, NT]), b2("rs", [P, NT])
            yg = b2("yg", [P, NT, 2, D])
            rows_in, ax, nsem, rs_in, rs_out, x_done, z1, out_st = [sem("c_" + n_) for n_ in ("rows_in", "alpha_x", "norm", "rs_in", "rs_out", "x_done", "z", "out_stored")]
            y_in = [sem(f"c_y_in{n}") for n in range(NT)]
            sidx = b2("sidx", [P, 2 * NT], i32)
            with nc.Block() as block:
                @block.sync
                def _(sp_):
                    sp_.dma_start(rows[:, 0, :], t["ln_moe_g"]).then_inc(rows_in, 16)
                    sp_.dma_start(rows[:, 1, :], t["ln_moe_b"]).then_inc(rows_in, 16)
                    for n in range(NT):
                        sp_.wait_ge(x_done, n + 1)
                        sp_.dma_start(out[0, n * P:(n + 1) * P, :], xres[:, n, :]).then_inc(out_st, 16)
                    sp_.wait_ge(out_st, 16 * NT)

                @block.gpsimd
                def _(pool):
                    for n in range(NT):
                        for c in range(2):
                            nc.gpsimd.indirect_dma_start(yg[:, n, c, :], None, y_dram, bass.IndirectOffsetOnAxis(ap=r_slot[:, c, n:n + 1], axis=0)).then_inc(y_in[n], 16)
                    for n in range(NT):
                        pool.wait_ge(rs_in, n + 1)
                        nc.gpsimd.tensor_tensor(rs[:, n:n + 1], var[:, n:n + 1], half[:, 0:1], ALU.pow).then_inc(rs_out, 1)

                @block.scalar
                def _(act):
                    for n in range(NT):
                        nc.scalar.activation(xres[:, n, :], xres[:, n, :], ACT.Copy, scale=ALPHA).then_inc(ax, 1)

                @block.vector
                def _(dve):
                    dve.wait_ge(rows_in, 32)
                    for n in range(NT):
                        dve.wait_ge(y_in[n], 32)
                        nc.vector.tensor_scalar(yg[:, n, 0, :], yg[:, n, 0, :], r_g[:, 0, n:n + 1], None, ALU.mult).then_inc(z1, 1)
                        dve.wait_ge(z1, 3 * n + 1)
                        nc.vector.scalar_tensor_tensor(out=yg[:, n, 1, :], in0=yg[:, n, 1, :], scalar=r_g[:, 1, n:n + 1], in1=yg[:, n, 0, :], op0=ALU.mult, op1=ALU.add).then_inc(z1, 1)
                        dve.wait_ge(z1, 3 * n + 2)
                        dve.wait_ge(ax, n + 1)
                        nc.vector.tensor_tensor(xres[:, n, :], xres[:, n, :], yg[:, n, 1, :], ALU.add).then_inc(z1, 1)
                        dve.wait_ge(z1, 3 * n + 3)
                        norm_rows(dve, stats, mv, var, rs, n, rs_in, rs_out, nsem, rows[:, 0, :], rows[:, 1, :], None, x_done)


def kernel(**inputs):
    import numpy as _np
    import concourse.bacc as _bacc
    from concourse import mybir as _mybir
    from concourse.bass_utils import run_bass_kernel_spmd as _run

    nc = _bacc.Bacc("TRN2", target_bir_lowering=False, num_devices=1)
    a = {k: _np.asarray(v) for k, v in inputs.items()}
    lay = {n: a[n] for n in ("x", "mem", "mix_w_in", "w_proj_gdn", "w_proj_ssd", "w_proj_ret", "mix_w_out", "xa_w_q", "xa_w_k", "xa_w_v", "xa_w_o",
                              "router_w", "moe_w_gate", "moe_w_up", "moe_w_down")}
    for n in ("ln_mix_g", "ln_mix_b", "ln_xa_g", "ln_xa_b", "ln_moe_g", "ln_moe_b"):
        lay[n] = _np.broadcast_to(a[n][0], (P, D))
    lay["router_rows"] = _np.broadcast_to(a["router_b"], (P, NE))
    rows = _np.concatenate([a["gdn_a_log"][0], a["ssd_a_log"][0], a["gdn_dt_bias"][0], a["ssd_dt_bias"][0], a["ssd_d"][0]])
    lay["par_rows"] = _np.broadcast_to(rows, (P, 64))
    lay["conv_g"] = a["gdn_conv_w"][0].reshape(4, 24, P).transpose(2, 0, 1)
    lay["conv_s"] = a["ssd_conv_w"][0].reshape(4, 16, P).transpose(2, 0, 1)
    lay["convb_s"] = a["ssd_conv_b"][0].reshape(16, P).T
    lay["norm_g"] = a["gdn_norm_w"][0].reshape(P, 1)
    lay["norm_s"] = a["ssd_norm_w"][0].reshape(KT, P).T
    lay["consts"] = shape_constants()
    arrays, t = {}, {}
    for name, v in lay.items():
        v = _np.ascontiguousarray(v)
        arrays[f"in_{name}"] = v
        t[name] = nc.dram_tensor(f"in_{name}", v.shape, _mybir.dt.from_np(v.dtype), kind="ExternalInput").ap()
    out = nc.dram_tensor("out_0", (1, S, D), _mybir.dt.float32, kind="ExternalOutput").ap()
    x2_dram = nc.dram_tensor("x2_rows", (S, D), _mybir.dt.float32, kind="Internal").ap()
    y_dram = nc.dram_tensor("expert_rows", (NB * P, D), _mybir.dt.float32, kind="Internal").ap()
    program(nc, t, out, x2_dram, y_dram)
    r = _run(nc, [arrays], core_ids=[0])
    return r.results[0]["out_0"]
```

```python
import concourse.bass as bass
from concourse import mybir
from contextlib import ExitStack
import numpy as np

D = 1024
S = 512
P = 128
KT = D // P
NT = S // P
GH = 8
SG, SR = 4, 4
SH = SG * SR
RH = 4
NE = 16
F = 512
MEM = 256
XH = 4
ALPHA = 2.0 ** 0.25
LN_EPS, RMS_EPS = 1e-5, 1e-6
NOV = 7
NB = NE + NOV
LEVELS = 7
NEG = -1e30
C_GQKV, C_GZ, C_GA, C_GB = 0, 3072, 4096, 4104
C_SX, C_SB, C_SC, C_SZ, C_SDT = 4112, 5136, 5648, 6160, 7184
C_RQ, C_RK, C_RV, C_RG, C_GATE = 7200, 7712, 8224, 9248, 10272
K_ID, K_U, K_L, K_ONE, K_NEG, K_MASK = 0, 128, 256, 384, 512, 640
K_RDEC = K_MASK + LEVELS * 128
K_RKW = K_RDEC + RH * 128
K_RCUM = K_RKW + RH
K_COS = K_RCUM + RH
K_SIN = K_COS + NT * 64
K_RTOT = K_SIN + NT * 64
K_SLOT = K_RTOT + RH
K_TOK = K_SLOT + 128
K_END = K_TOK + NT


def shape_constants():
    f = np.float32
    i = np.arange(P)
    c = np.zeros((P, K_END), f)
    c[:, K_ID:K_ID + P] = np.eye(P)
    c[:, K_U:K_U + P] = i[:, None] <= i[None, :]
    c[:, K_L:K_L + P] = i[:, None] > i[None, :]
    c[:, K_ONE:K_ONE + P] = 1.0
    c[:, K_NEG:K_NEG + P] = np.where(i[None, :] >= i[:, None], 0.0, NEG)
    for l in range(LEVELS):
        b = 1 << l
        same = (i[:, None] // (2 * b)) == (i[None, :] // (2 * b))
        c[:, K_MASK + l * P:K_MASK + (l + 1) * P] = same & ((i[:, None] // b) % 2 == 0) & ((i[None, :] // b) % 2 == 1)
    for h in range(RH):
        lg = np.log1p(-np.exp2(f(-5.0 - h))).astype(f)
        d = (i[None, :] - i[:, None]).astype(f)
        c[:, K_RDEC + h * P:K_RDEC + (h + 1) * P] = np.where(d >= 0, np.exp(np.minimum(d, P) * lg * (d >= 0)), 0.0)
        c[:, K_RKW + h] = np.exp(lg * (P - 1 - i))
        c[:, K_RCUM + h] = np.exp(lg * (i + 1))
        c[:, K_RTOT + h] = np.exp(lg * P)
    inv = (f(10000.0) ** (-np.arange(0, P, 2, dtype=f) / f(P))).astype(f)
    ang = (np.arange(S, dtype=f)[:, None] * inv[None, :]).astype(f)
    for n in range(NT):
        c[:, K_COS + n * 64:K_COS + (n + 1) * 64] = np.cos(ang[n * P:(n + 1) * P])
        c[:, K_SIN + n * 64:K_SIN + (n + 1) * 64] = np.sin(ang[n * P:(n + 1) * P])
        c[:, K_TOK + n] = n * P + i
    c[:, K_SLOT:K_SLOT + P] = i[None, :]
    return c


class Count:

    def __init__(self, eng, sem, per, turn=0, base=0):
        self.eng, self.sem, self.n, self.per, self.turn, self.base = eng, sem, 0, per, turn, base

    def __call__(self, ins):
        self.n += 1
        ins.then_inc(self.sem, 1)
        self.eng.wait_ge(self.sem, self.turn * self.per + (self.base + self.n))

    def done(self):
        assert self.n == self.per, (self.n, self.per)


def program(nc, t, out, x2_dram, y_dram):
    f32, bf16, i32 = mybir.dt.float32, mybir.dt.bfloat16, mybir.dt.int32
    ALU, ACT, AX = mybir.AluOpType, mybir.ActivationFunctionType, mybir.AxisListType
    ds = bass.ds
    ctx = ExitStack()
    with ctx:
        def sb(name, shape, dt=f32):
            return ctx.enter_context(nc.sbuf_tensor(name, shape, dt))

        def sem(name):
            return ctx.enter_context(nc.semaphore(name))

        cst = sb("cst", [P, K_END])
        ident = cst[:, K_ID:K_ID + P]
        identb = sb("identb", [P, P], bf16)
        negb = sb("negb", [P, NT, P], bf16)
        xres = sb("xres", [P, NT, D])
        par = sb("par", [P, 64])
        cw_g = sb("cw_g", [P, 4, 24])
        cw_s = sb("cw_s", [P, 4, 16])
        cb_s = sb("cb_s", [P, 16])
        nw_g = sb("nw_g", [P, 1])
        nw_s = sb("nw_s", [P, KT])
        half = sb("half", [P, 40])
        la = sb("la", [P, NT, 24])
        sp = sb("sp", [P, NT, 24])
        beta = sb("beta", [P, NT, 8])
        ecum = sb("ecum", [P, NT, 24])
        ekw = sb("ekw", [P, NT, 24])
        etot = sb("etot", [P, NT, 24])
        becum = sb("becum", [P, NT, 8])
        r_g = sb("r_g", [P, 2, NT])
        r_slot = sb("r_slot", [P, 2, NT], i32)
        r_idx = sb("r_idx", [P, NB], i32)
        r_tab = sb("r_tab", [1, 8], i32)
        upper = ExitStack()

        def ub_(name, shape, dt=f32):
            return upper.enter_context(nc.sbuf_tensor(name, shape, dt))

        xT = ub_("xT", [P, KT, S])
        ring = ub_("ring", [P, 6, KT, P])
        yT = ub_("yT", [P, 3, KT, S])
        psum = [ctx.enter_context(nc.psum_tensor(f"bank{i}", [P, 512], f32)) for i in range(8)]

        w_loaded = [sem(f"w_loaded{i}") for i in range(6)]
        w_free = [sem(f"w_free{i}") for i in range(6)]
        uses = [0] * 6
        g_ready = [sem(f"gemm_ready{i}") for i in range(2)]
        g_free = [sem(f"gemm_free{i}") for i in range(2)]
        units = [0, 0]

        sp_turn = sem("sp_turn")
        phase_sems = []

        def sem(name):
            phase_sems.append(nc.alloc_semaphore(name=name))
            return phase_sems[-1]

        def end_phase():
            nc.clear_and_free_semaphores(phase_sems)
            nc.all_engine_barrier()
            phase_sems.clear()

        w_in = t["mix_w_in"][0]

        def w_cols(w, c0, n):
            return w[:, ds(c0, n)].rearrange("(k p) c -> p k c", p=P)

        def v3(ap, n=NT):
            return ap.rearrange("p (n c) -> p n c", n=n)


        class Products:

            def __init__(self, per, cols, turns):
                self.per, self.cols, self.turns = per, cols, turns
                self.base, self.us = list(units), list(uses)
                for b in range(2):
                    units[b] += per * turns
                for j in range(2 * per):
                    uses[j] += turns

            def count(self, j, i):
                return i * self.per + (self.base[j % 2] + j // 2 + 1)

            def wait_ready(self, eng, j, i):
                eng.wait_ge(g_ready[j % 2], self.count(j, i))

            def wait_read(self, eng, j, i):
                eng.wait_ge(g_free[j % 2], i * self.per + (self.base[j % 2] + j // 2 + 2))

            def load_first(self, sp_, j):
                sp_.dma_start(ring[:, j], self.cols(j, 0)).then_inc(w_loaded[j], 16)

            def load_next(self, sp_, j, i):
                src = self.cols(j, i + 1)
                self.wait_ready(sp_, j, i)
                sp_.sem_inc(sp_turn, 1)
                sp_.dma_start(ring[:, j], src).then_inc(w_loaded[j], 16)

            def begin(self, pe, j, i):
                pe.wait_ge(w_loaded[j], (i + (self.us[j] + 1)) * 16)
                pe.wait_ge(g_free[j % 2], self.count(j, i))

            def features(self, pe, j, i, rhs, k0=0, k1=KT, cols=S):
                if k0 == 0:
                    self.begin(pe, j, i)
                for k in range(k0, k1):
                    ins = nc.tensor.matmul(psum[j % 2][:, 0:cols], ring[:, j, k, :], rhs[:, k, :], start=(k == 0), stop=(k == KT - 1))
                if k1 == KT:
                    ins.then_inc(g_ready[j % 2], 1)

            def tokens(self, pe, j, i, lhs, n0=0, n1=NT, last=NT):
                if n0 == 0:
                    self.begin(pe, j, i)
                for n in range(n0, n1):
                    for k in range(KT):
                        ins = nc.tensor.matmul(psum[j % 2][:, n * P:(n + 1) * P], lhs[:, k, n * P:(n + 1) * P], ring[:, j, k, :],
                                               start=(k == 0), stop=(k == KT - 1))
                if n1 == last:
                    ins.then_inc(g_ready[j % 2], 1)

        def in_turns(eng, turns, body):
            with eng.Fori(0, turns - 1) as i:
                body(i, True)
            body(turns - 1, False)

        def cols_of(*firsts):
            return lambda j, i: w_cols(w_in, i * firsts[j][1] + firsts[j][0], P)

        ret_g = Products(3, cols_of((C_RQ, P), (C_RK, P), (C_RV, 256), (C_RV + P, 256), (C_RG, 256), (C_RG + P, 256)), RH)
        ssd_g = Products(3, cols_of((C_SX, 256), (C_SX + P, 256), (C_SB, P), (C_SC, P), (C_SZ, 256), (C_SZ + P, 256)), SG)
        gdn_g = Products(2, cols_of((C_GQKV, P), (C_GQKV + 1024, P), (C_GQKV + 2048, P), (C_GZ, P)), GH)
        projs = [t["w_proj_gdn"][0], t["w_proj_ssd"][0], t["w_proj_ret"][0]]
        mrg_g = Products(3, lambda j, i: w_cols(projs[j // 2], i * P, P) if j % 2 else w_cols(w_in, i * P + (C_GATE + (j // 2) * D), P), KT)
        xw = [t["xa_w_q"][0], t["xa_w_k"][0], t["xa_w_v"][0]]
        xa_g = Products(3, lambda j, i: w_cols(xw[j // 2], i * 256 + (j % 2) * P, P), XH)

        with ExitStack() as c2:
            x_tok = xres
            wsm = c2.enter_context(nc.sbuf_tensor("wsm", [P, KT, 32], f32))
            sm = c2.enter_context(nc.sbuf_tensor("sm", [P, 12, NT, 24], f32))
            bsm = c2.enter_context(nc.sbuf_tensor("bsm", [P, 2, NT, 8], f32))
            nea = c2.enter_context(nc.sbuf_tensor("nea", [P, 24], f32))
            s_x, s_cst, s_par = sem("x_in"), sem("cst_in"), sem("par_in")
            s_xt, s_xtf, s_sm = sem("xT_psum"), sem("xT_done"), sem("small_psum")
            s_v, s_a, s_cum, s_half = sem("in_dve"), sem("in_act"), sem("cum_psum"), sem("half_set")
            with nc.Block() as block:
                @block.sync
                def _(sp_):
                    sp_.dma_start(cst[:, :], t["consts"]).then_inc(s_cst, 16)
                    for n in range(NT):
                        sp_.dma_start(x_tok[:, n, :], t["x"][0, n * P:(n + 1) * P, :]).then_inc(s_x, 16)
                    sp_.dma_start(wsm[:, :, 0:8], w_cols(w_in, C_GA, 8)).then_inc(s_par, 16)
                    sp_.dma_start(wsm[:, :, 8:24], w_cols(w_in, C_SDT, 16)).then_inc(s_par, 16)
                    sp_.dma_start(wsm[:, :, 24:32], w_cols(w_in, C_GB, 8)).then_inc(s_par, 16)
                    sp_.dma_start(par[:, :], t["par_rows"]).then_inc(s_par, 16)
                    sp_.dma_start(cw_g[:, :, :], t["conv_g"]).then_inc(s_par, 16)
                    sp_.dma_start(cw_s[:, :, :], t["conv_s"]).then_inc(s_par, 16)
                    sp_.dma_start(cb_s[:, :], t["convb_s"]).then_inc(s_par, 16)
                    sp_.dma_start(nw_g[:, :], t["norm_g"]).then_inc(s_par, 16)
                    sp_.dma_start(nw_s[:, :], t["norm_s"]).then_inc(s_par, 16)
                    for j in range(6):
                        ret_g.load_first(sp_, j)

                @block.gpsimd
                def _(pool):
                    nc.gpsimd.memset(half[:, :], -0.5).then_inc(s_half, 1)

                @block.tensor
                def _(pe):
                    pe.wait_ge(s_cst, 16)
                    pe.wait_ge(s_x, 16 * NT)
                    for k in range(KT):
                        if k >= 4:
                            pe.wait_ge(s_xtf, k - 3)
                        for n in range(NT):
                            ins = nc.tensor.transpose(psum[k % 4][:, n * P:(n + 1) * P], x_tok[:, n, k * P:(k + 1) * P], ident)
                        ins.then_inc(s_xt, 1)
                    pe.wait_ge(s_par, 16 * 9)
                    pe.wait_ge(s_xtf, KT)
                    for n in range(NT):
                        for k in range(KT):
                            ins = nc.tensor.matmul(psum[4][:, n * 32:(n + 1) * 32], xT[:, k, n * P:(n + 1) * P], wsm[:, k, :],
                                                   start=(k == 0), stop=(k == KT - 1))
                    ins.then_inc(s_sm, 1)
                    pe.wait_ge(s_cum, 1)
                    for n in range(NT):
                        nc.tensor.matmul(psum[5][:, n * 24:(n + 1) * 24], cst[:, K_U:K_U + P], la[:, n, :], start=True, stop=True)
                        ins = nc.tensor.matmul(psum[6][:, n * 24:(n + 1) * 24], cst[:, K_ONE:K_ONE + P], la[:, n, :], start=True, stop=True)
                    ins.then_inc(s_sm, 1)

                small = psum[4][:, 0:128].rearrange("p (n c) -> p n c", n=NT)
                cum_ps = psum[5][:, 0:96].rearrange("p (n c) -> p n c", n=NT)
                tot_ps = psum[6][:, 0:96].rearrange("p (n c) -> p n c", n=NT)

                @block.vector
                def _(dve):
                    link = Count(dve, s_v, 0)
                    for b in range(2):
                        dve.sem_inc(g_free[b], 1)
                    for k in range(KT):
                        dve.wait_ge(s_xt, k + 1)
                        nc.vector.tensor_copy(xT[:, k, :], psum[k % 4][:, :]).then_inc(s_xtf, 1)
                    dve.wait_ge(s_par, 16 * 9)
                    nc.vector.tensor_copy(identb[:, :], ident)
                    nc.vector.tensor_copy(negb[:, :, :], cst[:, K_NEG:K_NEG + P].unsqueeze(1).to_broadcast([P, NT, P]))
                    nc.vector.tensor_scalar(cw_g[:, :, :], cw_g[:, :, :], 0.5, None, ALU.mult)
                    nc.vector.tensor_scalar(cw_s[:, :, :], cw_s[:, :, :], 0.5, None, ALU.mult)
                    nc.vector.tensor_scalar(cb_s[:, :], cb_s[:, :], 0.5, None, ALU.mult)
                    dve.wait_ge(s_sm, 1)
                    z, m, neg, u, w, d, d0, dd, r, lnw, v, v2 = [sm[:, j] for j in range(12)]
                    nc.vector.tensor_scalar(bsm[:, 0], small[:, :, 24:32], -1.0, None, ALU.mult)
                    link(nc.vector.tensor_tensor(z, small[:, :, 0:24], par[:, 24:48].unsqueeze(1).to_broadcast([P, NT, 24]), ALU.add))
                    link(nc.vector.tensor_scalar(m, z, 0.0, None, ALU.max))
                    link(nc.vector.scalar_tensor_tensor(out=neg, in0=z, scalar=0.0, in1=m, op0=ALU.min, op1=ALU.subtract))
                    dve.wait_ge(s_a, 3)
                    link(nc.vector.tensor_scalar(w, u, 1.0, None, ALU.add))
                    link(nc.vector.tensor_scalar(d, w, -1.0, None, ALU.add))
                    link(nc.vector.tensor_scalar(d0, d, 0.0, None, ALU.is_equal))
                    link(nc.vector.tensor_tensor(dd, d, d0, ALU.add))
                    link(nc.vector.reciprocal(r, dd))
                    link(nc.vector.tensor_tensor(r, r, u, ALU.mult))
                    dve.wait_ge(s_a, 4)
                    link(nc.vector.tensor_tensor(v, lnw, r, ALU.mult))
                    link(nc.vector.tensor_tensor(v2, u, d0, ALU.mult))
                    link(nc.vector.tensor_tensor(v, v, v2, ALU.add))
                    link(nc.vector.tensor_tensor(sp[:, :, :], v, m, ALU.add))
                    link(nc.vector.tensor_tensor(la[:, :, :], sp[:, :, :], nea[:, :].unsqueeze(1).to_broadcast([P, NT, 24]), ALU.mult))
                    nc.vector.tensor_scalar(la[:, :, :], la[:, :, :], -1.0, None, ALU.mult).then_inc(s_cum, 1)
                    link(nc.vector.tensor_scalar(bsm[:, 0], bsm[:, 1], 1.0, None, ALU.add))
                    link(nc.vector.reciprocal(beta[:, :, :], bsm[:, 0]))
                    dve.wait_ge(s_sm, 2)
                    link(nc.vector.tensor_copy(z, cum_ps))
                    nc.vector.tensor_tensor(v, tot_ps, z, ALU.subtract).then_inc(s_cum, 1)
                    dve.wait_ge(s_a, 7)
                    nc.vector.tensor_tensor(becum[:, :, :], beta[:, :, :], ecum[:, :, 0:8], ALU.mult)

                @block.scalar
                def _(act):
                    act.wait_ge(s_v, 3)
                    nc.scalar.activation(sm[:, 3], sm[:, 2], ACT.Exp).then_inc(s_a, 1)
                    nc.scalar.activation(bsm[:, 1], bsm[:, 0], ACT.Exp).then_inc(s_a, 1)
                    nc.scalar.activation(nea[:, :], par[:, 0:24], ACT.Exp).then_inc(s_a, 1)
                    act.wait_ge(s_v, 4)
                    nc.scalar.activation(sm[:, 9], sm[:, 4], ACT.Ln).then_inc(s_a, 1)
                    act.wait_ge(s_cum, 2)
                    nc.scalar.activation(ekw[:, :, :], sm[:, 10], ACT.Exp).then_inc(s_a, 1)
                    nc.scalar.activation(ecum[:, :, :], cum_ps, ACT.Exp).then_inc(s_a, 1)
                    nc.scalar.activation(etot[:, :, :], tot_ps, ACT.Exp).then_inc(s_a, 1)

        end_phase()
        with ExitStack() as c2:
            def b2(name, shape, dt=f32):
                return c2.enter_context(nc.sbuf_tensor("r_" + name, shape, dt))

            t1, t2 = b2("t1", [P, NT, 2, 64]), b2("t2", [P, NT, 2, 64])
            qr, kr, qd, kd = [b2(n_, [P, NT, P]) for n_ in ("qr", "kr", "qd", "kd")]
            kT, qT, qdT, M = [b2(n_, [P, S]) for n_ in ("kT", "qT", "qdT", "M")]
            v = b2("v", [P, NT, 2, P])
            gh, gt, sg = b2("gh", [P, 2, S]), b2("gt", [P, 2, S]), b2("sg", [P, 2, S])
            St = b2("St", [P, 3, 2 * P])
            bn, mv = b2("bn", [P, NT, 6]), b2("mv", [P, NT, 2])
            var, rs = b2("var", [P, NT]), b2("rs", [P, NT])
            on = b2("on", [P, NT, 2, P])
            names = ("rot rot_done kd_done tokT_psum tokT_done score_psum m_done v_done gh_done gt_done sg_done kv_psum state o_psum "
                     "stat stat_all rs_in rs_out on_ready oT_psum y_done").split()
            q_ = {n_: sem("r_" + n_) for n_ in names}
            g = ret_g

            with nc.Block() as block:
                @block.sync
                def _(sp_):
                    in_turns(sp_, RH, lambda i, more: [g.load_next(sp_, j, i) for j in range(6)] if more else None)
                    for j in range(6):
                        g.wait_ready(sp_, j, RH - 1)
                        ssd_g.load_first(sp_, j)

                @block.tensor
                def _(pe):
                    def body(i, more):
                        g.tokens(pe, 2, i, xT)
                        pe.wait_ge(q_["y_done"], i * 2)
                        for j, src in enumerate((kr, qr, qd)):
                            pe.wait_ge(q_["rot_done"], i * 3 + (2, 1, 3)[j])
                            for n in range(NT):
                                ins = nc.tensor.transpose(psum[2 + j][:, n * P:(n + 1) * P], src[:, n, :], ident)
                            ins.then_inc(q_["tokT_psum"], 1)
                        pe.wait_ge(q_["tokT_done"], i * 3 + 3)
                        for n in range(NT):
                            c = slice(n * P, (n + 1) * P)
                            ins = nc.tensor.matmul(psum[2][:, c], kT[:, c], qT[:, c], start=True, stop=True)
                        ins.then_inc(q_["score_psum"], 1)
                        g.tokens(pe, 3, i, xT)
                        g.features(pe, 4, i, xT)
                        pe.wait_ge(q_["v_done"], i * 2 + 2)
                        pe.wait_ge(q_["kd_done"], i + 1)
                        for n in range(NT - 1):
                            bank, c0 = psum[3 + n // 2], (n % 2) * 256
                            ins = nc.tensor.matmul(bank[:, c0:c0 + 256], kd[:, n, :], v[:, n].rearrange("p a c -> p (a c)"), start=True, stop=True)
                        ins.then_inc(q_["kv_psum"], 1)
                        g.features(pe, 5, i, xT)
                        pe.wait_ge(q_["m_done"], i + 1)
                        pe.wait_ge(q_["state"], i * 3 + 3)
                        for n in range(NT):
                            c = slice(n * P, (n + 1) * P)
                            bank, c0 = psum[6 + n // 2], (n % 2) * 256
                            if n:
                                nc.tensor.matmul(bank[:, c0:c0 + 256], qdT[:, c], St[:, n - 1, :], start=True, stop=False)
                            ins = nc.tensor.matmul(bank[:, c0:c0 + 256], M[:, c], v[:, n].rearrange("p a c -> p (a c)"), start=(n == 0), stop=True)
                        ins.then_inc(q_["o_psum"], 1)
                        if more:
                            g.tokens(pe, 0, i + 1, xT)
                            g.tokens(pe, 1, i + 1, xT)
                        pe.wait_ge(q_["on_ready"], i + 1)
                        for a in range(2):
                            for n in range(NT):
                                ins = nc.tensor.transpose(psum[3 + a][:, n * P:(n + 1) * P], on[:, n, a, :], ident)
                            ins.then_inc(q_["oT_psum"], 1)

                    g.tokens(pe, 0, 0, xT)
                    g.tokens(pe, 1, 0, xT)
                    in_turns(pe, RH, body)

                @block.scalar
                def _(act):
                    def body(i, more):
                        for j, (dst, sc) in enumerate(((kT, P ** -0.5), (qT, 1.0), (qdT, 1.0))):
                            act.wait_ge(q_["tokT_psum"], i * 3 + (j + 1))
                            nc.scalar.activation(dst[:, :], psum[2 + j][:, :], ACT.Copy, scale=sc).then_inc(q_["tokT_done"], 1)
                        for a in range(2):
                            g.wait_ready(act, 2 + a, i)
                            nc.scalar.activation(v[:, :, a, :], v3(psum[a][:, :]), ACT.Copy).then_inc(g_free[a], 1)
                            g.wait_read(act, 2 + a, i)
                            act.sem_inc(q_["v_done"], 1)
                        for a in range(2):
                            g.wait_ready(act, 4 + a, i)
                            if a == 0:
                                act.wait_ge(q_["y_done"], i * 2)
                            nc.scalar.activation(gh[:, a, :], psum[a][:, :], ACT.Copy, scale=0.5).then_inc(q_["gh_done"], 1)
                            nc.scalar.activation(gt[:, a, :], psum[a][:, :], ACT.Tanh, scale=0.5).then_inc(g_free[a], 1)

                    in_turns(act, RH, body)

                @block.gpsimd
                def _(pool):
                    with pool.Fori(0, RH) as i:
                        pool.wait_ge(q_["rs_in"], i + 1)
                        nc.gpsimd.tensor_tensor(rs[:, :], var[:, :], half[:, 0:NT], ALU.pow).then_inc(q_["rs_out"], 1)

                @block.vector
                def _(dve):
                    cos = cst[:, K_COS:K_COS + NT * 64].rearrange("p (n c) -> p n c", n=NT).unsqueeze(2).to_broadcast([P, NT, 2, 64])
                    sin = cst[:, K_SIN:K_SIN + NT * 64].rearrange("p (n c) -> p n c", n=NT).unsqueeze(2).to_broadcast([P, NT, 2, 64])

                    def rotate(j, i):
                        dst = (qr, kr)[j]
                        g.wait_ready(dve, j, i)
                        ps = psum[j][:, :].rearrange("p (n a c) -> p n a c", n=NT, a=2)
                        nc.vector.tensor_tensor(t1[:, :, :, :], ps, cos, ALU.mult).then_inc(q_["rot"], 1)
                        nc.vector.tensor_tensor(t2[:, :, :, :], ps, sin, ALU.mult).then_inc(g_free[j], 1)
                        g.wait_read(dve, j, i)
                        dve.wait_ge(q_["rot"], i * 4 + (2 * j + 1))
                        nc.vector.tensor_tensor(dst[:, :, 0:64], t1[:, :, 0, :], t2[:, :, 1, :], ALU.subtract).then_inc(q_["rot"], 1)
                        nc.vector.tensor_tensor(dst[:, :, 64:128], t1[:, :, 1, :], t2[:, :, 0, :], ALU.add).then_inc(q_["rot_done"], 1)
                        dve.wait_ge(q_["rot_done"], i * 3 + (j + 1))
                        dve.wait_ge(q_["rot"], i * 4 + (2 * j + 2))

                    def decayed(i):
                        nc.vector.tensor_scalar(qd[:, :, :], qr[:, :, :], cst[:, ds(i + K_RCUM, 1)], None, ALU.mult).then_inc(q_["rot_done"], 1)
                        nc.vector.tensor_scalar(kd[:, :, :], kr[:, :, :], cst[:, ds(i + K_RKW, 1)], P ** -0.5, ALU.mult, ALU.mult).then_inc(q_["kd_done"], 1)

                    def body(i, more):
                        dve.wait_ge(q_["score_psum"], i + 1)
                        nc.vector.tensor_tensor(v3(M[:, :]), v3(psum[2][:, :]), cst[:, ds(i * P + K_RDEC, P)].unsqueeze(1).to_broadcast([P, NT, P]),
                                                ALU.mult).then_inc(q_["m_done"], 1)
                        dve.wait_ge(q_["kv_psum"], i + 1)
                        for n in range(NT - 1):
                            kv = psum[3 + n // 2][:, (n % 2) * 256:(n % 2) * 256 + 256]
                            if n == 0:
                                nc.vector.tensor_copy(St[:, 0, :], kv).then_inc(q_["state"], 1)
                            else:
                                dve.wait_ge(q_["state"], i * 3 + n)
                                nc.vector.scalar_tensor_tensor(out=St[:, n, :], in0=St[:, n - 1, :], scalar=cst[:, ds(i + K_RTOT, 1)], in1=kv,
                                                               op0=ALU.mult, op1=ALU.add).then_inc(q_["state"], 1)
                        for a in range(2):
                            g.wait_read(dve, 4 + a, i)
                            nc.vector.scalar_tensor_tensor(out=sg[:, a, :], in0=gt[:, a, :], scalar=1.0, in1=gh[:, a, :], op0=ALU.add, op1=ALU.mult).then_inc(q_["sg_done"], 1)
                        dve.wait_ge(q_["o_psum"], i + 1)
                        for n in range(NT):
                            nc.vector.bn_stats(bn[:, n, :], psum[6 + n // 2][:, (n % 2) * 256:(n % 2) * 256 + 256]).then_inc(q_["stat"], 1)
                        dve.wait_ge(q_["stat"], i * 8 + 4)
                        dve.sem_inc(q_["stat_all"], 1)
                        for n in range(NT):
                            nc.vector.bn_aggr(mv[:, n, :], bn[:, n, :]).then_inc(q_["stat"], 1)
                        dve.wait_ge(q_["stat"], i * 8 + 8)
                        nc.vector.tensor_scalar(var[:, :], mv[:, :, 1], LN_EPS, None, ALU.add).then_inc(q_["rs_in"], 1)
                        dve.wait_ge(q_["rs_out"], i + 1)
                        for n in range(NT):
                            ins = nc.vector.tensor_scalar(on[:, n].rearrange("p a c -> p (a c)"), psum[6 + n // 2][:, (n % 2) * 256:(n % 2) * 256 + 256],
                                                          mv[:, n, 0:1], rs[:, n:n + 1], ALU.subtract, ALU.mult)
                        ins.then_inc(q_["on_ready"], 1)
                        if more:
                            rotate(0, i + 1)
                            rotate(1, i + 1)
                            decayed(i + 1)
                        dve.wait_ge(q_["sg_done"], i * 2 + 2)
                        for a in range(2):
                            dve.wait_ge(q_["oT_psum"], i * 2 + (a + 1))
                            nc.vector.tensor_tensor(yT[:, 2, ds(i * 2 + a, 1), :].rearrange("p a c -> p (a c)"), psum[3 + a][:, :], sg[:, a, :], ALU.mult).then_inc(q_["y_done"], 1)

                    rotate(0, 0)
                    rotate(1, 0)
                    decayed(0)
                    in_turns(dve, RH, body)

        end_phase()
        with ExitStack() as c2:
            def b2(name, shape, dt=f32):
                return c2.enter_context(nc.sbuf_tensor("s_" + name, shape, dt))

            acc, th, fm = b2("acc", [P, 4, S]), b2("th", [P, 4, S]), b2("fm", [P, 4, S])
            zh, zt, sz = b2("zh", [P, NT, 2, P]), b2("zt", [P, NT, 2, P]), b2("sz", [P, NT, 2, P])
            xs, bt = b2("xs", [P, NT, 2, P]), b2("bt", [P, NT, P])
            v, vk, y = b2("v", [P, NT, 256]), b2("vk", [P, NT, 256]), b2("y", [P, NT, 256])
            lla, dec, M = b2("lla", [P, SR, NT, P]), b2("dec", [P, SR, S]), b2("M", [P, SR, S])
            St, ts = b2("St", [P, 3, 256]), b2("ts", [P, 2, 256])
            yi = b2("yi", [P, 3, 256])
            ssq, rs = b2("ssq", [P, NT]), b2("rs", [P, NT])
            names = ("conv_acc conv_th conv_fm fm_done cv zh_done zt_done sz_done tok_psum tok_done lla_ready dec_psum dec_ready score_psum m_done "
                     "v_done vk_done kv_psum st state y_psum yw sq_done rs_in rs_out on_ready oT_psum y_done").split()
            q_ = {n_: sem("s_" + n_) for n_ in names}
            g = ssd_g

            with nc.Block() as block:
                @block.sync
                def _(sp_):
                    in_turns(sp_, SG, lambda i, more: [g.load_next(sp_, j, i) for j in range(6)] if more else None)
                    for j in range(4):
                        g.wait_ready(sp_, j, SG - 1)
                        gdn_g.load_first(sp_, j)

                @block.tensor
                def _(pe):
                    def decays(i, r):
                        pe.wait_ge(q_["lla_ready"], i * 4 + (r + 1))
                        if r >= 2:
                            pe.wait_ge(q_["dec_ready"], i * 4 + (r - 1))
                        b = psum[6 + r % 2]
                        for n in range(NT):
                            nc.tensor.matmul(b[:, n * P:(n + 1) * P], lla[:, r, n, :], cst[:, K_U:K_U + P], start=(n == 0), stop=False, skip_group_check=True)
                        nc.tensor.matmul(b[:, :], identb[:, :], negb[:, :, :].rearrange("p n c -> p (n c)"), start=False, stop=True,
                                         skip_group_check=True).then_inc(q_["dec_psum"], 1)

                    def body(i, more):
                        for j in range(3):
                            pe.wait_ge(q_["fm_done"], i * 4 + (j + 1))
                            for n in range(NT):
                                ins = nc.tensor.transpose(psum[2 + j][:, n * P:(n + 1) * P], fm[:, j, n * P:(n + 1) * P], ident)
                            ins.then_inc(q_["tok_psum"], 1)
                        pe.wait_ge(q_["yw"], i * 7)
                        decays(i, 0)
                        decays(i, 1)
                        pe.wait_ge(q_["fm_done"], i * 4 + 4)
                        for n in range(NT):
                            c = slice(n * P, (n + 1) * P)
                            ins = nc.tensor.matmul(psum[5][:, c], fm[:, 2, c], fm[:, 3, c], start=True, stop=True)
                        ins.then_inc(q_["score_psum"], 1)
                        g.tokens(pe, 4, i, xT, 0, 2)
                        decays(i, 2)
                        decays(i, 3)
                        g.tokens(pe, 4, i, xT, 2, 4)
                        pe.wait_ge(q_["tok_done"], i * 3 + 3)
                        pe.wait_ge(q_["vk_done"], i + 1)
                        for n in range(NT - 1):
                            bank, c0 = psum[2 + n // 2], (n % 2) * 256
                            ins = nc.tensor.matmul(bank[:, c0:c0 + 256], bt[:, n, :], vk[:, n, :], start=True, stop=True)
                        ins.then_inc(q_["kv_psum"], 1)
                        g.tokens(pe, 5, i, xT)
                        pe.wait_ge(q_["m_done"], i * 4 + 4)
                        for n in range(NT):
                            for r in range(SR):
                                c0 = (n % 2) * 256 + r * 64
                                ins = nc.tensor.matmul(psum[6 + n // 2][:, c0:c0 + 64], M[:, r, n * P:(n + 1) * P], v[:, n, r * 64:(r + 1) * 64], start=True, stop=True)
                        ins.then_inc(q_["y_psum"], 1)
                        pe.wait_ge(q_["state"], i * 3 + 3)
                        for n in range(1, NT):
                            c0 = (n % 2) * 256
                            ins = nc.tensor.matmul(psum[4 + n // 2][:, c0:c0 + 256], fm[:, 3, n * P:(n + 1) * P], St[:, n - 1, :], start=True, stop=True)
                        ins.then_inc(q_["y_psum"], 1)
                        if more:
                            for j in range(2):
                                g.features(pe, j, i + 1, xT)
                        pe.wait_ge(q_["on_ready"], i + 1)
                        for a in range(2):
                            for n in range(NT):
                                ins = nc.tensor.transpose(psum[2 + a][:, n * P:(n + 1) * P], vk[:, n, a * P:(a + 1) * P], ident)
                            ins.then_inc(q_["oT_psum"], 1)
                        if more:
                            for j in range(2, 4):
                                g.features(pe, j, i + 1, xT)
                        pe.wait_ge(q_["y_done"], i * 2 + 2)

                    for j in range(4):
                        g.features(pe, j, 0, xT)
                    in_turns(pe, SG, body)

                @block.scalar
                def _(act):
                    def conv(j, i):
                        ch = (i * 2, i * 2 + 1, i + 8, i + 12)[j]
                        g.wait_ready(act, j, i)
                        nc.scalar.activation(acc[:, j, :], psum[j % 2][:, :], ACT.Identity, scale=cw_s[:, 3, ds(ch, 1)], bias=cb_s[:, ds(ch, 1)]).then_inc(q_["conv_acc"], 1)
                        g.wait_read(act, j, i)
                        nc.scalar.activation(th[:, j, :], acc[:, j, :], ACT.Tanh).then_inc(q_["conv_th"], 1)

                    def body(i, more):
                        for j, dst in enumerate((xs[:, :, 0, :], xs[:, :, 1, :], bt[:, :, :])):
                            act.wait_ge(q_["tok_psum"], i * 3 + (j + 1))
                            nc.scalar.activation(dst, v3(psum[2 + j][:, :]), ACT.Copy).then_inc(q_["tok_done"], 1)
                        for r in range(SR):
                            act.wait_ge(q_["dec_psum"], i * 4 + (r + 1))
                            nc.scalar.activation(dec[:, r, :], psum[6 + r % 2][:, :], ACT.Exp).then_inc(q_["dec_ready"], 1)
                        for a in range(2):
                            g.wait_ready(act, 4 + a, i)
                            nc.scalar.activation(zh[:, :, a, :], v3(psum[a][:, :]), ACT.Copy, scale=0.5).then_inc(q_["zh_done"], 1)
                            nc.scalar.activation(zt[:, :, a, :], v3(psum[a][:, :]), ACT.Tanh, scale=0.5).then_inc(g_free[a], 1)
                        if more:
                            conv(0, i + 1)
                        act.wait_ge(q_["yw"], i * 7 + 7)
                        nc.scalar.activation(v[:, :, :], y[:, :, :], ACT.Square).then_inc(q_["sq_done"], 1)
                        if more:
                            conv(1, i + 1)
                        for a in range(2):
                            act.wait_ge(q_["oT_psum"], i * 2 + (a + 1))
                            nc.scalar.activation(yT[:, 1, ds(i * 2 + a, 1), :].rearrange("p a c -> p (a c)"), psum[2 + a][:, :], ACT.Copy,
                                                 scale=nw_s[:, ds(i * 2 + a, 1)]).then_inc(q_["y_done"], 1)
                        if more:
                            conv(2, i + 1)
                            conv(3, i + 1)

                    for j in range(4):
                        conv(j, 0)
                    in_turns(act, SG, body)

                @block.gpsimd
                def _(pool):
                    with pool.Fori(0, SG) as i:
                        for r in range(SR):
                            nc.gpsimd.tensor_tensor(lla[:, r], cst[:, K_L:K_L + P].unsqueeze(1).to_broadcast([P, NT, P]),
                                                    la[:, :, ds(i * 4 + (8 + r), 1)].to_broadcast([P, NT, P]), ALU.mult).then_inc(q_["lla_ready"], 1)
                        pool.wait_ge(q_["rs_in"], i + 1)
                        nc.gpsimd.tensor_tensor(rs[:, :], ssq[:, :], half[:, 0:NT], ALU.pow).then_inc(q_["rs_out"], 1)

                def heads(ap):
                    return ap.unsqueeze(3).to_broadcast([P, ap.shape[1], 4, 64])

                def r4(ap):
                    return ap.rearrange("p n (r c) -> p n r c", r=4)

                @block.vector
                def _(dve):
                    def conv(j, i):
                        ch = (i * 2, i * 2 + 1, i + 8, i + 12)[j]
                        dve.wait_ge(q_["conv_acc"], i * 4 + (j + 1))
                        p = psum[j % 2]
                        for m in (1, 2):
                            nc.vector.scalar_tensor_tensor(out=acc[:, j, m:S], in0=p[:, 0:S - m], scalar=cw_s[:, 3 - m, ds(ch, 1)],
                                                           in1=acc[:, j, m:S], op0=ALU.mult, op1=ALU.add).then_inc(q_["conv_fm"], 1)
                            dve.wait_ge(q_["conv_fm"], i * 8 + (2 * j + m))
                        nc.vector.scalar_tensor_tensor(out=acc[:, j, 3:S], in0=p[:, 0:S - 3], scalar=cw_s[:, 0, ds(ch, 1)],
                                                       in1=acc[:, j, 3:S], op0=ALU.mult, op1=ALU.add).then_inc(g_free[j % 2], 1)

                    def silu(j, i):
                        dve.wait_ge(q_["conv_th"], i * 4 + (j + 1))
                        nc.vector.scalar_tensor_tensor(out=fm[:, j, :], in0=th[:, j, :], scalar=1.0, in1=acc[:, j, :], op0=ALU.add, op1=ALU.mult).then_inc(q_["fm_done"], 1)

                    def body(i, more):
                        link = Count(dve, q_["cv"], 5, i)
                        dve.wait_ge(q_["tok_done"], i * 3 + 3)
                        xs4 = xs[:, :, :, :].rearrange("p n a (b c) -> p n (a b) c", b=2)
                        nc.vector.tensor_tensor(r4(v[:, :, :]), xs4, heads(sp[:, :, ds(i * 4 + 8, 4)]), ALU.mult).then_inc(q_["v_done"], 1)
                        dve.wait_ge(q_["v_done"], i + 1)
                        nc.vector.tensor_tensor(r4(vk[:, :, :]), r4(v[:, :, :]), heads(ekw[:, :, ds(i * 4 + 8, 4)]), ALU.mult).then_inc(q_["vk_done"], 1)
                        dve.wait_ge(q_["score_psum"], i + 1)
                        for r in range(SR):
                            dve.wait_ge(q_["dec_ready"], i * 4 + (r + 1))
                            nc.vector.tensor_tensor(M[:, r, :], psum[5][:, :], dec[:, r, :], ALU.mult).then_inc(q_["m_done"], 1)
                        dve.wait_ge(q_["kv_psum"], i + 1)
                        for n in range(NT - 1):
                            kv = psum[2 + n // 2][:, (n % 2) * 256:(n % 2) * 256 + 256]
                            if n == 0:
                                nc.vector.tensor_copy(St[:, 0, :], kv).then_inc(q_["state"], 1)
                            else:
                                dve.wait_ge(q_["state"], i * 3 + n)
                                link(nc.vector.tensor_tensor(ts[:, n - 1, :].rearrange("p (r c) -> p r c", r=4), St[:, n - 1, :].rearrange("p (r c) -> p r c", r=4),
                                                             etot[:, n, ds(i * 4 + 8, 4)].unsqueeze(2).to_broadcast([P, 4, 64]), ALU.mult))
                                nc.vector.tensor_tensor(St[:, n, :], ts[:, n - 1, :], kv, ALU.add).then_inc(q_["state"], 1)
                        link(nc.vector.tensor_tensor(r4(y[:, :, :]), xs4, heads(par[:, ds(i * 4 + 48, 4)].unsqueeze(1).to_broadcast([P, NT, 4])), ALU.mult))
                        for a in range(2):
                            g.wait_read(dve, 4 + a, i)
                        link(nc.vector.scalar_tensor_tensor(out=sz[:, :, :, :].rearrange("p n a c -> p (n a c)"), in0=zt[:, :, :, :].rearrange("p n a c -> p (n a c)"),
                                                            scalar=1.0, in1=zh[:, :, :, :].rearrange("p n a c -> p (n a c)"), op0=ALU.add, op1=ALU.mult))
                        dve.wait_ge(q_["y_psum"], i * 2 + 2)
                        for b in range(2):
                            nc.vector.tensor_tensor(y[:, 2 * b:2 * b + 2, :].rearrange("p n c -> p (n c)"), y[:, 2 * b:2 * b + 2, :].rearrange("p n c -> p (n c)"),
                                                    psum[6 + b][:, :], ALU.add).then_inc(q_["yw"], 1)
                        for n in range(1, NT):
                            nc.vector.tensor_tensor(yi[:, n - 1, :].rearrange("p (r c) -> p r c", r=4), psum[4 + n // 2][:, (n % 2) * 256:(n % 2) * 256 + 256].rearrange("p (r c) -> p r c", r=4),
                                                    ecum[:, n, ds(i * 4 + 8, 4)].unsqueeze(2).to_broadcast([P, 4, 64]), ALU.mult).then_inc(q_["yw"], 1)
                        dve.wait_ge(q_["yw"], i * 7 + 5)
                        nc.vector.tensor_tensor(y[:, 1:NT, :], y[:, 1:NT, :], yi[:, :, :], ALU.add).then_inc(q_["yw"], 1)
                        dve.wait_ge(q_["yw"], i * 7 + 6)
                        nc.vector.tensor_tensor(y[:, :, :], y[:, :, :], sz[:, :, :, :].rearrange("p n a c -> p n (a c)"), ALU.mult).then_inc(q_["yw"], 1)
                        if more:
                            conv(0, i + 1)
                        dve.wait_ge(q_["sq_done"], i + 1)
                        link(nc.vector.tensor_reduce(ssq[:, :], v[:, :, :], AX.X, ALU.add))
                        nc.vector.tensor_scalar(ssq[:, :], ssq[:, :], 1.0 / 256, RMS_EPS, ALU.mult, ALU.add).then_inc(q_["rs_in"], 1)
                        if more:
                            silu(0, i + 1)
                        dve.wait_ge(q_["rs_out"], i + 1)
                        nc.vector.tensor_tensor(vk[:, :, :], y[:, :, :], rs[:, :].unsqueeze(2).to_broadcast([P, NT, 256]), ALU.mult).then_inc(q_["on_ready"], 1)
                        if more:
                            for j in range(1, 4):
                                conv(j, i + 1)
                                silu(j, i + 1)
                        link.done()

                    for j in range(4):
                        conv(j, 0)
                        silu(j, 0)
                    in_turns(dve, SG, body)

        end_phase()
        with ExitStack() as c2:
            def b2(name, shape, dt=f32):
                return c2.enter_context(nc.sbuf_tensor("g_" + name, shape, dt))

            acc, th = b2("acc", [P, 4, S]), b2("th", [P, 4, S])
            fm = b2("fm", [P, 4, S])
            sq = b2("sq", [P, 3, NT, P])
            ssq, rs = b2("ssq", [P, 12]), b2("rs", [P, 12])
            kn, kb, kbe, kd = [b2(n_, [P, NT, P]) for n_ in ("kn", "kb", "kbe", "kd")]
            qn, qd, vb = [b2(n_, [P, NT, P]) for n_ in ("qn", "qd", "vb")]
            knT, kbT, qnT, qdT = [b2(n_, [P, S]) for n_ in ("knT", "kbT", "qnT", "qdT")]
            lla, dec = b2("lla", [P, NT, P]), b2("dec", [P, S])
            AT, atT = b2("AT", [P, S]), b2("atT", [P, S])
            Cl = b2("Cl", [P, LEVELS - 1, S])
            T, TT, X = b2("T", [P, S]), b2("TT", [P, S]), b2("X", [P, S])
            nwT, vn = b2("nwT", [P, S]), b2("vn", [P, S])
            St = b2("St", [P, 3, P])
            on = b2("on", [P, S])

            names = ("conv_acc conv_th conv_fm fm_done tok_psum tok_norm rs_in rs_out tokT_psum tokT_done lla_ready dec_psum dec_ready "
                     "score_psum score_done cl_ready t0_psum lev_x_psum lev_x lev_y_psum lev_t wT_psum wT_ready vn_psum vn_ready kv_psum state "
                     "z_acc lev_tt x0 o_psum on_ready oT_psum y_done tok_sq g_dve g_lv").split()
            q_ = {n_: sem("g_" + n_) for n_ in names}
            g = gdn_g

            with nc.Block() as block:
                @block.sync
                def _(sp_):
                    in_turns(sp_, GH, lambda i, more: [g.load_next(sp_, j, i) for j in range(4)] if more else None)
                    for j in range(6):
                        if j < 4:
                            g.wait_ready(sp_, j, GH - 1)
                        mrg_g.load_first(sp_, j)

                @block.tensor
                def _(pe):
                    def four(dst, lhs, rhs):
                        for n in range(NT):
                            c = slice(n * P, (n + 1) * P)
                            ins = nc.tensor.matmul(dst[:, c], lhs[:, c], rhs[:, c], start=True, stop=True)
                        return ins

                    def turned(bank, src):
                        for n in range(NT):
                            ins = nc.tensor.transpose(bank[:, n * P:(n + 1) * P], src(n), ident)
                        return ins

                    def body(i, more):
                        def ahead(j, k0, k1):
                            if more:
                                g.features(pe, j, i + 1, xT, k0, k1)

                        for j in range(3):
                            pe.wait_ge(q_["fm_done"], i * 4 + (j + 1))
                            turned(psum[2 + j], lambda n: fm[:, j, n * P:(n + 1) * P]).then_inc(q_["tok_psum"], 1)
                        g.features(pe, 3, i, xT)
                        pe.wait_ge(q_["lla_ready"], i + 1)
                        for n in range(NT):
                            nc.tensor.matmul(psum[5][:, n * P:(n + 1) * P], lla[:, n, :], cst[:, K_U:K_U + P], start=(n == 0), stop=False, skip_group_check=True)
                        nc.tensor.matmul(psum[5][:, :], identb[:, :], negb[:, :, :].rearrange("p n c -> p (n c)"), start=False, stop=True,
                                         skip_group_check=True).then_inc(q_["dec_psum"], 1)
                        pe.wait_ge(q_["on_ready"], i)
                        for j, src in enumerate((kn, kb, qn, qd)):
                            pe.wait_ge(q_["tok_norm"], i * 7 + (1, 2, 4, 5)[j])
                            turned(psum[(6, 7, 2, 3)[j]], lambda n: src[:, n, :]).then_inc(q_["tokT_psum"], 1)
                        ahead(0, 0, 2)
                        pe.wait_ge(q_["tokT_done"], i * 4 + 2)
                        four(psum[6], knT, kbT).then_inc(q_["score_psum"], 1)
                        ahead(0, 2, 3)
                        pe.wait_ge(q_["tokT_done"], i * 4 + 4)
                        four(psum[7], knT, qnT).then_inc(q_["score_psum"], 1)
                        ahead(0, 3, 6)
                        pe.wait_ge(q_["lev_tt"], i * 7 + 1)
                        turned(psum[4], lambda n: TT[:, n * P:(n + 1) * P]).then_inc(q_["t0_psum"], 1)
                        ahead(0, 6, 8)
                        for l in range(1, LEVELS):
                            pe.wait_ge(q_["cl_ready"], i * 6 + l)
                            pe.wait_ge(q_["lev_t"], i * 6 + l)
                            four(psum[5], Cl[:, l - 1], T).then_inc(q_["lev_x_psum"], 1)
                            ahead(1, l - 1, l)
                            pe.wait_ge(q_["lev_x"], i * 6 + l)
                            pe.wait_ge(q_["lev_tt"], i * 7 + l)
                            if l < LEVELS - 1:
                                four(psum[7], TT, X).then_inc(q_["lev_y_psum"], 1)
                            four(psum[6], X, TT).then_inc(q_["lev_y_psum"], 1)
                        ahead(1, 6, 8)
                        pe.wait_ge(q_["lev_tt"], i * 7 + 7)
                        for n in range(NT):
                            c = slice(n * P, (n + 1) * P)
                            ins = nc.tensor.matmul(psum[4][:, c], kbe[:, n, :], TT[:, c], start=True, stop=True)
                        ins.then_inc(q_["wT_psum"], 1)
                        pe.wait_ge(q_["score_done"], i * 2 + 2)
                        for n in range(NT):
                            c = slice(n * P, (n + 1) * P)
                            ins = nc.tensor.matmul(psum[5][:, c], TT[:, c], vb[:, n, :], start=True, stop=(n == 0))
                            if n:
                                pe.wait_ge(q_["wT_ready"], i + 1)
                                pe.wait_ge(q_["state"], i * 3 + n)
                                ins = nc.tensor.matmul(psum[5][:, c], nwT[:, c], St[:, n - 1, :], start=False, stop=True)
                            ins.then_inc(q_["vn_psum"], 1)
                            ahead(2, n, n + 1)
                            pe.wait_ge(q_["vn_ready"], i * 4 + (n + 1))
                            if n < NT - 1:
                                nc.tensor.matmul(psum[6][:, c], kd[:, n, :], vn[:, c], start=True, stop=True).then_inc(q_["kv_psum"], 1)
                            if n:
                                nc.tensor.matmul(psum[7][:, c], qdT[:, c], St[:, n - 1, :], start=True, stop=False)
                            ins = nc.tensor.matmul(psum[7][:, c], atT[:, c], vn[:, c], start=(n == 0), stop=True)
                        ins.then_inc(q_["o_psum"], 1)
                        ahead(2, 4, 8)
                        pe.wait_ge(q_["on_ready"], i + 1)
                        turned(psum[2], lambda n: on[:, n * P:(n + 1) * P]).then_inc(q_["oT_psum"], 1)
                        pe.wait_ge(q_["y_done"], i + 1)

                    for j in range(3):
                        g.features(pe, j, 0, xT)
                    in_turns(pe, GH, body)

                @block.scalar
                def _(act):
                    def tap(j, i):
                        g.wait_ready(act, j, i)
                        nc.scalar.activation(acc[:, j, :], psum[j % 2][:, :], ACT.Copy, scale=cw_g[:, 3, ds(i + 8 * j, 1)]).then_inc(q_["conv_acc"], 1)

                    def tanh(j, i):
                        g.wait_read(act, j, i)
                        nc.scalar.activation(th[:, j, :], acc[:, j, :], ACT.Tanh).then_inc(q_["conv_th"], 1)

                    def body(i, more):
                        for j in range(2):
                            act.wait_ge(q_["tok_psum"], i * 3 + (j + 1))
                            nc.scalar.activation(sq[:, j], v3(psum[2 + j][:, :]), ACT.Square).then_inc(q_["tok_sq"], 1)
                        g.wait_ready(act, 3, i)
                        act.wait_ge(q_["y_done"], i)
                        nc.scalar.activation(acc[:, 3, :], psum[1][:, :], ACT.Copy, scale=0.5).then_inc(q_["z_acc"], 1)
                        nc.scalar.activation(th[:, 3, :], psum[1][:, :], ACT.Tanh, scale=0.5).then_inc(g_free[1], 1)
                        act.wait_ge(q_["dec_psum"], i + 1)
                        nc.scalar.activation(dec[:, :], psum[5][:, :], ACT.Exp).then_inc(q_["dec_ready"], 1)
                        for j, (dst, b) in enumerate(((knT, 6), (kbT, 7), (qnT, 2), (qdT, 3))):
                            act.wait_ge(q_["tokT_psum"], i * 4 + (j + 1))
                            nc.scalar.activation(dst[:, :], psum[b][:, :], ACT.Copy).then_inc(q_["tokT_done"], 1)
                        for l in range(1, LEVELS):
                            act.wait_ge(q_["lev_x_psum"], i * 6 + l)
                            nc.scalar.activation(X[:, :], psum[5][:, :], ACT.Copy).then_inc(q_["lev_x"], 1)
                            if more and l == 1:
                                tap(0, i + 1)
                            if more and l == 5:
                                tanh(0, i + 1)
                        act.wait_ge(q_["wT_psum"], i + 1)
                        nc.scalar.activation(nwT[:, :], psum[4][:, :], ACT.Copy, scale=-1.0).then_inc(q_["wT_ready"], 1)
                        for n in range(NT):
                            c = slice(n * P, (n + 1) * P)
                            act.wait_ge(q_["vn_psum"], i * 4 + (n + 1))
                            nc.scalar.activation(vn[:, c], psum[5][:, c], ACT.Copy).then_inc(q_["vn_ready"], 1)
                            if more and n == 0:
                                tap(1, i + 1)
                            if more and n == 3:
                                tanh(1, i + 1)
                        act.wait_ge(q_["o_psum"], i + 1)
                        nc.scalar.activation(sq[:, 2], v3(psum[7][:, :]), ACT.Square).then_inc(q_["tok_sq"], 1)
                        if more:
                            tap(2, i + 1)
                            tanh(2, i + 1)

                    for j in range(3):
                        tap(j, 0)
                        tanh(j, 0)
                    in_turns(act, GH, body)

                @block.gpsimd
                def _(pool):
                    def body(i, more):
                        nc.gpsimd.tensor_tensor(lla[:, :, :], cst[:, K_L:K_L + P].unsqueeze(1).to_broadcast([P, NT, P]),
                                                la[:, :, ds(i, 1)].to_broadcast([P, NT, P]), ALU.mult).then_inc(q_["lla_ready"], 1)
                        pool.wait_ge(q_["rs_in"], i * 2 + 1)
                        nc.gpsimd.tensor_tensor(rs[:, 0:8], ssq[:, 0:8], half[:, 0:8], ALU.pow).then_inc(q_["rs_out"], 1)
                        pool.wait_ge(q_["score_done"], i * 2 + 1)
                        for l in range(1, LEVELS):
                            nc.gpsimd.tensor_tensor(v3(Cl[:, l - 1, :]), v3(AT[:, :]), cst[:, K_MASK + l * P:K_MASK + (l + 1) * P].unsqueeze(1).to_broadcast([P, NT, P]),
                                                    ALU.mult).then_inc(q_["cl_ready"], 1)
                        pool.wait_ge(q_["rs_in"], i * 2 + 2)
                        nc.gpsimd.tensor_tensor(rs[:, 8:12], ssq[:, 8:12], half[:, 0:4], ALU.pow).then_inc(q_["rs_out"], 1)

                    in_turns(pool, GH, body)

                @block.vector
                def _(dve):
                    def tap(j, i, m):
                        if m == 1:
                            dve.wait_ge(q_["conv_acc"], i * 3 + (j + 1))
                        ins = nc.vector.scalar_tensor_tensor(out=acc[:, j, m:S], in0=psum[j % 2][:, 0:S - m], scalar=cw_g[:, 3 - m, ds(i + 8 * j, 1)],
                                                             in1=acc[:, j, m:S], op0=ALU.mult, op1=ALU.add)
                        if m < 3:
                            ins.then_inc(q_["conv_fm"], 1)
                            dve.wait_ge(q_["conv_fm"], i * 6 + (2 * j + m))
                        else:
                            ins.then_inc(g_free[j % 2], 1)

                    def silu(j, i):
                        if j < 3:
                            dve.wait_ge(q_["conv_th"], i * 3 + (j + 1))
                        else:
                            g.wait_read(dve, 3, i)
                        nc.vector.scalar_tensor_tensor(out=fm[:, j, :], in0=th[:, j, :], scalar=1.0, in1=acc[:, j, :], op0=ALU.add, op1=ALU.mult).then_inc(q_["fm_done"], 1)

                    def body(i, more):
                        link = Count(dve, q_["g_dve"], 3, i)
                        dve.wait_ge(q_["tok_sq"], i * 3 + 2)
                        link(nc.vector.tensor_reduce(ssq[:, 0:8], sq[:, 0:2].rearrange("p a n c -> p (a n) c"), AX.X, ALU.add))
                        link(nc.vector.tensor_scalar(ssq[:, 0:4], ssq[:, 0:4], RMS_EPS, float(P), ALU.add, ALU.mult))
                        nc.vector.tensor_scalar(ssq[:, 4:8], ssq[:, 4:8], RMS_EPS, None, ALU.add).then_inc(q_["rs_in"], 1)
                        dve.wait_ge(q_["tok_psum"], i * 3 + 3)

                        def by(dst, src, scale, w):
                            nc.vector.tensor_tensor(dst[:, :, :], src, scale.to_broadcast([P, NT, P]), ALU.mult).then_inc(q_["tok_norm"], 1)

                        dve.wait_ge(q_["rs_out"], i * 2 + 1)
                        by(kn, v3(psum[3][:, :]), rs[:, 4:8].unsqueeze(2), 1)
                        dve.wait_ge(q_["tok_norm"], i * 7 + 1)
                        by(kb, kn[:, :, :], beta[:, :, ds(i, 1)], 2)
                        by(vb, v3(psum[4][:, :]), beta[:, :, ds(i, 1)], 3)
                        by(qn, v3(psum[2][:, :]), rs[:, 0:4].unsqueeze(2), 4)
                        dve.wait_ge(q_["tok_norm"], i * 7 + 4)
                        by(qd, qn[:, :, :], ecum[:, :, ds(i, 1)], 5)
                        by(kbe, kn[:, :, :], becum[:, :, ds(i, 1)], 6)
                        by(kd, kn[:, :, :], ekw[:, :, ds(i, 1)], 7)
                        silu(3, i)
                        dve.wait_ge(q_["dec_ready"], i + 1)
                        dve.wait_ge(q_["score_psum"], i * 2 + 1)
                        nc.vector.tensor_tensor(AT[:, :], psum[6][:, :], dec[:, :], ALU.mult).then_inc(q_["score_done"], 1)
                        dve.wait_ge(q_["score_done"], i * 2 + 1)
                        nc.vector.tensor_tensor(v3(X[:, :]), v3(AT[:, :]), cst[:, K_MASK:K_MASK + P].unsqueeze(1).to_broadcast([P, NT, P]), ALU.mult).then_inc(q_["x0"], 1)
                        dve.wait_ge(q_["x0"], i + 1)
                        nc.vector.tensor_tensor(v3(TT[:, :]), ident.unsqueeze(1).to_broadcast([P, NT, P]), v3(X[:, :]), ALU.subtract).then_inc(q_["lev_tt"], 1)
                        dve.wait_ge(q_["score_psum"], i * 2 + 2)
                        nc.vector.tensor_tensor(atT[:, :], psum[7][:, :], dec[:, :], ALU.mult).then_inc(q_["score_done"], 1)
                        dve.wait_ge(q_["t0_psum"], i + 1)
                        nc.vector.tensor_copy(T[:, :], psum[4][:, :]).then_inc(q_["lev_t"], 1)
                        for l in range(1, LEVELS):
                            if l < LEVELS - 1:
                                dve.wait_ge(q_["lev_y_psum"], i * 11 + (2 * l - 1))
                                dve.wait_ge(q_["lev_t"], i * 6 + l)
                                nc.vector.tensor_tensor(T[:, :], T[:, :], psum[7][:, :], ALU.subtract).then_inc(q_["lev_t"], 1)
                            dve.wait_ge(q_["lev_y_psum"], i * 11 + min(2 * l, 11))
                            dve.wait_ge(q_["lev_tt"], i * 7 + l)
                            nc.vector.tensor_tensor(TT[:, :], TT[:, :], psum[6][:, :], ALU.subtract).then_inc(q_["lev_tt"], 1)
                            if more and l in (2, 3, 4):
                                tap(0, i + 1, l - 1)
                        if more:
                            silu(0, i + 1)
                        for n in range(NT - 1):
                            c = slice(n * P, (n + 1) * P)
                            dve.wait_ge(q_["kv_psum"], i * 3 + (n + 1))
                            if n == 0:
                                nc.vector.tensor_copy(St[:, 0, :], psum[6][:, c]).then_inc(q_["state"], 1)
                            else:
                                dve.wait_ge(q_["state"], i * 3 + n)
                                nc.vector.scalar_tensor_tensor(out=St[:, n, :], in0=St[:, n - 1, :], scalar=etot[:, n, ds(i, 1)], in1=psum[6][:, c],
                                                               op0=ALU.mult, op1=ALU.add).then_inc(q_["state"], 1)
                            if more:
                                tap(1, i + 1, n + 1)
                        if more:
                            silu(1, i + 1)
                        dve.wait_ge(q_["tok_sq"], i * 3 + 3)
                        link(nc.vector.tensor_reduce(ssq[:, 8:12], sq[:, 2], AX.X, ALU.add))
                        nc.vector.tensor_scalar(ssq[:, 8:12], ssq[:, 8:12], 1.0 / P, RMS_EPS, ALU.mult, ALU.add).then_inc(q_["rs_in"], 1)
                        dve.wait_ge(q_["rs_out"], i * 2 + 2)
                        nc.vector.tensor_tensor(v3(on[:, :]), v3(psum[7][:, :]), rs[:, 8:12].unsqueeze(2).to_broadcast([P, NT, P]), ALU.mult).then_inc(q_["on_ready"], 1)
                        if more:
                            for m in (1, 2, 3):
                                tap(2, i + 1, m)
                            silu(2, i + 1)
                        dve.wait_ge(q_["oT_psum"], i + 1)
                        nc.vector.scalar_tensor_tensor(out=yT[:, 0, ds(i, 1), :].rearrange("p a c -> p (a c)"), in0=psum[2][:, :], scalar=nw_g[:, 0:1], in1=fm[:, 3, :],
                                                       op0=ALU.mult, op1=ALU.mult).then_inc(q_["y_done"], 1)
                        link.done()

                    for j in range(3):
                        for m in (1, 2, 3):
                            tap(j, 0, m)
                        silu(j, 0)
                    in_turns(dve, GH, body)

        end_phase()
        mT = ub_("mT", [P, KT, S])
        with ExitStack() as c2:
            def b2(name, shape, dt=f32):
                return c2.enter_context(nc.sbuf_tensor("m_" + name, shape, dt))

            gt, pr, s01 = b2("gt", [P, 3, S]), b2("pr", [P, 3, S]), b2("s01", [P, S])
            names = "s01_done m_done".split()
            q_ = {n_: sem("m_" + n_) for n_ in names}
            g = mrg_g

            with nc.Block() as block:
                @block.sync
                def _(sp_):
                    in_turns(sp_, KT, lambda i, more: [g.load_next(sp_, j, i) for j in range(6)] if more else None)
                    for j in range(6):
                        g.wait_ready(sp_, j, KT - 1)
                        xa_g.load_first(sp_, j)

                @block.tensor
                def _(pe):
                    with pe.Fori(0, KT) as i:
                        for j in range(6):
                            g.features(pe, j, i, yT[:, j // 2] if j % 2 else xT)

                @block.scalar
                def _(act):
                    with act.Fori(0, KT) as i:
                        for j in range(3):
                            g.wait_ready(act, 2 * j, i)
                            act.wait_ge(q_["m_done"], i)
                            nc.scalar.activation(gt[:, j, :], psum[0][:, :], ACT.Tanh, scale=0.5).then_inc(g_free[0], 1)

                @block.vector
                def _(dve):
                    with dve.Fori(0, KT) as i:
                        for j in range(3):
                            g.wait_ready(dve, 2 * j + 1, i)
                            g.wait_read(dve, 2 * j, i)
                            nc.vector.scalar_tensor_tensor(out=pr[:, j, :], in0=gt[:, j, :], scalar=1.0, in1=psum[1][:, :], op0=ALU.add, op1=ALU.mult).then_inc(g_free[1], 1)
                            if j == 1:
                                g.wait_read(dve, 3, i)
                                nc.vector.tensor_tensor(s01[:, :], pr[:, 0, :], pr[:, 1, :], ALU.add).then_inc(q_["s01_done"], 1)
                        g.wait_read(dve, 5, i)
                        dve.wait_ge(q_["s01_done"], i + 1)
                        nc.vector.tensor_tensor(mT[:, ds(i, 1), :].rearrange("p a c -> p (a c)"), s01[:, :], pr[:, 2, :], ALU.add).then_inc(q_["m_done"], 1)

        def norm_rows(dve, stats, mv, var, rs, n, rs_in, rs_out, nsem, grow, brow, ready, done):
            for h in range(2):
                nc.vector.bn_stats(stats[:, n, h, :], xres[:, n, h * F:(h + 1) * F]).then_inc(nsem, 1)
            dve.wait_ge(nsem, n * 5 + 2)
            nc.vector.bn_aggr(mv[:, n, :], stats[:, n, :, :].rearrange("p h c -> p (h c)")).then_inc(nsem, 1)
            dve.wait_ge(nsem, n * 5 + 3)
            nc.vector.tensor_scalar(var[:, n:n + 1], mv[:, n, 1:2], LN_EPS, None, ALU.add).then_inc(rs_in, 1)
            dve.wait_ge(rs_out, n + 1)
            nc.vector.tensor_scalar(xres[:, n, :], xres[:, n, :], mv[:, n, 0:1], rs[:, n:n + 1], ALU.subtract, ALU.mult).then_inc(nsem, 1)
            dve.wait_ge(nsem, n * 5 + 4)
            nc.vector.tensor_tensor(xres[:, n, :], xres[:, n, :], grow, ALU.mult).then_inc(nsem, 1)
            dve.wait_ge(nsem, n * 5 + 5)
            nc.vector.tensor_tensor(xres[:, n, :], xres[:, n, :], brow, ALU.add).then_inc(done, 1)

        def dense_and_norm(tag, srcT, w, scale, g_dram, b_dram):
            with ExitStack() as c2:
                def b2(name, shape, dt=f32):
                    return c2.enter_context(nc.sbuf_tensor(f"{tag}_{name}", shape, dt))

                rows = b2("rows", [P, 2, D])
                wide = [b2(f"w{h}", [P, KT, F]) for h in range(2)]
                stats, mv, var, rs = b2("stats", [P, NT, 2, 6]), b2("mv", [P, NT, 2]), b2("var", [P, NT]), b2("rs", [P, NT])
                w_in_, rows_in = sem(tag + "_w_in"), sem(tag + "_rows_in")
                ax, prod, z_done, nsem = sem(tag + "_alpha_x"), sem(tag + "_prod"), sem(tag + "_z_done"), sem(tag + "_norm")
                rs_in, rs_out, x_done, t_psum, t_done = [sem(f"{tag}_{n_}") for n_ in ("rs_in", "rs_out", "x_done", "t_psum", "t_done")]
                with nc.Block() as block:
                    @block.sync
                    def _(sp_):
                        for h in range(2):
                            sp_.dma_start(wide[h][:, :, :], w_cols(w, h * F, F)).then_inc(w_in_, 16)
                        sp_.dma_start(rows[:, 0, :], g_dram).then_inc(rows_in, 16)
                        sp_.dma_start(rows[:, 1, :], b_dram).then_inc(rows_in, 16)

                    @block.tensor
                    def _(pe):
                        pe.wait_ge(w_in_, 32)
                        for n in range(NT):
                            for h in range(2):
                                u = 2 * n + h
                                if u >= 4:
                                    pe.wait_ge(z_done, u - 3)
                                for k in range(KT):
                                    ins = nc.tensor.matmul(psum[u % 4][:, :], srcT[:, k, n * P:(n + 1) * P], wide[h][:, k, :], start=(k == 0), stop=(k == KT - 1))
                                ins.then_inc(prod, 1)
                        for n in range(NT):
                            pe.wait_ge(x_done, n + 1)
                            for a in range(2):
                                u = 2 * n + a
                                if u >= 4:
                                    pe.wait_ge(t_done, u - 3)
                                for k in range(4):
                                    ins = nc.tensor.transpose(psum[4 + u % 4][:, k * P:(k + 1) * P], xres[:, n, (4 * a + k) * P:(4 * a + k + 1) * P], ident)
                                ins.then_inc(t_psum, 1)

                    @block.scalar
                    def _(act):
                        for n in range(NT):
                            nc.scalar.activation(xres[:, n, :], xres[:, n, :], ACT.Copy, scale=ALPHA).then_inc(ax, 1)
                        for u in range(2 * NT):
                            n, a = u // 2, u % 2
                            act.wait_ge(t_psum, u + 1)
                            nc.scalar.activation(xT[:, 4 * a:4 * a + 4, n * P:(n + 1) * P], v3(psum[4 + u % 4][:, :]), ACT.Copy).then_inc(t_done, 1)

                    @block.gpsimd
                    def _(pool):
                        for n in range(NT):
                            pool.wait_ge(rs_in, n + 1)
                            nc.gpsimd.tensor_tensor(rs[:, n:n + 1], var[:, n:n + 1], half[:, 0:1], ALU.pow).then_inc(rs_out, 1)

                    @block.vector
                    def _(dve):
                        dve.wait_ge(rows_in, 32)
                        for n in range(NT):
                            dve.wait_ge(ax, n + 1)
                            for h in range(2):
                                u = 2 * n + h
                                dve.wait_ge(prod, u + 1)
                                c = slice(h * F, (h + 1) * F)
                                nc.vector.scalar_tensor_tensor(out=xres[:, n, c], in0=psum[u % 4][:, :], scalar=scale, in1=xres[:, n, c], op0=ALU.mult, op1=ALU.add).then_inc(z_done, 1)
                            dve.wait_ge(z_done, 2 * n + 2)
                            norm_rows(dve, stats, mv, var, rs, n, rs_in, rs_out, nsem, rows[:, 0, :], rows[:, 1, :], None, x_done)

        end_phase()
        dense_and_norm("mix", mT, t["mix_w_out"][0], 0.5, t["ln_mix_g"], t["ln_mix_b"])

        end_phase()
        with ExitStack() as c2:
            def b2(name, shape, dt=f32):
                return c2.enter_context(nc.sbuf_tensor("x_" + name, shape, dt))

            mem_tok, memT = b2("mem_tok", [P, 2, D]), b2("memT", [P, KT, MEM])
            qT, kT, v = b2("qT", [P, 2, S]), b2("kT", [P, 2, MEM]), b2("v", [P, 2, 2, P])
            mx, nb, sm_, ri = b2("mx", [P, NT]), b2("nb", [P, NT]), b2("sm", [P, NT]), b2("ri", [P, NT])
            pe_, pn = b2("pexp", [P, NT, MEM]), b2("pn", [P, NT, MEM])
            pT = b2("pT", [P, 2, S])
            names = ("mem_in mem_psum mem_done q_done k_done v_done s_psum mx_done nb_done e_done ri_done pn_done pT_psum pT_done o_psum o_done").split()
            q_ = {n_: sem("x_" + n_) for n_ in names}
            g = xa_g
            SC = (D // XH) ** -0.5

            with nc.Block() as block:
                @block.sync
                def _(sp_):
                    for m in range(2):
                        sp_.dma_start(mem_tok[:, m, :], t["mem"][0, m * P:(m + 1) * P, :]).then_inc(q_["mem_in"], 16)
                    in_turns(sp_, XH, lambda i, more: [g.load_next(sp_, j, i) for j in range(6)] if more else None)

                @block.tensor
                def _(pe):
                    pe.wait_ge(q_["mem_in"], 32)
                    for k2 in range(4):
                        for kk in range(2):
                            for m in range(2):
                                ins = nc.tensor.transpose(psum[2 + k2][:, (2 * kk + m) * P:(2 * kk + m + 1) * P], mem_tok[:, m, (2 * k2 + kk) * P:(2 * k2 + kk + 1) * P], ident)
                        ins.then_inc(q_["mem_psum"], 1)
                    pe.wait_ge(q_["mem_done"], 4)
                    def product(j, i):
                        if j < 4:
                            g.features(pe, j, i, (xT, memT)[j // 2], cols=(S, MEM)[j // 2])
                        else:
                            g.tokens(pe, j, i, memT, 0, 2, last=2)

                    def body(i, more):
                        pe.wait_ge(q_["q_done"], i * 2 + 2)
                        pe.wait_ge(q_["k_done"], i * 2 + 2)
                        for n in range(NT):
                            for c in range(2):
                                ins = nc.tensor.matmul(psum[2 + n // 2][:, (n % 2) * MEM:(n % 2 + 1) * MEM], qT[:, c, n * P:(n + 1) * P], kT[:, c, :], start=(c == 0), stop=(c == 1))
                        ins.then_inc(q_["s_psum"], 1)
                        product(4, i)
                        product(5, i)
                        if more:
                            product(0, i + 1)
                        pe.wait_ge(q_["pn_done"], i + 1)
                        for m in range(2):
                            for n in range(NT):
                                ins = nc.tensor.transpose(psum[4 + m][:, n * P:(n + 1) * P], pn[:, n, m * P:(m + 1) * P], ident)
                            ins.then_inc(q_["pT_psum"], 1)
                        if more:
                            product(1, i + 1)
                        pe.wait_ge(q_["pT_done"], i * 2 + 2)
                        pe.wait_ge(q_["v_done"], i * 2 + 2)
                        pe.wait_ge(q_["o_done"], i * 2)
                        for c in range(2):
                            for m in range(2):
                                ins = nc.tensor.matmul(psum[6 + c][:, :], v[:, m, c, :], pT[:, m, :], start=(m == 0), stop=(m == 1))
                            ins.then_inc(q_["o_psum"], 1)
                        if more:
                            product(2, i + 1)
                            product(3, i + 1)

                    for j in range(4):
                        product(j, 0)
                    in_turns(pe, XH, body)

                @block.scalar
                def _(act):
                    for k2 in range(4):
                        act.wait_ge(q_["mem_psum"], k2 + 1)
                        nc.scalar.activation(memT[:, 2 * k2:2 * k2 + 2, :].rearrange("p k m -> p (k m)"), psum[2 + k2][:, :], ACT.Copy).then_inc(q_["mem_done"], 1)
                    def take(j, i):
                        b = j % 2
                        key = ("q_done", "k_done", "v_done")[j // 2]
                        dst, src = ((qT[:, b, :], psum[b][:, :]), (kT[:, b, :], psum[b][:, 0:MEM]),
                                    (v[:, :, b, :], psum[b][:, 0:MEM].rearrange("p (m c) -> p m c", m=2)))[j // 2]
                        g.wait_ready(act, j, i)
                        nc.scalar.activation(dst, src, ACT.Copy).then_inc(g_free[b], 1)
                        g.wait_read(act, j, i)
                        act.sem_inc(q_[key], 1)

                    def body(i, more):
                        act.wait_ge(q_["nb_done"], i + 1)
                        for n in range(NT):
                            nc.scalar.activation(pe_[:, n, :], psum[2 + n // 2][:, (n % 2) * MEM:(n % 2 + 1) * MEM], ACT.Exp, bias=nb[:, n:n + 1], scale=SC,
                                                 accum_out=sm_[:, n:n + 1]).then_inc(q_["e_done"], 1)
                        take(4, i)
                        take(5, i)
                        if more:
                            take(0, i + 1)
                        for m in range(2):
                            act.wait_ge(q_["pT_psum"], i * 2 + (m + 1))
                            nc.scalar.activation(pT[:, m, :], psum[4 + m][:, :], ACT.Copy).then_inc(q_["pT_done"], 1)
                        if more:
                            take(1, i + 1)
                        for c in range(2):
                            act.wait_ge(q_["o_psum"], i * 2 + (c + 1))
                            nc.scalar.activation(mT[:, ds(i * 2 + c, 1), :].rearrange("p a c -> p (a c)"), psum[6 + c][:, :], ACT.Copy).then_inc(q_["o_done"], 1)
                        if more:
                            take(2, i + 1)
                            take(3, i + 1)

                    for j in range(4):
                        take(j, 0)
                    in_turns(act, XH, body)

                @block.vector
                def _(dve):
                    with dve.Fori(0, XH) as i:
                        dve.wait_ge(q_["s_psum"], i + 1)
                        for b in range(2):
                            nc.vector.tensor_reduce(mx[:, 2 * b:2 * b + 2], psum[2 + b][:, :].rearrange("p (n c) -> p n c", n=2), AX.X, ALU.max).then_inc(q_["mx_done"], 1)
                        dve.wait_ge(q_["mx_done"], i * 2 + 2)
                        nc.vector.tensor_scalar(nb[:, :], mx[:, :], -SC, None, ALU.mult).then_inc(q_["nb_done"], 1)
                        dve.wait_ge(q_["e_done"], i * 4 + 4)
                        nc.vector.reciprocal(ri[:, :], sm_[:, :]).then_inc(q_["ri_done"], 1)
                        dve.wait_ge(q_["ri_done"], i + 1)
                        nc.vector.tensor_tensor(pn[:, :, :], pe_[:, :, :], ri[:, :].unsqueeze(2).to_broadcast([P, NT, MEM]), ALU.mult).then_inc(q_["pn_done"], 1)
        end_phase()
        dense_and_norm("xa", mT, t["xa_w_o"][0], 1.0, t["ln_xa_g"], t["ln_xa_b"])
        end_phase()
        BIG = 1e9
        with ExitStack() as c2:
            def b2(name, shape, dt=f32):
                return c2.enter_context(nc.sbuf_tensor("q_" + name, shape, dt))

            rw, rb = b2("rw", [P, KT, NE]), b2("rb", [P, NE])
            R = b2("R", [P, 24, NT, NE])
            G = b2("G", [P, 12, NT, 4])
            one = b2("one", [P, 10, NT])
            E16 = b2("E16", [P, 8, NE])
            ge, ohh = b2("ge", [P, 2, NT, NB + 1]), b2("ohh", [P, 2, NT, NB])
            ohl = b2("ohl", [P, 2, NT, P])
            lo = b2("lo", [P, 2, NT])
            thr = b2("thr", [P, NB + 1])
            eo = b2("eo", [P, 8, NE])
            tab = b2("tab", [P, 8])
            zero, zero_set = b2("zero", [P, D]), sem("q_zero_set")
            r_in, lg_psum, e_done, oh_done, rk_psum, list_in, list_psum, chain, x2_st = [sem("q_" + n_) for n_ in
                ("in", "logit_psum", "e_done", "oh_done", "rank_psum", "list_in", "list_psum", "chain", "x2_stored")]
            with nc.Block() as block:
                @block.sync
                def _(sp_):
                    sp_.dma_start(rw[:, :, :], t["router_w"].rearrange("(k p) e -> p k e", p=P)).then_inc(r_in, 16)
                    sp_.dma_start(rb[:, :], t["router_rows"]).then_inc(r_in, 16)
                    for n in range(NT):
                        sp_.dma_start(x2_dram[n * P:(n + 1) * P, :], xres[:, n, :]).then_inc(x2_st, 16)
                    sp_.wait_ge(zero_set, 1)
                    for j in range(NOV):
                        sp_.dma_start(y_dram[(NE + j) * P:(NE + j + 1) * P, :], zero[:, :]).then_inc(x2_st, 16)
                    sp_.wait_ge(x2_st, 16 * (NT + NOV))

                @block.gpsimd
                def _(pool):
                    nc.gpsimd.memset(zero[:, :], 0.0).then_inc(zero_set, 1)

                @block.tensor
                def _(pe):
                    pe.wait_ge(r_in, 32)
                    for n in range(NT):
                        for k in range(KT):
                            ins = nc.tensor.matmul(psum[0][:, n * NE:(n + 1) * NE], xT[:, k, n * P:(n + 1) * P], rw[:, k, :], start=(k == 0), stop=(k == KT - 1))
                    ins.then_inc(lg_psum, 1)
                    pe.wait_ge(oh_done, 1)
                    for n in range(NT):
                        for m in range(n + 1):
                            ins = nc.tensor.matmul(psum[1][:, n * NE:(n + 1) * NE], cst[:, K_U:K_U + P] if m == n else cst[:, K_ONE:K_ONE + P], R[:, 12, m, :], start=(m == 0), stop=(m == n))
                    for m in range(NT):
                        ins = nc.tensor.matmul(psum[1][:, NT * NE:(NT + 1) * NE], cst[:, K_ONE:K_ONE + P], R[:, 12, m, :], start=(m == 0), stop=(m == NT - 1))
                    ins.then_inc(rk_psum, 1)
                    pe.wait_ge(list_in, 1)
                    for c in range(2):
                        for n in range(NT):
                            ins = nc.tensor.matmul(psum[2][:, 0:NB], ohl[:, c, n, :], ohh[:, c, n, :], start=(c + n == 0), stop=(c == 1 and n == NT - 1))
                    ins.then_inc(list_psum, 1)

                @block.scalar
                def _(act):
                    act.wait_ge(lg_psum, 1)
                    nc.scalar.activation(R[:, 0], psum[0][:, 0:NT * NE].rearrange("p (n e) -> p n e", n=NT), ACT.Exp, scale=-1.0).then_inc(e_done, 1)

                iota = cst[:, K_SLOT:K_SLOT + NE].unsqueeze(1).to_broadcast([P, NT, NE])
                iota4 = cst[:, K_SLOT:K_SLOT + 4].unsqueeze(1).to_broadcast([P, NT, 4])

                @block.vector
                def _(dve):
                    link = Count(dve, chain, 0)
                    V = nc.vector

                    def first_max(vals, io, mxv, eq, cand, idx, oh, n_):
                        link(V.tensor_reduce(mxv, vals, AX.X, ALU.max))
                        link(V.tensor_tensor(eq, vals, mxv.unsqueeze(2).to_broadcast([P, NT, n_]), ALU.is_equal))
                        link(V.scalar_tensor_tensor(out=cand, in0=eq, scalar=-64.0, in1=io, op0=ALU.mult, op1=ALU.add))
                        link(V.tensor_reduce(idx, cand, AX.X, ALU.min))
                        link(V.tensor_scalar(idx, idx, 64.0, None, ALU.add))
                        link(V.tensor_tensor(oh, io, idx.unsqueeze(2).to_broadcast([P, NT, n_]), ALU.is_equal))

                    dve.wait_ge(e_done, 1)
                    link(V.tensor_scalar(R[:, 1], R[:, 0], 1.0, None, ALU.add))
                    link(V.reciprocal(R[:, 2], R[:, 1]))
                    link(V.tensor_tensor(R[:, 3], R[:, 2], rb[:, :].unsqueeze(1).to_broadcast([P, NT, NE]), ALU.add))
                    s4 = R[:, 3].rearrange("p n (g e) -> p n g e", g=4)
                    a_, b_, c_, d_ = [s4[:, :, :, j] for j in range(4)]
                    link(V.tensor_tensor(G[:, 0], a_, b_, ALU.max))
                    link(V.tensor_tensor(G[:, 1], a_, b_, ALU.min))
                    link(V.tensor_tensor(G[:, 2], c_, d_, ALU.max))
                    link(V.tensor_tensor(G[:, 3], c_, d_, ALU.min))
                    link(V.tensor_tensor(G[:, 4], G[:, 0], G[:, 2], ALU.max))
                    link(V.tensor_tensor(G[:, 5], G[:, 0], G[:, 2], ALU.min))
                    link(V.tensor_tensor(G[:, 6], G[:, 1], G[:, 3], ALU.max))
                    link(V.tensor_tensor(G[:, 5], G[:, 5], G[:, 6], ALU.max))
                    link(V.tensor_tensor(G[:, 7], G[:, 4], G[:, 5], ALU.add))
                    first_max(G[:, 7], iota4, one[:, 0], G[:, 8], G[:, 9], one[:, 1], G[:, 10], 4)
                    link(V.tensor_scalar(G[:, 11], G[:, 10], -1.0, BIG, ALU.add, ALU.mult))
                    link(V.tensor_tensor(R[:, 4].rearrange("p n (g e) -> p n g e", g=4), s4, G[:, 11].unsqueeze(3).to_broadcast([P, NT, 4, 4]), ALU.add))
                    first_max(R[:, 4], iota, one[:, 0], R[:, 5], R[:, 6], one[:, 1], R[:, 7], NE)
                    link(V.scalar_tensor_tensor(out=R[:, 8], in0=R[:, 7], scalar=-4 * BIG, in1=R[:, 4], op0=ALU.mult, op1=ALU.add))
                    first_max(R[:, 8], iota, one[:, 0], R[:, 5], R[:, 6], one[:, 1], R[:, 11], NE)
                    link(V.tensor_tensor(R[:, 12], R[:, 7], R[:, 11], ALU.add))
                    dve.sem_inc(oh_done, 1)
                    for c, oh in enumerate((7, 11)):
                        link(V.tensor_tensor(R[:, 13], R[:, 2], R[:, oh], ALU.mult))
                        link(V.tensor_reduce(one[:, 2 + c], R[:, 13], AX.X, ALU.add))
                    link(V.tensor_tensor(one[:, 4], one[:, 2], one[:, 3], ALU.add))
                    link(V.reciprocal(one[:, 5], one[:, 4]))
                    for c in range(2):
                        link(V.tensor_tensor(r_g[:, c, :], one[:, 2 + c], one[:, 5], ALU.mult))
                    dve.wait_ge(rk_psum, 1)
                    cnt = psum[1][:, NT * NE:(NT + 1) * NE]
                    link(V.tensor_scalar(E16[:, 0], cnt, float(P), None, ALU.is_gt))
                    link(V.tensor_scalar(E16[:, 1], cnt, 2.0 * P, None, ALU.is_gt))
                    link(V.tensor_scalar(E16[:, 2], cnt, 3.0 * P, None, ALU.is_gt))
                    link(V.tensor_tensor(E16[:, 0], E16[:, 0], E16[:, 1], ALU.add))
                    link(V.tensor_tensor(E16[:, 0], E16[:, 0], E16[:, 2], ALU.add))
                    link(V.tensor_copy(E16[:, 3], E16[:, 0]))
                    src, dst = 3, 4
                    for sh in (1, 2, 4, 8):
                        link(V.tensor_copy(E16[:, dst, 0:sh], E16[:, src, 0:sh]))
                        link(V.tensor_tensor(E16[:, dst, sh:NE], E16[:, src, sh:NE], E16[:, src, 0:NE - sh], ALU.add))
                        src, dst = dst, src
                    inc = E16[:, src]
                    link(V.tensor_tensor(E16[:, 5], inc, E16[:, 0], ALU.subtract))
                    link(V.tensor_tensor(R[:, 14], psum[1][:, 0:NT * NE].rearrange("p (n e) -> p n e", n=NT), R[:, 12], ALU.subtract))
                    link(V.tensor_scalar(R[:, 15], R[:, 14], float(P), None, ALU.is_ge))
                    link(V.tensor_scalar(E16[:, 6], cst[:, K_SLOT:K_SLOT + NE], float(P), None, ALU.mult))
                    link(V.tensor_scalar(E16[:, 7], E16[:, 5], float(P), float((NE - 1) * P), ALU.mult, ALU.add))
                    link(V.tensor_tensor(E16[:, 7], E16[:, 7], E16[:, 6], ALU.subtract))
                    link(V.tensor_tensor(R[:, 16], R[:, 15], E16[:, 7].unsqueeze(1).to_broadcast([P, NT, NE]), ALU.mult))
                    link(V.tensor_tensor(R[:, 16], R[:, 16], E16[:, 6].unsqueeze(1).to_broadcast([P, NT, NE]), ALU.add))
                    link(V.tensor_tensor(R[:, 16], R[:, 16], R[:, 14], ALU.add))
                    link(V.tensor_scalar(thr[:, :], cst[:, K_SLOT:K_SLOT + NB + 1], float(P), None, ALU.mult))
                    for c, oh in enumerate((7, 11)):
                        link(V.tensor_tensor(R[:, 13], R[:, 16], R[:, oh], ALU.mult))
                        link(V.tensor_reduce(one[:, 6 + c], R[:, 13], AX.X, ALU.add))
                        link(V.tensor_copy(r_slot[:, c, :], one[:, 6 + c]))
                        link(V.tensor_tensor(ge[:, c], one[:, 6 + c].unsqueeze(2).to_broadcast([P, NT, NB + 1]), thr[:, :].unsqueeze(1).to_broadcast([P, NT, NB + 1]), ALU.is_ge))
                        link(V.tensor_tensor(ohh[:, c], ge[:, c, :, 0:NB], ge[:, c, :, 1:NB + 1], ALU.subtract))
                        link(V.tensor_reduce(lo[:, c], ge[:, c, :, 1:NB + 1], AX.X, ALU.add))
                        link(V.scalar_tensor_tensor(out=lo[:, c], in0=lo[:, c], scalar=-float(P), in1=one[:, 6 + c], op0=ALU.mult, op1=ALU.add))
                        link(V.tensor_tensor(ohl[:, c], lo[:, c].unsqueeze(2).to_broadcast([P, NT, P]), cst[:, K_SLOT:K_SLOT + P].unsqueeze(1).to_broadcast([P, NT, P]), ALU.is_equal))
                        link(V.tensor_tensor(ohh[:, c], ohh[:, c], cst[:, K_TOK:K_TOK + NT].unsqueeze(2).to_broadcast([P, NT, NB]), ALU.mult))
                    dve.sem_inc(list_in, 1)
                    link(V.tensor_tensor(eo[:, :, :], inc.unsqueeze(1).to_broadcast([P, 8, NE]), cst[:, K_SLOT:K_SLOT + 8].unsqueeze(2).to_broadcast([P, 8, NE]), ALU.is_le))
                    link(V.tensor_reduce(tab[:, :], eo[:, :, :], AX.X, ALU.add))
                    link(V.tensor_copy(tab[:, 7:8], inc[:, NE - 1:NE]))
                    link(V.tensor_copy(r_tab[0:1, :], tab[0:1, :]))
                    dve.wait_ge(list_psum, 1)
                    link(V.tensor_copy(r_idx[:, :], psum[2][:, 0:NB]))

        end_phase()
        upper.close()
        with ExitStack() as c2:
            def b2(name, shape, dt=f32):
                return c2.enter_context(nc.sbuf_tensor("e_" + name, shape, dt))

            wg, wu, wd = b2("wg", [P, 2, KT, F]), b2("wu", [P, 2, KT, F]), b2("wd", [P, 2, 4, D])
            idx = b2("idx", [P, 2], i32)
            xg, xgT = b2("xg", [P, 2, D]), b2("xgT", [P, 2, KT, P])
            gt, sg, hid = b2("gt", [P, F]), b2("sg", [P, F]), b2("hid", [P, F])
            hT, ye = b2("hT", [P, 4, P]), b2("ye", [P, 2, D])
            w_sets = [t["moe_w_gate"][0], t["moe_w_up"][0], t["moe_w_down"][0]]

            def expert_sems(tag):
                return {n_: sem(f"{tag}_{n_}") for n_ in
                        "turn w_in0 w_in1 idx xg_in xT_psum xT_done up_psum gt sg hid hT_psum hT_done y_psum ye stored".split()}

            main, over = expert_sems("e"), expert_sems("o")

            def load_expert(sp_, e, u, s, part):
                w = (wg, wu, wd)[part]
                src = w_sets[part][ds(e, 1)].rearrange("a (k p) f -> p (a k) f", p=P)
                sp_.dma_start(w[:, u], src).then_inc(s[f"w_in{u}"], 16)

            def pe_block(pe, s, m, q, u):
                pe.wait_ge(s["xg_in"], (m + 1) * 16)
                for a in range(2):
                    for k in range(4):
                        ins = nc.tensor.transpose(psum[a][:, k * P:(k + 1) * P], xg[:, u, (4 * a + k) * P:(4 * a + k + 1) * P], ident)
                    ins.then_inc(s["xT_psum"], 1)
                pe.wait_ge(s[f"w_in{u}"], (q + 1) * 48)
                pe.wait_ge(s["xT_done"], m * 2 + 2)
                for w, b in ((wg, 2), (wu, 3)):
                    for k in range(KT):
                        ins = nc.tensor.matmul(psum[b][:, :], xgT[:, u, k, :], w[:, u, k, :], start=(k == 0), stop=(k == KT - 1))
                    ins.then_inc(s["up_psum"], 1)
                pe.wait_ge(s["hid"], m + 1)
                for f in range(4):
                    ins = nc.tensor.transpose(psum[4][:, f * P:(f + 1) * P], hid[:, f * P:(f + 1) * P], ident)
                ins.then_inc(s["hT_psum"], 1)
                pe.wait_ge(s["hT_done"], m + 1)
                for h in range(2):
                    for f in range(4):
                        ins = nc.tensor.matmul(psum[6 + h][:, :], hT[:, f, :], wd[:, u, f, h * F:(h + 1) * F], start=(f == 0), stop=(f == 3))
                    ins.then_inc(s["y_psum"], 1)
                pe.wait_ge(s["ye"], m * 2 + 2)

            def act_block(act, s, m, u):
                for a in range(2):
                    act.wait_ge(s["xT_psum"], m * 2 + (a + 1))
                    nc.scalar.activation(xgT[:, u, 4 * a:4 * a + 4, :], v3(psum[a][:, :]), ACT.Copy).then_inc(s["xT_done"], 1)
                act.wait_ge(s["up_psum"], m * 2 + 1)
                nc.scalar.activation(gt[:, :], psum[2][:, :], ACT.Tanh, scale=0.5).then_inc(s["gt"], 1)
                act.wait_ge(s["hT_psum"], m + 1)
                nc.scalar.activation(hT[:, :, :], v3(psum[4][:, :]), ACT.Copy).then_inc(s["hT_done"], 1)

            def dve_block(dve, s, m, u):
                dve.wait_ge(s["gt"], m + 1)
                nc.vector.scalar_tensor_tensor(out=sg[:, :], in0=gt[:, :], scalar=1.0, in1=psum[2][:, :], op0=ALU.add, op1=ALU.mult).then_inc(s["sg"], 1)
                dve.wait_ge(s["sg"], m + 1)
                dve.wait_ge(s["up_psum"], m * 2 + 2)
                nc.vector.scalar_tensor_tensor(out=hid[:, :], in0=sg[:, :], scalar=0.5, in1=psum[3][:, :], op0=ALU.mult, op1=ALU.mult).then_inc(s["hid"], 1)
                for h in range(2):
                    dve.wait_ge(s["y_psum"], m * 2 + (h + 1))
                    nc.vector.tensor_copy(ye[:, u, h * F:(h + 1) * F], psum[6 + h][:, :]).then_inc(s["ye"], 1)

            with nc.Block() as block:
                @block.sync
                def _(sp_):
                    for u in range(2):
                        for part in range(3):
                            load_expert(sp_, u, u, main, part)
                    def store(i, u):
                        sp_.wait_ge(main["ye"], i * 4 + (2 * u + 2))
                        sp_.sem_inc(main["turn"], 1)
                        sp_.dma_start(y_dram[ds(i * 256 + u * P, P), :], ye[:, u, :]).then_inc(main["stored"], 16)

                    with sp_.Fori(0, NE // 2 - 1) as i:
                        for u in range(2):
                            store(i, u)
                            for part in range(3):
                                load_expert(sp_, i * 2 + (u + 2), u, main, part)
                    for u in range(2):
                        store(NE // 2 - 1, u)
                    sp_.wait_ge(main["stored"], 16 * NE)
                    nov = sp_.value_load(r_tab[0:1, 7:8], min_val=0, max_val=NOV)
                    with sp_.Fori(0, NOV) as j:
                        with sp_.If(nov > j):
                            e = sp_.value_load(r_tab[0:1, ds(j, 1)], min_val=0, max_val=NE - 1)
                            for part in range(3):
                                load_expert(sp_, e, 0, over, part)
                            sp_.wait_ge(over["ye"], j * 2 + 2)
                            sp_.sem_inc(over["turn"], 1)
                            sp_.dma_start(y_dram[ds(j * P + NE * P, P), :], ye[:, 0, :]).then_inc(over["stored"], 16)
                            sp_.wait_ge(over["stored"], (j + 1) * 16)
                            sp_.sem_inc(over["turn"], 1)

                @block.gpsimd
                def _(pool):
                    with pool.Fori(0, NE // 2) as i:
                        for u in range(2):
                            pool.wait_ge(main["idx"], i * 2 + (u + 1))
                            pool.sem_inc(main["turn"], 1)
                            nc.gpsimd.indirect_dma_start(xg[:, u, :], None, x2_dram, bass.IndirectOffsetOnAxis(ap=idx[:, u:u + 1], axis=0)).then_inc(main["xg_in"], 16)
                            pool.wait_ge(main["xg_in"], (i * 2 + (u + 1)) * 16)
                            pool.sem_inc(main["turn"], 1)
                    nov = pool.value_load(r_tab[0:1, 7:8], min_val=0, max_val=NOV)
                    with pool.Fori(0, NOV) as j:
                        with pool.If(nov > j):
                            pool.wait_ge(over["idx"], j + 1)
                            pool.sem_inc(over["turn"], 1)
                            nc.gpsimd.indirect_dma_start(xg[:, 0, :], None, x2_dram, bass.IndirectOffsetOnAxis(ap=idx[:, 0:1], axis=0)).then_inc(over["xg_in"], 16)
                            pool.wait_ge(over["xg_in"], (j + 1) * 16)
                            pool.sem_inc(over["turn"], 1)

                @block.tensor
                def _(pe):
                    with pe.Fori(0, NE // 2) as i:
                        for u in range(2):
                            pe_block(pe, main, i * 2 + u, i, u)
                    nov = pe.value_load(r_tab[0:1, 7:8], min_val=0, max_val=NOV)
                    with pe.Fori(0, NOV) as j:
                        with pe.If(nov > j):
                            pe_block(pe, over, j, j, 0)

                @block.scalar
                def _(act):
                    with act.Fori(0, NE // 2) as i:
                        for u in range(2):
                            act_block(act, main, i * 2 + u, u)
                    nov = act.value_load(r_tab[0:1, 7:8], min_val=0, max_val=NOV)
                    with act.Fori(0, NOV) as j:
                        with act.If(nov > j):
                            act_block(act, over, j, 0)

                @block.vector
                def _(dve):
                    for u in range(2):
                        nc.vector.tensor_copy(idx[:, u:u + 1], r_idx[:, u:u + 1]).then_inc(main["idx"], 1)
                    with dve.Fori(0, NE // 2) as i:
                        for u in range(2):
                            if u == 0:
                                dve.wait_ge(main["stored"], i * 32)
                            dve_block(dve, main, i * 2 + u, u)
                            dve.wait_ge(main["xg_in"], (i * 2 + (u + 1)) * 16)
                            nc.vector.tensor_copy(idx[:, u:u + 1], r_idx[:, ds(i * 2 + (u + 2), 1)]).then_inc(main["idx"], 1)
                    nov = dve.value_load(r_tab[0:1, 7:8], min_val=0, max_val=NOV)
                    dve.wait_ge(main["stored"], 16 * NE)
                    dve.wait_ge(main["xg_in"], 16 * NE)
                    with dve.Fori(0, NOV) as j:
                        with dve.If(nov > j):
                            nc.vector.tensor_copy(idx[:, 0:1], r_idx[:, ds(j + NE, 1)]).then_inc(over["idx"], 1)
                            dve_block(dve, over, j, 0)
                            dve.wait_ge(over["stored"], (j + 1) * 16)
                            dve.sem_inc(over["turn"], 1)

        end_phase()
        with ExitStack() as c2:
            def b2(name, shape, dt=f32):
                return c2.enter_context(nc.sbuf_tensor("c_" + name, shape, dt))

            rows = b2("rows", [P, 2, D])
            stats, mv, var, rs = b2("stats", [P, NT, 2, 6]), b2("mv", [P, NT, 2]), b2("var", [P, NT]), b2("rs", [P, NT])
            yg = b2("yg", [P, NT, 2, D])
            rows_in, ax, nsem, rs_in, rs_out, x_done, z1, out_st = [sem("c_" + n_) for n_ in ("rows_in", "alpha_x", "norm", "rs_in", "rs_out", "x_done", "z", "out_stored")]
            y_in = [sem(f"c_y_in{n}") for n in range(NT)]
            sidx = b2("sidx", [P, 2 * NT], i32)
            with nc.Block() as block:
                @block.sync
                def _(sp_):
                    sp_.dma_start(rows[:, 0, :], t["ln_moe_g"]).then_inc(rows_in, 16)
                    sp_.dma_start(rows[:, 1, :], t["ln_moe_b"]).then_inc(rows_in, 16)
                    for n in range(NT):
                        sp_.wait_ge(x_done, n + 1)
                        sp_.dma_start(out[0, n * P:(n + 1) * P, :], xres[:, n, :]).then_inc(out_st, 16)
                    sp_.wait_ge(out_st, 16 * NT)

                @block.gpsimd
                def _(pool):
                    for n in range(NT):
                        for c in range(2):
                            nc.gpsimd.indirect_dma_start(yg[:, n, c, :], None, y_dram, bass.IndirectOffsetOnAxis(ap=r_slot[:, c, n:n + 1], axis=0)).then_inc(y_in[n], 16)
                    for n in range(NT):
                        pool.wait_ge(rs_in, n + 1)
                        nc.gpsimd.tensor_tensor(rs[:, n:n + 1], var[:, n:n + 1], half[:, 0:1], ALU.pow).then_inc(rs_out, 1)

                @block.scalar
                def _(act):
                    for n in range(NT):
                        nc.scalar.activation(xres[:, n, :], xres[:, n, :], ACT.Copy, scale=ALPHA).then_inc(ax, 1)

                @block.vector
                def _(dve):
                    dve.wait_ge(rows_in, 32)
                    for n in range(NT):
                        dve.wait_ge(y_in[n], 32)
                        nc.vector.tensor_scalar(yg[:, n, 0, :], yg[:, n, 0, :], r_g[:, 0, n:n + 1], None, ALU.mult).then_inc(z1, 1)
                        dve.wait_ge(z1, 3 * n + 1)
                        nc.vector.scalar_tensor_tensor(out=yg[:, n, 1, :], in0=yg[:, n, 1, :], scalar=r_g[:, 1, n:n + 1], in1=yg[:, n, 0, :], op0=ALU.mult, op1=ALU.add).then_inc(z1, 1)
                        dve.wait_ge(z1, 3 * n + 2)
                        dve.wait_ge(ax, n + 1)
                        nc.vector.tensor_tensor(xres[:, n, :], xres[:, n, :], yg[:, n, 1, :], ALU.add).then_inc(z1, 1)
                        dve.wait_ge(z1, 3 * n + 3)
                        norm_rows(dve, stats, mv, var, rs, n, rs_in, rs_out, nsem, rows[:, 0, :], rows[:, 1, :], None, x_done)


def kernel(**inputs):
    import numpy as _np
    import concourse.bacc as _bacc
    from concourse import mybir as _mybir
    from concourse.bass_utils import run_bass_kernel_spmd as _run

    nc = _bacc.Bacc("TRN2", target_bir_lowering=False, num_devices=1)
    a = {k: _np.asarray(v) for k, v in inputs.items()}
    lay = {n: a[n] for n in ("x", "mem", "mix_w_in", "w_proj_gdn", "w_proj_ssd", "w_proj_ret", "mix_w_out", "xa_w_q", "xa_w_k", "xa_w_v", "xa_w_o",
                              "router_w", "moe_w_gate", "moe_w_up", "moe_w_down")}
    for n in ("ln_mix_g", "ln_mix_b", "ln_xa_g", "ln_xa_b", "ln_moe_g", "ln_moe_b"):
        lay[n] = _np.broadcast_to(a[n][0], (P, D))
    lay["router_rows"] = _np.broadcast_to(a["router_b"], (P, NE))
    rows = _np.concatenate([a["gdn_a_log"][0], a["ssd_a_log"][0], a["gdn_dt_bias"][0], a["ssd_dt_bias"][0], a["ssd_d"][0]])
    lay["par_rows"] = _np.broadcast_to(rows, (P, 64))
    lay["conv_g"] = a["gdn_conv_w"][0].reshape(4, 24, P).transpose(2, 0, 1)
    lay["conv_s"] = a["ssd_conv_w"][0].reshape(4, 16, P).transpose(2, 0, 1)
    lay["convb_s"] = a["ssd_conv_b"][0].reshape(16, P).T
    lay["norm_g"] = a["gdn_norm_w"][0].reshape(P, 1)
    lay["norm_s"] = a["ssd_norm_w"][0].reshape(KT, P).T
    lay["consts"] = shape_constants()
    arrays, t = {}, {}
    for name, v in lay.items():
        v = _np.ascontiguousarray(v)
        arrays[f"in_{name}"] = v
        t[name] = nc.dram_tensor(f"in_{name}", v.shape, _mybir.dt.from_np(v.dtype), kind="ExternalInput").ap()
    out = nc.dram_tensor("out_0", (1, S, D), _mybir.dt.float32, kind="ExternalOutput").ap()
    x2_dram = nc.dram_tensor("x2_rows", (S, D), _mybir.dt.float32, kind="Internal").ap()
    y_dram = nc.dram_tensor("expert_rows", (NB * P, D), _mybir.dt.float32, kind="Internal").ap()
    program(nc, t, out, x2_dram, y_dram)
    r = _run(nc, [arrays], core_ids=[0])
    return r.results[0]["out_0"]
```

```python
import concourse.bass as bass
from concourse import mybir
from contextlib import ExitStack
import numpy as np

D = 1024
S = 512
P = 128
KT = D // P
NT = S // P
GH = 8
SG, SR = 4, 4
SH = SG * SR
RH = 4
NE = 16
F = 512
MEM = 256
XH = 4
ALPHA = 2.0 ** 0.25
LN_EPS, RMS_EPS = 1e-5, 1e-6
NOV = 7
NB = NE + NOV
LEVELS = 7
NEG = -1e30
C_GQKV, C_GZ, C_GA, C_GB = 0, 3072, 4096, 4104
C_SX, C_SB, C_SC, C_SZ, C_SDT = 4112, 5136, 5648, 6160, 7184
C_RQ, C_RK, C_RV, C_RG, C_GATE = 7200, 7712, 8224, 9248, 10272
K_ID, K_U, K_L, K_ONE, K_NEG, K_MASK = 0, 128, 256, 384, 512, 640
K_RDEC = K_MASK + LEVELS * 128
K_RKW = K_RDEC + RH * 128
K_RCUM = K_RKW + RH
K_COS = K_RCUM + RH
K_SIN = K_COS + NT * 64
K_RTOT = K_SIN + NT * 64
K_SLOT = K_RTOT + RH
K_TOK = K_SLOT + 128
K_END = K_TOK + NT


def shape_constants():
    f = np.float32
    i = np.arange(P)
    c = np.zeros((P, K_END), f)
    c[:, K_ID:K_ID + P] = np.eye(P)
    c[:, K_U:K_U + P] = i[:, None] <= i[None, :]
    c[:, K_L:K_L + P] = i[:, None] > i[None, :]
    c[:, K_ONE:K_ONE + P] = 1.0
    c[:, K_NEG:K_NEG + P] = np.where(i[None, :] >= i[:, None], 0.0, NEG)
    for l in range(LEVELS):
        b = 1 << l
        same = (i[:, None] // (2 * b)) == (i[None, :] // (2 * b))
        c[:, K_MASK + l * P:K_MASK + (l + 1) * P] = same & ((i[:, None] // b) % 2 == 0) & ((i[None, :] // b) % 2 == 1)
    for h in range(RH):
        lg = np.log1p(-np.exp2(f(-5.0 - h))).astype(f)
        d = (i[None, :] - i[:, None]).astype(f)
        c[:, K_RDEC + h * P:K_RDEC + (h + 1) * P] = np.where(d >= 0, np.exp(np.minimum(d, P) * lg * (d >= 0)), 0.0)
        c[:, K_RKW + h] = np.exp(lg * (P - 1 - i))
        c[:, K_RCUM + h] = np.exp(lg * (i + 1))
        c[:, K_RTOT + h] = np.exp(lg * P)
    inv = (f(10000.0) ** (-np.arange(0, P, 2, dtype=f) / f(P))).astype(f)
    ang = (np.arange(S, dtype=f)[:, None] * inv[None, :]).astype(f)
    for n in range(NT):
        c[:, K_COS + n * 64:K_COS + (n + 1) * 64] = np.cos(ang[n * P:(n + 1) * P])
        c[:, K_SIN + n * 64:K_SIN + (n + 1) * 64] = np.sin(ang[n * P:(n + 1) * P])
        c[:, K_TOK + n] = n * P + i
    c[:, K_SLOT:K_SLOT + P] = i[None, :]
    return c


class Count:

    def __init__(self, eng, sem, per, turn=0, base=0):
        self.eng, self.sem, self.n, self.per, self.turn, self.base = eng, sem, 0, per, turn, base

    def __call__(self, ins):
        self.n += 1
        ins.then_inc(self.sem, 1)
        self.eng.wait_ge(self.sem, self.turn * self.per + (self.base + self.n))

    def done(self):
        assert self.n == self.per, (self.n, self.per)


def program(nc, t, out, x2_dram, y_dram):
    f32, f32r, bf16, i32 = mybir.dt.float32, mybir.dt.float32r, mybir.dt.bfloat16, mybir.dt.int32
    ALU, ACT, AX = mybir.AluOpType, mybir.ActivationFunctionType, mybir.AxisListType
    ds = bass.ds
    ctx = ExitStack()
    with ctx:
        def sb(name, shape, dt=f32):
            return ctx.enter_context(nc.sbuf_tensor(name, shape, dt))

        def sem(name):
            return ctx.enter_context(nc.semaphore(name))

        def pair(stack, name, shape):
            with nc.sbuf_tensor(name, shape, f32) as whole:
                pass
            return whole, stack.enter_context(nc.sbuf_tensor(name + "_lo", shape, f32r))

        cst = sb("cst", [P, K_END])
        ident = cst[:, K_ID:K_ID + P]
        identb = sb("identb", [P, P], bf16)
        negb = sb("negb", [P, NT, P], bf16)
        xres = sb("xres", [P, NT, D])
        par = sb("par", [P, 64])
        cw_g = sb("cw_g", [P, 4, 24])
        cw_s = sb("cw_s", [P, 4, 16])
        cb_s = sb("cb_s", [P, 16])
        nw_g = sb("nw_g", [P, 1])
        nw_s = sb("nw_s", [P, KT])
        half = sb("half", [P, 40])
        la = sb("la", [P, NT, 24])
        sp = sb("sp", [P, NT, 24])
        beta = sb("beta", [P, NT, 8])
        ecum = sb("ecum", [P, NT, 24])
        ekw = sb("ekw", [P, NT, 24])
        etot = sb("etot", [P, NT, 24])
        becum = sb("becum", [P, NT, 8])
        r_g = sb("r_g", [P, 2, NT])
        r_slot = sb("r_slot", [P, 2, NT], i32)
        r_idx = sb("r_idx", [P, NB], i32)
        r_tab = sb("r_tab", [1, 8], i32)
        yT, ylo = pair(ctx, "yT", [P, 3, KT, S])
        upper = ExitStack()

        def ub_(name, shape, dt=f32):
            return upper.enter_context(nc.sbuf_tensor(name, shape, dt))

        xT, xlo = pair(upper, "xT", [P, KT, S])
        rw, rb = ub_("rw", [P, KT, NE]), ub_("rb", [P, NE])
        mid = ExitStack()
        upper.push(mid)
        ring, ringlo = pair(mid, "ring", [P, 6, KT, P])
        psum = [ctx.enter_context(nc.psum_tensor(f"bank{i}", [P, 512], f32)) for i in range(8)]

        w_loaded = [sem(f"w_loaded{i}") for i in range(6)]
        uses = [0] * 6
        g_ready = [sem(f"gemm_ready{i}") for i in range(2)]
        g_free = [sem(f"gemm_free{i}") for i in range(2)]
        hi_ready = [sem(f"weight_hi{i}") for i in range(2)]
        lo_ready = [sem(f"weight_lo{i}") for i in range(2)]
        splits = [0, 0]
        units = [0, 0]

        sp_turn = sem("sp_turn")
        phase_sems = []
        psem = sem

        def sem(name):
            phase_sems.append(nc.alloc_semaphore(name=name))
            return phase_sems[-1]

        def end_phase():
            nc.clear_and_free_semaphores(phase_sems)
            nc.all_engine_barrier()
            phase_sems.clear()

        wide_in, rows_in = [psem(f"wide_in{h}") for h in range(2)], psem("rows_in")

        w_in = t["mix_w_in"][0]

        def w_cols(w, c0, n):
            return w[:, ds(c0, n)].rearrange("(k p) c -> p k c", p=P)

        def v3(ap, n=NT):
            return ap.rearrange("p (n c) -> p n c", n=n)


        class Products:

            def __init__(self, per, cols, turns, splits_per=0, joint=()):
                self.joint = joint
                self.per, self.cols, self.turns, self.splits_per = per, cols, turns, splits_per
                self.split_base = list(splits)
                for b in range(2):
                    splits[b] += splits_per * turns
                self.base, self.us = list(units), list(uses)
                for b in range(2):
                    units[b] += per * turns
                for j in range(2 * per):
                    uses[j] += turns

            def count(self, j, i):
                return i * self.per + (self.base[j % 2] + j // 2 + 1)

            def wait_ready(self, eng, j, i):
                eng.wait_ge(g_ready[j % 2], self.count(j, i))

            def wait_read(self, eng, j, i):
                eng.wait_ge(g_free[j % 2], i * self.per + (self.base[j % 2] + j // 2 + 2))

            def wait_used(self, eng, j, i):
                if j in self.joint:
                    self.wait_ready(eng, j ^ 1, i)
                self.wait_ready(eng, j, i)

            def load_first(self, sp_, j):
                sp_.dma_start(ring[:, j], self.cols(j, 0)).then_inc(w_loaded[j], 16)

            def load_next(self, sp_, j, i):
                src = self.cols(j, i + 1)
                self.wait_used(sp_, j, i)
                sp_.sem_inc(sp_turn, 1)
                sp_.dma_start(ring[:, j], src).then_inc(w_loaded[j], 16)

            def split_count(self, j, i):
                return i * self.splits_per + (self.split_base[j % 2] + j // 2 + 1)

            def split_hi(self, act, j, i, hi):
                act.wait_ge(w_loaded[j], (i + (self.us[j] + 1)) * 16)
                nc.scalar.activation(hi[j % len(hi)], ring[:, j], ACT.Copy).then_inc(hi_ready[j % 2], 1)

            def split_lo(self, eng, unit, j, i, hi):
                eng.wait_ge(hi_ready[j % 2], self.split_count(j, i))
                unit.tensor_tensor(ringlo[:, j], ring[:, j], hi[j % len(hi)].bitcast(f32), ALU.subtract).then_inc(lo_ready[j % 2], 1)

            def features3(self, pe, j, i, hi, rhs_hi, rhs_lo, cols=S, rhs_split=None, k0=0, k1=KT):
                if k0 == 0:
                    pe.wait_ge(lo_ready[j % 2], self.split_count(j, i))
                    pe.wait_ge(g_free[j % 2], self.count(j, i))
                for k in range(k0, k1):
                    if rhs_split:
                        rhs_split(k)
                    for m, (a, b) in enumerate(((hi[j % len(hi)][:, k, :], rhs_hi), (hi[j % len(hi)][:, k, :], rhs_lo), (ringlo[:, j, k, :], rhs_hi))):
                        ins = nc.tensor.matmul(psum[j % 2][:, 0:cols], a, b[:, k, :], start=(k + m == 0), stop=(k == KT - 1 and m == 2))
                if k1 == KT:
                    ins.then_inc(g_ready[j % 2], 1)

            def pair_tokens3(self, pe, j, half, i, hi2, x_hi, x_lo, tiles=2):
                if half == 0:
                    for b in range(2):
                        pe.wait_ge(lo_ready[b], self.split_count(j + b, i))
                pe.wait_ge(g_free[half], self.count(j + half, i))
                for n in range(tiles * half, tiles * half + tiles):
                    bank = psum[half][:, (n % tiles) * 256:(n % tiles) * 256 + 256].rearrange("p (a c) -> p a c", a=2)
                    for k in range(KT):
                        for m, (a, b) in enumerate(((x_hi, hi2), (x_hi, ringlo[:, j:j + 2]), (x_lo, hi2))):
                            ins = nc.tensor.matmul(bank, a[:, k, n * P:(n + 1) * P], b[:, :, k, :], start=(k + m == 0), stop=(k == KT - 1 and m == 2))
                ins.then_inc(g_ready[half], 1)

        def in_turns(eng, turns, body):
            with eng.Fori(0, turns - 1) as i:
                body(i, True)
            body(turns - 1, False)

        def cols_of(*firsts):
            return lambda j, i: w_cols(w_in, i * firsts[j][1] + firsts[j][0], P)

        ret_g = Products(3, cols_of((C_RQ, P), (C_RK, P), (C_RV, 256), (C_RV + P, 256), (C_RG, 256), (C_RG + P, 256)), RH, 3, (0, 1, 2, 3))
        ssd_g = Products(3, cols_of((C_SX, 256), (C_SX + P, 256), (C_SB, P), (C_SC, P), (C_SZ, 256), (C_SZ + P, 256)), SG, 3, (4, 5))
        gdn_g = Products(2, cols_of((C_GQKV, P), (C_GQKV + 1024, P), (C_GQKV + 2048, P), (C_GZ, P)), GH, 2)
        projs = [t["w_proj_gdn"][0], t["w_proj_ssd"][0], t["w_proj_ret"][0]]
        mrg_g = [Products(2, lambda j, i, b=b: w_cols(projs[b], i * 256 + (j // 2) * P, P) if j % 2 else w_cols(w_in, i * 256 + (C_GATE + b * D + (j // 2) * P), P),
                          KT // 2, 2) for b in range(3)]
        xw = [t["xa_w_q"][0], t["xa_w_k"][0], t["xa_w_v"][0]]
        xa_g = Products(3, lambda j, i: w_cols(xw[j // 2], i * 256 + (j % 2) * P, P), XH, 3, (4, 5))

        xsplit = ylo[:, 0]

        with ExitStack() as c2:
            x_tok = xres
            quarters = [(2 * n + a, n, a) for n in range(NT) for a in range(2)]

            def quarter(ap, n, a):
                return ap[:, 4 * a:4 * a + 4, n * P:(n + 1) * P]

            wsm = c2.enter_context(nc.sbuf_tensor("wsm", [P, KT, 32], f32))
            sm = c2.enter_context(nc.sbuf_tensor("sm", [P, 12, NT, 24], f32))
            bsm = c2.enter_context(nc.sbuf_tensor("bsm", [P, 2, NT, 8], f32))
            nea = c2.enter_context(nc.sbuf_tensor("nea", [P, 24], f32))
            s_x, s_cst, s_par = [sem(f"x_in{n}") for n in range(NT)], sem("cst_in"), sem("par_in")
            s_wsm = sem("small_columns_in")
            s_xt, s_xtf, s_sm, s_xhi, s_xlo = sem("xT_psum"), sem("xT_done"), sem("small_psum"), sem("x_hi"), sem("x_lo")
            s_v, s_a, s_cum, s_half = sem("in_dve"), sem("in_act"), sem("cum_psum"), sem("half_set")
            with nc.Block() as block:
                @block.sync
                def _(sp_):
                    sp_.dma_start(cst[:, 0:P], t["consts"][:, 0:P]).then_inc(s_cst, 16)
                    for n in range(NT):
                        sp_.dma_start(x_tok[:, n, :], t["x"][0, n * P:(n + 1) * P, :]).then_inc(s_x[n], 16)
                    sp_.dma_start(wsm[:, :, 0:8], w_cols(w_in, C_GA, 8)).then_inc(s_wsm, 16)
                    sp_.dma_start(wsm[:, :, 8:24], w_cols(w_in, C_SDT, 16)).then_inc(s_wsm, 16)
                    sp_.dma_start(wsm[:, :, 24:32], w_cols(w_in, C_GB, 8)).then_inc(s_wsm, 16)
                    sp_.dma_start(par[:, :], t["par_rows"]).then_inc(s_par, 16)
                    sp_.dma_start(cst[:, P:K_END], t["consts"][:, P:K_END]).then_inc(s_par, 16)
                    sp_.dma_start(cw_g[:, :, :], t["conv_g"]).then_inc(s_par, 16)
                    sp_.dma_start(cw_s[:, :, :], t["conv_s"]).then_inc(s_par, 16)
                    sp_.dma_start(cb_s[:, :], t["convb_s"]).then_inc(s_par, 16)
                    sp_.dma_start(nw_g[:, :], t["norm_g"]).then_inc(s_par, 16)
                    sp_.dma_start(nw_s[:, :], t["norm_s"]).then_inc(s_par, 16)
                    for j in range(6):
                        ret_g.load_first(sp_, j)

                @block.gpsimd
                def _(pool):
                    nc.gpsimd.memset(half[:, :], -0.5).then_inc(s_half, 1)
                    pool.wait_ge(s_sm, 1)
                    for u, n, a in quarters:
                        pool.wait_ge(s_xhi, u + 1)
                        nc.gpsimd.tensor_tensor(quarter(xlo, n, a), quarter(xT, n, a), quarter(xsplit, n, a).bitcast(f32), ALU.subtract).then_inc(s_xlo, 1)

                @block.tensor
                def _(pe):
                    pe.wait_ge(s_cst, 16)
                    for u, n, a in quarters:
                        pe.wait_ge(s_x[n], 16)
                        if u >= 4:
                            pe.wait_ge(s_xtf, u - 3)
                        for k in range(4):
                            ins = nc.tensor.transpose(psum[u % 4][:, k * P:(k + 1) * P], x_tok[:, n, (4 * a + k) * P:(4 * a + k + 1) * P], ident)
                        ins.then_inc(s_xt, 1)
                    pe.wait_ge(s_wsm, 16 * 3)
                    pe.wait_ge(s_xtf, KT)
                    for n in range(NT):
                        for k in range(KT):
                            ins = nc.tensor.matmul(psum[4][:, n * 32:(n + 1) * 32], xT[:, k, n * P:(n + 1) * P], wsm[:, k, :],
                                                   start=(k == 0), stop=(k == KT - 1))
                    ins.then_inc(s_sm, 1)
                    pe.wait_ge(s_par, 16 * 7)
                    pe.wait_ge(s_cum, 1)
                    for n in range(NT):
                        nc.tensor.matmul(psum[5][:, n * 24:(n + 1) * 24], cst[:, K_U:K_U + P], la[:, n, :], start=True, stop=True)
                        ins = nc.tensor.matmul(psum[6][:, n * 24:(n + 1) * 24], cst[:, K_ONE:K_ONE + P], la[:, n, :], start=True, stop=True)
                    ins.then_inc(s_sm, 1)

                small = psum[4][:, 0:128].rearrange("p (n c) -> p n c", n=NT)
                cum_ps = psum[5][:, 0:96].rearrange("p (n c) -> p n c", n=NT)
                tot_ps = psum[6][:, 0:96].rearrange("p (n c) -> p n c", n=NT)

                @block.vector
                def _(dve):
                    link = Count(dve, s_v, 0)
                    for b in range(2):
                        dve.sem_inc(g_free[b], 1)
                    for u, n, a in quarters:
                        dve.wait_ge(s_xt, u + 1)
                        nc.vector.tensor_copy(quarter(xT, n, a), v3(psum[u % 4][:, :])).then_inc(s_xtf, 1)
                    dve.wait_ge(s_par, 16 * 7)
                    nc.vector.tensor_copy(identb[:, :], ident)
                    nc.vector.tensor_copy(negb[:, :, :], cst[:, K_NEG:K_NEG + P].unsqueeze(1).to_broadcast([P, NT, P]))
                    nc.vector.tensor_scalar(cw_g[:, :, :], cw_g[:, :, :], 0.5, None, ALU.mult)
                    nc.vector.tensor_scalar(cw_s[:, :, :], cw_s[:, :, :], 0.5, None, ALU.mult)
                    nc.vector.tensor_scalar(cb_s[:, :], cb_s[:, :], 0.5, None, ALU.mult)
                    dve.wait_ge(s_sm, 1)
                    z, m, neg, u, w, d, d0, dd, r, lnw, v, v2 = [sm[:, j] for j in range(12)]
                    nc.vector.tensor_scalar(bsm[:, 0], small[:, :, 24:32], -1.0, None, ALU.mult)
                    link(nc.vector.tensor_tensor(z, small[:, :, 0:24], par[:, 24:48].unsqueeze(1).to_broadcast([P, NT, 24]), ALU.add))
                    link(nc.vector.tensor_scalar(m, z, 0.0, None, ALU.max))
                    link(nc.vector.scalar_tensor_tensor(out=neg, in0=z, scalar=0.0, in1=m, op0=ALU.min, op1=ALU.subtract))
                    dve.wait_ge(s_a, 3)
                    link(nc.vector.tensor_scalar(w, u, 1.0, None, ALU.add))
                    link(nc.vector.tensor_scalar(d, w, -1.0, None, ALU.add))
                    link(nc.vector.tensor_scalar(d0, d, 0.0, None, ALU.is_equal))
                    link(nc.vector.tensor_tensor(dd, d, d0, ALU.add))
                    link(nc.vector.reciprocal(r, dd))
                    link(nc.vector.tensor_tensor(r, r, u, ALU.mult))
                    dve.wait_ge(s_a, 4)
                    link(nc.vector.tensor_tensor(v, lnw, r, ALU.mult))
                    link(nc.vector.tensor_tensor(v2, u, d0, ALU.mult))
                    link(nc.vector.tensor_tensor(v, v, v2, ALU.add))
                    link(nc.vector.tensor_tensor(sp[:, :, :], v, m, ALU.add))
                    link(nc.vector.tensor_tensor(la[:, :, :], sp[:, :, :], nea[:, :].unsqueeze(1).to_broadcast([P, NT, 24]), ALU.mult))
                    nc.vector.tensor_scalar(la[:, :, :], la[:, :, :], -1.0, None, ALU.mult).then_inc(s_cum, 1)
                    link(nc.vector.tensor_scalar(bsm[:, 0], bsm[:, 1], 1.0, None, ALU.add))
                    link(nc.vector.reciprocal(beta[:, :, :], bsm[:, 0]))
                    dve.wait_ge(s_sm, 2)
                    link(nc.vector.tensor_copy(z, cum_ps))
                    nc.vector.tensor_tensor(v, tot_ps, z, ALU.subtract).then_inc(s_cum, 1)
                    dve.wait_ge(s_a, 7)
                    nc.vector.tensor_tensor(becum[:, :, :], beta[:, :, :], ecum[:, :, 0:8], ALU.mult)

                @block.scalar
                def _(act):
                    for u, n, a in quarters:
                        act.wait_ge(s_xtf, u + 1)
                        nc.scalar.activation(quarter(xsplit, n, a), quarter(xT, n, a), ACT.Copy).then_inc(s_xhi, 1)
                    act.wait_ge(s_v, 3)
                    nc.scalar.activation(sm[:, 3], sm[:, 2], ACT.Exp).then_inc(s_a, 1)
                    nc.scalar.activation(bsm[:, 1], bsm[:, 0], ACT.Exp).then_inc(s_a, 1)
                    nc.scalar.activation(nea[:, :], par[:, 0:24], ACT.Exp).then_inc(s_a, 1)
                    act.wait_ge(s_v, 4)
                    nc.scalar.activation(sm[:, 9], sm[:, 4], ACT.Ln).then_inc(s_a, 1)
                    act.wait_ge(s_cum, 2)
                    nc.scalar.activation(ekw[:, :, :], sm[:, 10], ACT.Exp).then_inc(s_a, 1)
                    nc.scalar.activation(ecum[:, :, :], cum_ps, ACT.Exp).then_inc(s_a, 1)
                    nc.scalar.activation(etot[:, :, :], tot_ps, ACT.Exp).then_inc(s_a, 1)

        end_phase()
        with ExitStack() as c2:
            def b2(name, shape, dt=f32):
                return c2.enter_context(nc.sbuf_tensor("r_" + name, shape, dt))

            t1, t2 = b2("t1", [P, 2, 4, 64]), b2("t2", [P, 2, 4, 64])
            qk = b2("qk", [P, NT, 2, P])
            qr, kr = qk[:, :, 0, :], qk[:, :, 1, :]
            qd, kd = b2("qd", [P, NT, P]), b2("kd", [P, NT, P])
            hi6 = b2("hi", [P, 6, KT, P], f32r)
            hi = [hi6[:, j] for j in range(6)]
            kT, qT, qdT, M = [b2(n_, [P, S]) for n_ in ("kT", "qT", "qdT", "M")]
            v = b2("v", [P, NT, 2, P])
            gh, gt, sg = b2("gh", [P, 2, S]), b2("gt", [P, 2, S]), b2("sg", [P, 2, S])
            St = b2("St", [P, 3, 2 * P])
            bn, mv = b2("bn", [P, NT, 6]), b2("mv", [P, NT, 2])
            var, rs = b2("var", [P, NT]), b2("rs", [P, NT])
            on = b2("on", [P, NT, 2, P])
            names = ("rot rot_done kd_done tokT_psum tokT_done score_psum m_done v_done gh_done gt_done sg_done kv_psum state o_psum "
                     "stat stat_all rs_in rs_out on_ready oT_psum y_done").split()
            q_ = {n_: sem("r_" + n_) for n_ in names}
            zero, zero_set, zeros_out = b2("zero", [P, D]), sem("r_zero_set"), sem("r_zeros_stored")
            g = ret_g

            with nc.Block() as block:
                @block.sync
                def _(sp_):
                    sp_.wait_ge(zero_set, 1)
                    for j in range(NOV):
                        sp_.dma_start(y_dram[(NE + j) * P:(NE + j + 1) * P, :], zero[:, :]).then_inc(zeros_out, 16)
                    in_turns(sp_, RH, lambda i, more: [g.load_next(sp_, j, i) for j in range(6)] if more else None)
                    for j in range(6):
                        g.wait_used(sp_, j, RH - 1)
                        ssd_g.load_first(sp_, j)
                    sp_.wait_ge(zeros_out, 16 * NOV)

                @block.tensor
                def _(pe):
                    def body(i, more):
                        for half in range(2):
                            g.pair_tokens3(pe, 2, half, i, hi6[:, 2:4], xsplit, xlo)
                        pe.wait_ge(q_["y_done"], i * 2 + 2)
                        for j, src in enumerate((kr, qr, qd)):
                            pe.wait_ge(q_["rot_done"], i * 5 + (4, 4, 5)[j])
                            for n in range(NT):
                                ins = nc.tensor.transpose(psum[2 + j][:, n * P:(n + 1) * P], src[:, n, :], ident)
                            ins.then_inc(q_["tokT_psum"], 1)
                        pe.wait_ge(q_["tokT_done"], i * 3 + 3)
                        for n in range(NT):
                            c = slice(n * P, (n + 1) * P)
                            ins = nc.tensor.matmul(psum[2][:, c], kT[:, c], qT[:, c], start=True, stop=True)
                        ins.then_inc(q_["score_psum"], 1)
                        g.features3(pe, 4, i, hi, xsplit, xlo)
                        pe.wait_ge(q_["v_done"], i * 2 + 2)
                        pe.wait_ge(q_["kd_done"], i + 1)
                        for n in range(NT - 1):
                            bank, c0 = psum[3 + n // 2], (n % 2) * 256
                            ins = nc.tensor.matmul(bank[:, c0:c0 + 256], kd[:, n, :], v[:, n].rearrange("p a c -> p (a c)"), start=True, stop=True)
                        ins.then_inc(q_["kv_psum"], 1)
                        g.features3(pe, 5, i, hi, xsplit, xlo)
                        pe.wait_ge(q_["m_done"], i + 1)
                        pe.wait_ge(q_["state"], i * 3 + 3)
                        for n in range(NT):
                            c = slice(n * P, (n + 1) * P)
                            bank, c0 = psum[6 + n // 2], (n % 2) * 256
                            if n:
                                nc.tensor.matmul(bank[:, c0:c0 + 256], qdT[:, c], St[:, n - 1, :], start=True, stop=False)
                            ins = nc.tensor.matmul(bank[:, c0:c0 + 256], M[:, c], v[:, n].rearrange("p a c -> p (a c)"), start=(n == 0), stop=True)
                        ins.then_inc(q_["o_psum"], 1)
                        if more:
                            for half in range(2):
                                g.pair_tokens3(pe, 0, half, i + 1, hi6[:, 0:2], xsplit, xlo)
                        pe.wait_ge(q_["on_ready"], i + 1)
                        for a in range(2):
                            for n in range(NT):
                                ins = nc.tensor.transpose(psum[3 + a][:, n * P:(n + 1) * P], on[:, n, a, :], ident)
                            ins.then_inc(q_["oT_psum"], 1)

                    for half in range(2):
                        g.pair_tokens3(pe, 0, half, 0, hi6[:, 0:2], xsplit, xlo)
                    in_turns(pe, RH, body)

                @block.scalar
                def _(act):
                    def body(i, more):
                        for j, (dst, sc) in enumerate(((kT, P ** -0.5), (qT, 1.0), (qdT, 1.0))):
                            act.wait_ge(q_["tokT_psum"], i * 3 + (j + 1))
                            nc.scalar.activation(dst[:, :], psum[2 + j][:, :], ACT.Copy, scale=sc).then_inc(q_["tokT_done"], 1)
                        for a in range(2):
                            g.wait_ready(act, 2 + a, i)
                            nc.scalar.activation(v[:, 2 * a:2 * a + 2].rearrange("p n a c -> p (n a c)"), psum[a][:, :], ACT.Copy).then_inc(g_free[a], 1)
                            g.wait_read(act, 2 + a, i)
                            act.sem_inc(q_["v_done"], 1)
                        if more:
                            for j in range(2):
                                g.split_hi(act, j, i + 1, hi)
                        for a in range(2):
                            g.wait_ready(act, 4 + a, i)
                            if a == 0:
                                act.wait_ge(q_["y_done"], i * 2 + 2)
                            nc.scalar.activation(gh[:, a, :], psum[a][:, :], ACT.Copy, scale=0.5).then_inc(q_["gh_done"], 1)
                            nc.scalar.activation(gt[:, a, :], psum[a][:, :], ACT.Tanh, scale=0.5).then_inc(g_free[a], 1)
                        if more:
                            for j in range(2, 6):
                                g.split_hi(act, j, i + 1, hi)

                    for j in range(6):
                        g.split_hi(act, j, 0, hi)
                    in_turns(act, RH, body)

                @block.gpsimd
                def _(pool):
                    def body(i, more):
                        if more:
                            for j in range(4):
                                g.split_lo(pool, nc.gpsimd, j, i + 1, hi)
                        pool.wait_ge(q_["rs_in"], i + 1)
                        nc.gpsimd.tensor_tensor(rs[:, :], var[:, :], half[:, 0:NT], ALU.pow).then_inc(q_["rs_out"], 1)
                        if more:
                            for j in range(4, 6):
                                g.split_lo(pool, nc.gpsimd, j, i + 1, hi)

                    nc.gpsimd.memset(zero[:, :], 0.0).then_inc(zero_set, 1)
                    in_turns(pool, RH, body)

                @block.vector
                def _(dve):
                    cos, sin = [cst[:, c:c + NT * 64].rearrange("p (n c) -> p n c", n=NT) for c in (K_COS, K_SIN)]

                    def rotate(b, i):
                        g.wait_ready(dve, b, i)
                        n = slice(2 * b, 2 * b + 2)
                        ps = psum[b][:, :].rearrange("p (n a c) -> p n a c", n=2, a=4)
                        for tmp, table, done in ((t1, cos, q_["rot"]), (t2, sin, g_free[b])):
                            nc.vector.tensor_tensor(tmp[:, :, :, :], ps, table[:, n].unsqueeze(2).to_broadcast([P, 2, 4, 64]), ALU.mult).then_inc(done, 1)
                        g.wait_read(dve, b, i)
                        dve.wait_ge(q_["rot"], i * 2 + (b + 1))
                        a1, a2 = [x_[:, :, :, :].rearrange("p n (j a) c -> p n j a c", j=2) for x_ in (t1, t2)]
                        nc.vector.tensor_tensor(qk[:, n, :, 0:64], a1[:, :, :, 0, :], a2[:, :, :, 1, :], ALU.subtract).then_inc(q_["rot_done"], 1)
                        nc.vector.tensor_tensor(qk[:, n, :, 64:128], a1[:, :, :, 1, :], a2[:, :, :, 0, :], ALU.add).then_inc(q_["rot_done"], 1)
                        dve.wait_ge(q_["rot_done"], i * 5 + (2 * b + 2))

                    def decayed(i):
                        nc.vector.tensor_scalar(qd[:, :, :], qr, cst[:, ds(i + K_RCUM, 1)], None, ALU.mult).then_inc(q_["rot_done"], 1)
                        nc.vector.tensor_scalar(kd[:, :, :], kr, cst[:, ds(i + K_RKW, 1)], P ** -0.5, ALU.mult, ALU.mult).then_inc(q_["kd_done"], 1)

                    def body(i, more):
                        dve.wait_ge(q_["score_psum"], i + 1)
                        nc.vector.tensor_tensor(v3(M[:, :]), v3(psum[2][:, :]), cst[:, ds(i * P + K_RDEC, P)].unsqueeze(1).to_broadcast([P, NT, P]),
                                                ALU.mult).then_inc(q_["m_done"], 1)
                        dve.wait_ge(q_["kv_psum"], i + 1)
                        for n in range(NT - 1):
                            kv = psum[3 + n // 2][:, (n % 2) * 256:(n % 2) * 256 + 256]
                            if n == 0:
                                nc.vector.tensor_copy(St[:, 0, :], kv).then_inc(q_["state"], 1)
                            else:
                                dve.wait_ge(q_["state"], i * 3 + n)
                                nc.vector.scalar_tensor_tensor(out=St[:, n, :], in0=St[:, n - 1, :], scalar=cst[:, ds(i + K_RTOT, 1)], in1=kv,
                                                               op0=ALU.mult, op1=ALU.add).then_inc(q_["state"], 1)
                        for a in range(2):
                            g.wait_read(dve, 4 + a, i)
                            nc.vector.scalar_tensor_tensor(out=sg[:, a, :], in0=gt[:, a, :], scalar=1.0, in1=gh[:, a, :], op0=ALU.add, op1=ALU.mult).then_inc(q_["sg_done"], 1)
                        dve.wait_ge(q_["o_psum"], i + 1)
                        for n in range(NT):
                            nc.vector.bn_stats(bn[:, n, :], psum[6 + n // 2][:, (n % 2) * 256:(n % 2) * 256 + 256]).then_inc(q_["stat"], 1)
                        dve.wait_ge(q_["stat"], i * 8 + 4)
                        dve.sem_inc(q_["stat_all"], 1)
                        for n in range(NT):
                            nc.vector.bn_aggr(mv[:, n, :], bn[:, n, :]).then_inc(q_["stat"], 1)
                        dve.wait_ge(q_["stat"], i * 8 + 8)
                        nc.vector.tensor_scalar(var[:, :], mv[:, :, 1], LN_EPS, None, ALU.add).then_inc(q_["rs_in"], 1)
                        dve.wait_ge(q_["rs_out"], i + 1)
                        for n in range(NT):
                            ins = nc.vector.tensor_scalar(on[:, n].rearrange("p a c -> p (a c)"), psum[6 + n // 2][:, (n % 2) * 256:(n % 2) * 256 + 256],
                                                          mv[:, n, 0:1], rs[:, n:n + 1], ALU.subtract, ALU.mult)
                        ins.then_inc(q_["on_ready"], 1)
                        if more:
                            rotate(0, i + 1)
                            rotate(1, i + 1)
                            decayed(i + 1)
                        dve.wait_ge(q_["sg_done"], i * 2 + 2)
                        for a in range(2):
                            dve.wait_ge(q_["oT_psum"], i * 2 + (a + 1))
                            nc.vector.tensor_tensor(yT[:, 2, ds(i * 2 + a, 1), :].rearrange("p a c -> p (a c)"), psum[3 + a][:, :], sg[:, a, :], ALU.mult).then_inc(q_["y_done"], 1)

                    dve.sem_inc(q_["y_done"], 2)
                    for j in range(4):
                        g.split_lo(dve, nc.vector, j, 0, hi)
                    rotate(0, 0)
                    rotate(1, 0)
                    for j in range(4, 6):
                        g.split_lo(dve, nc.vector, j, 0, hi)
                    decayed(0)
                    in_turns(dve, RH, body)

        end_phase()
        with ExitStack() as c2:
            def b2(name, shape, dt=f32):
                return c2.enter_context(nc.sbuf_tensor("s_" + name, shape, dt))

            acc, th, fm = b2("acc", [P, 4, S]), b2("th", [P, 4, S]), b2("fm", [P, 4, S])
            zh, zt = b2("zh", [P, NT, 2, P]), b2("zt", [P, NT, 2, P])
            sz = zt
            xs, bt = b2("xs", [P, NT, 2, P]), b2("bt", [P, NT, P])
            v, vk, y = b2("v", [P, NT, 256]), b2("vk", [P, NT, 256]), b2("y", [P, NT, 256])
            lla, dec = b2("lla", [P, SR, NT, P]), b2("dec", [P, SR, S])
            M = dec
            hi4 = b2("hi", [P, 4, KT, P], f32r)
            hi = [hi4[:, b] for b in (2, 3, 0, 1, 0, 1)]
            St, ts = b2("St", [P, 3, 256]), b2("ts", [P, 2, 256])
            yi = zh[:, 0:3].rearrange("p n a c -> p n (a c)")
            ssq, rs = b2("ssq", [P, NT]), b2("rs", [P, NT])
            names = ("conv_acc conv_th conv_fm fm_done cv zh_done zt_done sz_done tok_psum tok_done lla_ready dec_psum dec_ready score_psum m_done "
                     "v_done vk_done kv_psum st state y_psum yw sq_done rs_in rs_out on_ready oT_psum y_done").split()
            q_ = {n_: sem("s_" + n_) for n_ in names}
            g = ssd_g

            with nc.Block() as block:
                @block.sync
                def _(sp_):
                    in_turns(sp_, SG, lambda i, more: [g.load_next(sp_, j, i) for j in range(6)] if more else None)
                    for j in range(4):
                        g.wait_used(sp_, j, SG - 1)
                        gdn_g.load_first(sp_, j)

                @block.tensor
                def _(pe):
                    def decays(i, r):
                        pe.wait_ge(q_["lla_ready"], i * 4 + (r + 1))
                        if r >= 2:
                            pe.wait_ge(q_["dec_ready"], i * 4 + (r - 1))
                        b = psum[6 + r % 2]
                        for n in range(NT):
                            nc.tensor.matmul(b[:, n * P:(n + 1) * P], lla[:, r, n, :], cst[:, K_U:K_U + P], start=(n == 0), stop=False, skip_group_check=True)
                        nc.tensor.matmul(b[:, :], identb[:, :], negb[:, :, :].rearrange("p n c -> p (n c)"), start=False, stop=True,
                                         skip_group_check=True).then_inc(q_["dec_psum"], 1)

                    def body(i, more):
                        for j in range(3):
                            pe.wait_ge(q_["fm_done"], i * 4 + (j + 1))
                            for n in range(NT):
                                ins = nc.tensor.transpose(psum[2 + j][:, n * P:(n + 1) * P], fm[:, j, n * P:(n + 1) * P], ident)
                            ins.then_inc(q_["tok_psum"], 1)
                        pe.wait_ge(q_["yw"], i * 7 + 7)
                        decays(i, 0)
                        decays(i, 1)
                        g.pair_tokens3(pe, 4, 0, i, hi4[:, 0:2], xsplit, xlo)
                        pe.wait_ge(q_["fm_done"], i * 4 + 4)
                        for n in range(NT):
                            c = slice(n * P, (n + 1) * P)
                            ins = nc.tensor.matmul(psum[5][:, c], fm[:, 2, c], fm[:, 3, c], start=True, stop=True)
                        ins.then_inc(q_["score_psum"], 1)
                        decays(i, 2)
                        decays(i, 3)
                        pe.wait_ge(q_["tok_done"], i * 3 + 3)
                        pe.wait_ge(q_["vk_done"], i + 1)
                        for n in range(NT - 1):
                            bank, c0 = psum[2 + n // 2], (n % 2) * 256
                            ins = nc.tensor.matmul(bank[:, c0:c0 + 256], bt[:, n, :], vk[:, n, :], start=True, stop=True)
                        ins.then_inc(q_["kv_psum"], 1)
                        g.pair_tokens3(pe, 4, 1, i, hi4[:, 0:2], xsplit, xlo)
                        pe.wait_ge(q_["m_done"], i * 4 + 4)
                        for n in range(NT):
                            for r in range(SR):
                                c0 = (n % 2) * 256 + r * 64
                                ins = nc.tensor.matmul(psum[6 + n // 2][:, c0:c0 + 64], M[:, r, n * P:(n + 1) * P], v[:, n, r * 64:(r + 1) * 64], start=True, stop=True)
                        ins.then_inc(q_["y_psum"], 1)
                        pe.wait_ge(q_["state"], i * 3 + 3)
                        for n in range(1, NT):
                            c0 = (n % 2) * 256
                            ins = nc.tensor.matmul(psum[4 + n // 2][:, c0:c0 + 256], fm[:, 3, n * P:(n + 1) * P], St[:, n - 1, :], start=True, stop=True)
                        ins.then_inc(q_["y_psum"], 1)
                        if more:
                            for j in range(3):
                                g.features3(pe, j, i + 1, hi, xsplit, xlo)
                        pe.wait_ge(q_["on_ready"], i + 1)
                        for a in range(2):
                            for n in range(NT):
                                ins = nc.tensor.transpose(psum[2 + a][:, n * P:(n + 1) * P], vk[:, n, a * P:(a + 1) * P], ident)
                            ins.then_inc(q_["oT_psum"], 1)
                        if more:
                            for j in range(3, 4):
                                g.features3(pe, j, i + 1, hi, xsplit, xlo)
                        pe.wait_ge(q_["y_done"], i * 2 + 2)

                    for j in range(4):
                        g.features3(pe, j, 0, hi, xsplit, xlo)
                    in_turns(pe, SG, body)

                @block.scalar
                def _(act):
                    def conv(j, i):
                        ch = (i * 2, i * 2 + 1, i + 8, i + 12)[j]
                        g.wait_ready(act, j, i)
                        nc.scalar.activation(acc[:, j, :], psum[j % 2][:, :], ACT.Identity, scale=cw_s[:, 3, ds(ch, 1)], bias=cb_s[:, ds(ch, 1)]).then_inc(q_["conv_acc"], 1)
                        if j >= 2:
                            g.split_hi(act, j + 2, i, hi)
                        g.wait_read(act, j, i)
                        nc.scalar.activation(th[:, j, :], acc[:, j, :], ACT.Tanh).then_inc(q_["conv_th"], 1)

                    def body(i, more):
                        for j, dst in enumerate((xs[:, :, 0, :], xs[:, :, 1, :], bt[:, :, :])):
                            act.wait_ge(q_["tok_psum"], i * 3 + (j + 1))
                            nc.scalar.activation(dst, v3(psum[2 + j][:, :]), ACT.Copy).then_inc(q_["tok_done"], 1)
                        for r in range(SR):
                            act.wait_ge(q_["dec_psum"], i * 4 + (r + 1))
                            nc.scalar.activation(dec[:, r, :], psum[6 + r % 2][:, :], ACT.Exp).then_inc(q_["dec_ready"], 1)
                        if more:
                            for j in range(2):
                                g.split_hi(act, j, i + 1, hi)
                        for a in range(2):
                            g.wait_ready(act, 4 + a, i)
                            nc.scalar.activation(zh[:, 2 * a:2 * a + 2].rearrange("p n a c -> p (n a c)"), psum[a][:, :], ACT.Copy, scale=0.5).then_inc(q_["zh_done"], 1)
                            nc.scalar.activation(zt[:, 2 * a:2 * a + 2].rearrange("p n a c -> p (n a c)"), psum[a][:, :], ACT.Tanh, scale=0.5).then_inc(g_free[a], 1)
                        if more:
                            g.split_hi(act, 2, i + 1, hi)
                            g.split_hi(act, 3, i + 1, hi)
                            conv(0, i + 1)
                        act.wait_ge(q_["yw"], i * 7 + 14)
                        nc.scalar.activation(v[:, :, :], y[:, :, :], ACT.Square).then_inc(q_["sq_done"], 1)
                        if more:
                            conv(1, i + 1)
                        for a in range(2):
                            act.wait_ge(q_["oT_psum"], i * 2 + (a + 1))
                            nc.scalar.activation(yT[:, 1, ds(i * 2 + a, 1), :].rearrange("p a c -> p (a c)"), psum[2 + a][:, :], ACT.Copy,
                                                 scale=nw_s[:, ds(i * 2 + a, 1)]).then_inc(q_["y_done"], 1)
                        if more:
                            conv(2, i + 1)
                            conv(3, i + 1)

                    for j in range(4):
                        g.split_hi(act, j, 0, hi)
                    for j in range(4):
                        conv(j, 0)
                    in_turns(act, SG, body)

                @block.gpsimd
                def _(pool):
                    def log_decays(i):
                        for r in range(SR):
                            nc.gpsimd.tensor_tensor(lla[:, r], cst[:, K_L:K_L + P].unsqueeze(1).to_broadcast([P, NT, P]),
                                                    la[:, :, ds(i * 4 + (8 + r), 1)].to_broadcast([P, NT, P]), ALU.mult).then_inc(q_["lla_ready"], 1)

                    def body(i, more):
                        if more:
                            for j in range(2):
                                g.split_lo(pool, nc.gpsimd, j, i + 1, hi)
                            pool.wait_ge(q_["dec_psum"], i * 4 + 4)
                            log_decays(i + 1)
                            for j in range(2, 4):
                                g.split_lo(pool, nc.gpsimd, j, i + 1, hi)
                        pool.wait_ge(q_["rs_in"], i + 1)
                        nc.gpsimd.tensor_tensor(rs[:, :], ssq[:, :], half[:, 0:NT], ALU.pow).then_inc(q_["rs_out"], 1)
                        if more:
                            for j in (4, 5):
                                g.split_lo(pool, nc.gpsimd, j, i + 1, hi)

                    log_decays(0)
                    in_turns(pool, SG, body)

                def heads(ap):
                    return ap.unsqueeze(3).to_broadcast([P, ap.shape[1], 4, 64])

                def r4(ap):
                    return ap.rearrange("p n (r c) -> p n r c", r=4)

                @block.vector
                def _(dve):
                    def conv(j, i):
                        ch = (i * 2, i * 2 + 1, i + 8, i + 12)[j]
                        dve.wait_ge(q_["conv_acc"], i * 4 + (j + 1))
                        p = psum[j % 2]
                        for m in (1, 2):
                            nc.vector.scalar_tensor_tensor(out=acc[:, j, m:S], in0=p[:, 0:S - m], scalar=cw_s[:, 3 - m, ds(ch, 1)],
                                                           in1=acc[:, j, m:S], op0=ALU.mult, op1=ALU.add).then_inc(q_["conv_fm"], 1)
                            dve.wait_ge(q_["conv_fm"], i * 8 + (2 * j + m))
                        nc.vector.scalar_tensor_tensor(out=acc[:, j, 3:S], in0=p[:, 0:S - 3], scalar=cw_s[:, 0, ds(ch, 1)],
                                                       in1=acc[:, j, 3:S], op0=ALU.mult, op1=ALU.add).then_inc(g_free[j % 2], 1)

                    def silu(j, i):
                        dve.wait_ge(q_["conv_th"], i * 4 + (j + 1))
                        nc.vector.scalar_tensor_tensor(out=fm[:, j, :], in0=th[:, j, :], scalar=1.0, in1=acc[:, j, :], op0=ALU.add, op1=ALU.mult).then_inc(q_["fm_done"], 1)

                    def body(i, more):
                        link = Count(dve, q_["cv"], 5, i)
                        dve.wait_ge(q_["tok_done"], i * 3 + 3)
                        xs4 = xs[:, :, :, :].rearrange("p n a (b c) -> p n (a b) c", b=2)
                        nc.vector.tensor_tensor(r4(v[:, :, :]), xs4, heads(sp[:, :, ds(i * 4 + 8, 4)]), ALU.mult).then_inc(q_["v_done"], 1)
                        dve.wait_ge(q_["v_done"], i + 1)
                        nc.vector.tensor_tensor(r4(vk[:, :, :]), r4(v[:, :, :]), heads(ekw[:, :, ds(i * 4 + 8, 4)]), ALU.mult).then_inc(q_["vk_done"], 1)
                        dve.wait_ge(q_["score_psum"], i + 1)
                        for r in range(SR):
                            dve.wait_ge(q_["dec_ready"], i * 4 + (r + 1))
                            nc.vector.tensor_tensor(M[:, r, :], psum[5][:, :], dec[:, r, :], ALU.mult).then_inc(q_["m_done"], 1)
                        dve.wait_ge(q_["kv_psum"], i + 1)
                        for n in range(NT - 1):
                            kv = psum[2 + n // 2][:, (n % 2) * 256:(n % 2) * 256 + 256]
                            if n == 0:
                                nc.vector.tensor_copy(St[:, 0, :], kv).then_inc(q_["state"], 1)
                            else:
                                dve.wait_ge(q_["state"], i * 3 + n)
                                link(nc.vector.tensor_tensor(ts[:, n - 1, :].rearrange("p (r c) -> p r c", r=4), St[:, n - 1, :].rearrange("p (r c) -> p r c", r=4),
                                                             etot[:, n, ds(i * 4 + 8, 4)].unsqueeze(2).to_broadcast([P, 4, 64]), ALU.mult))
                                nc.vector.tensor_tensor(St[:, n, :], ts[:, n - 1, :], kv, ALU.add).then_inc(q_["state"], 1)
                        link(nc.vector.tensor_tensor(r4(y[:, :, :]), xs4, heads(par[:, ds(i * 4 + 48, 4)].unsqueeze(1).to_broadcast([P, NT, 4])), ALU.mult))
                        for a in range(2):
                            g.wait_read(dve, 4 + a, i)
                        link(nc.vector.scalar_tensor_tensor(out=sz[:, :, :, :].rearrange("p n a c -> p (n a c)"), in0=zt[:, :, :, :].rearrange("p n a c -> p (n a c)"),
                                                            scalar=1.0, in1=zh[:, :, :, :].rearrange("p n a c -> p (n a c)"), op0=ALU.add, op1=ALU.mult))
                        dve.wait_ge(q_["y_psum"], i * 2 + 2)
                        for b in range(2):
                            nc.vector.tensor_tensor(y[:, 2 * b:2 * b + 2, :].rearrange("p n c -> p (n c)"), y[:, 2 * b:2 * b + 2, :].rearrange("p n c -> p (n c)"),
                                                    psum[6 + b][:, :], ALU.add).then_inc(q_["yw"], 1)
                        for n in range(1, NT):
                            nc.vector.tensor_tensor(yi[:, n - 1, :].rearrange("p (r c) -> p r c", r=4), psum[4 + n // 2][:, (n % 2) * 256:(n % 2) * 256 + 256].rearrange("p (r c) -> p r c", r=4),
                                                    ecum[:, n, ds(i * 4 + 8, 4)].unsqueeze(2).to_broadcast([P, 4, 64]), ALU.mult).then_inc(q_["yw"], 1)
                        dve.wait_ge(q_["yw"], i * 7 + 12)
                        nc.vector.tensor_tensor(y[:, 1:NT, :], y[:, 1:NT, :], yi[:, :, :], ALU.add).then_inc(q_["yw"], 1)
                        dve.wait_ge(q_["yw"], i * 7 + 13)
                        nc.vector.tensor_tensor(y[:, :, :], y[:, :, :], sz[:, :, :, :].rearrange("p n a c -> p n (a c)"), ALU.mult).then_inc(q_["yw"], 1)
                        if more:
                            conv(0, i + 1)
                        dve.wait_ge(q_["sq_done"], i + 1)
                        link(nc.vector.tensor_reduce(ssq[:, :], v[:, :, :], AX.X, ALU.add))
                        nc.vector.tensor_scalar(ssq[:, :], ssq[:, :], 1.0 / 256, RMS_EPS, ALU.mult, ALU.add).then_inc(q_["rs_in"], 1)
                        if more:
                            silu(0, i + 1)
                        dve.wait_ge(q_["rs_out"], i + 1)
                        nc.vector.tensor_tensor(vk[:, :, :], y[:, :, :], rs[:, :].unsqueeze(2).to_broadcast([P, NT, 256]), ALU.mult).then_inc(q_["on_ready"], 1)
                        if more:
                            for j in range(1, 4):
                                conv(j, i + 1)
                                silu(j, i + 1)
                        link.done()

                    dve.sem_inc(q_["yw"], 7)
                    for j in range(4):
                        g.split_lo(dve, nc.vector, j, 0, hi)
                    for j in range(4):
                        conv(j, 0)
                        silu(j, 0)
                    for j in (4, 5):
                        g.split_lo(dve, nc.vector, j, 0, hi)
                    in_turns(dve, SG, body)

        end_phase()
        xhi = mid.enter_context(nc.sbuf_tensor("xhi", [P, KT, S], f32r))
        with ExitStack() as c2:
            def b2(name, shape, dt=f32):
                return c2.enter_context(nc.sbuf_tensor("g_" + name, shape, dt))

            acc, th = b2("acc", [P, 4, S]), b2("th", [P, 4, S])
            fm = b2("fm", [P, 3, S])
            sz = th[:, 3, :]
            sq = b2("sq", [P, 2, NT, P])
            ssq, rs = b2("ssq", [P, 12]), b2("rs", [P, 12])
            kn, kb, kbe, kd = [b2(n_, [P, NT, P]) for n_ in ("kn", "kb", "kbe", "kd")]
            qn, qd, vb = [b2(n_, [P, NT, P]) for n_ in ("qn", "qd", "vb")]
            knT, kbT, qnT, qdT = [b2(n_, [P, S]) for n_ in ("knT", "kbT", "qnT", "qdT")]
            lla, dec = b2("lla", [P, NT, P]), b2("dec", [P, S])
            AT, atT = b2("AT", [P, S]), b2("atT", [P, S])
            Cl = b2("Cl", [P, LEVELS - 1, S])
            T, X, vn, on = [x_[:, :, :].rearrange("p n c -> p (n c)") for x_ in (qd, kb, kn, qn)]
            TT, nwT = b2("TT", [P, S]), kbT
            hi = [ringlo[:, 4], ringlo[:, 5], ringlo[:, 4], ringlo[:, 5]]
            St = b2("St", [P, 3, P])

            names = ("conv_acc conv_th conv_fm fm_done tok_psum tok_norm rs_in rs_out tokT_psum tokT_done lla_ready dec_psum dec_ready "
                     "score_psum score_done cl_ready t0_psum lev_x_psum lev_x lev_y_psum lev_t wT_psum wT_ready vn_psum vn_ready kv_psum state "
                     "z_acc lev_tt x0 o_psum on_ready oT_psum y_done x_moved tok_sq g_dve g_lv").split()
            q_ = {n_: sem("g_" + n_) for n_ in names}
            g = gdn_g

            with nc.Block() as block:
                @block.sync
                def _(sp_):
                    in_turns(sp_, GH, lambda i, more: [g.load_next(sp_, j, i) for j in range(4)] if more else None)
                    for j in range(4):
                        g.wait_used(sp_, j, GH - 1)
                        mrg_g[0].load_first(sp_, j)

                @block.tensor
                def _(pe):
                    def four(dst, lhs, rhs):
                        for n in range(NT):
                            c = slice(n * P, (n + 1) * P)
                            ins = nc.tensor.matmul(dst[:, c], lhs[:, c], rhs[:, c], start=True, stop=True)
                        return ins

                    def turned(bank, src):
                        for n in range(NT):
                            ins = nc.tensor.transpose(bank[:, n * P:(n + 1) * P], src(n), ident)
                        return ins

                    def body(i, more):
                        def ahead(j, k0, k1):
                            if more:
                                g.features3(pe, j, i + 1, hi, xhi, xlo, k0=k0, k1=k1)

                        def token_major(j):
                            pe.wait_ge(q_["fm_done"], i * 4 + (j + 1))
                            turned(psum[2 + j], lambda n: fm[:, j, n * P:(n + 1) * P]).then_inc(q_["tok_psum"], 1)

                        token_major(1)
                        pe.wait_ge(q_["lla_ready"], i + 1)
                        for n in range(NT):
                            nc.tensor.matmul(psum[5][:, n * P:(n + 1) * P], lla[:, n, :], cst[:, K_U:K_U + P], start=(n == 0), stop=False, skip_group_check=True)
                        nc.tensor.matmul(psum[5][:, :], identb[:, :], negb[:, :, :].rearrange("p n c -> p (n c)"), start=False, stop=True,
                                         skip_group_check=True).then_inc(q_["dec_psum"], 1)
                        pe.wait_ge(q_["y_done"], i + 1)
                        token_major(0)
                        g.features3(pe, 3, i, hi, xhi, xlo)
                        token_major(2)
                        pe.wait_ge(q_["on_ready"], i + 1)
                        for j, src in enumerate((kn, kb, qn, qd)):
                            pe.wait_ge(q_["tok_norm"], i * 7 + (1, 2, 4, 5)[j])
                            turned(psum[(6, 7, 2, 3)[j]], lambda n: src[:, n, :]).then_inc(q_["tokT_psum"], 1)
                        ahead(0, 0, 2)
                        pe.wait_ge(q_["tokT_done"], i * 4 + 2)
                        four(psum[6], knT, kbT).then_inc(q_["score_psum"], 1)
                        ahead(0, 2, 3)
                        pe.wait_ge(q_["tokT_done"], i * 4 + 4)
                        four(psum[7], knT, qnT).then_inc(q_["score_psum"], 1)
                        ahead(0, 3, 6)
                        pe.wait_ge(q_["lev_tt"], i * 7 + 1)
                        turned(psum[4], lambda n: TT[:, n * P:(n + 1) * P]).then_inc(q_["t0_psum"], 1)
                        ahead(0, 6, 8)
                        for l in range(1, LEVELS):
                            pe.wait_ge(q_["cl_ready"], i * 6 + l)
                            pe.wait_ge(q_["lev_t"], i * 6 + l)
                            four(psum[5], Cl[:, l - 1], T).then_inc(q_["lev_x_psum"], 1)
                            ahead(1, l - 1, l)
                            pe.wait_ge(q_["lev_x"], i * 6 + l)
                            pe.wait_ge(q_["lev_tt"], i * 7 + l)
                            if l < LEVELS - 1:
                                four(psum[7], TT, X).then_inc(q_["lev_y_psum"], 1)
                            four(psum[6], X, TT).then_inc(q_["lev_y_psum"], 1)
                        ahead(1, 6, 8)
                        pe.wait_ge(q_["lev_tt"], i * 7 + 7)
                        for n in range(NT):
                            c = slice(n * P, (n + 1) * P)
                            ins = nc.tensor.matmul(psum[4][:, c], kbe[:, n, :], TT[:, c], start=True, stop=True)
                        ins.then_inc(q_["wT_psum"], 1)
                        pe.wait_ge(q_["score_done"], i * 2 + 2)
                        for n in range(NT):
                            c = slice(n * P, (n + 1) * P)
                            ins = nc.tensor.matmul(psum[5][:, c], TT[:, c], vb[:, n, :], start=True, stop=(n == 0))
                            if n:
                                pe.wait_ge(q_["wT_ready"], i + 1)
                                pe.wait_ge(q_["state"], i * 3 + n)
                                ins = nc.tensor.matmul(psum[5][:, c], nwT[:, c], St[:, n - 1, :], start=False, stop=True)
                            ins.then_inc(q_["vn_psum"], 1)
                            ahead(2, n, n + 1)
                            pe.wait_ge(q_["vn_ready"], i * 4 + (n + 1))
                            if n < NT - 1:
                                nc.tensor.matmul(psum[6][:, c], kd[:, n, :], vn[:, c], start=True, stop=True).then_inc(q_["kv_psum"], 1)
                            if n:
                                nc.tensor.matmul(psum[7][:, c], qdT[:, c], St[:, n - 1, :], start=True, stop=False)
                            ins = nc.tensor.matmul(psum[7][:, c], atT[:, c], vn[:, c], start=(n == 0), stop=True)
                        ins.then_inc(q_["o_psum"], 1)
                        ahead(2, 4, 8)
                        pe.wait_ge(q_["on_ready"], i + 2)
                        turned(psum[2], lambda n: on[:, n * P:(n + 1) * P]).then_inc(q_["oT_psum"], 1)

                    for j in range(3):
                        g.features3(pe, j, 0, hi, xhi, xlo, rhs_split=(lambda k: pe.wait_ge(q_["x_moved"], k + 1)) if j == 0 else None)
                    in_turns(pe, GH, body)

                @block.scalar
                def _(act):
                    def tap(j, i):
                        g.wait_ready(act, j, i)
                        nc.scalar.activation(acc[:, j, :], psum[j % 2][:, :], ACT.Copy, scale=cw_g[:, 3, ds(i + 8 * j, 1)]).then_inc(q_["conv_acc"], 1)

                    def tanh(j, i):
                        g.wait_read(act, j, i)
                        nc.scalar.activation(th[:, j, :], acc[:, j, :], ACT.Tanh).then_inc(q_["conv_th"], 1)

                    def body(i, more):
                        for j in (1, 0):
                            act.wait_ge(q_["tok_psum"], i * 3 + (2 - j))
                            nc.scalar.activation(sq[:, j], v3(psum[2 + j][:, :]), ACT.Square).then_inc(q_["tok_sq"], 1)
                        g.wait_ready(act, 3, i)
                        act.wait_ge(q_["y_done"], i + 1)
                        nc.scalar.activation(acc[:, 3, :], psum[1][:, :], ACT.Copy, scale=0.5).then_inc(q_["z_acc"], 1)
                        nc.scalar.activation(th[:, 3, :], psum[1][:, :], ACT.Tanh, scale=0.5).then_inc(g_free[1], 1)
                        if more:
                            for j in range(2):
                                g.split_hi(act, j, i + 1, hi)
                        act.wait_ge(q_["dec_psum"], i + 1)
                        nc.scalar.activation(dec[:, :], psum[5][:, :], ACT.Exp).then_inc(q_["dec_ready"], 1)
                        for j, (dst, b) in enumerate(((knT, 6), (kbT, 7), (qnT, 2), (qdT, 3))):
                            act.wait_ge(q_["tokT_psum"], i * 4 + (j + 1))
                            nc.scalar.activation(dst[:, :], psum[b][:, :], ACT.Copy).then_inc(q_["tokT_done"], 1)
                        for l in range(1, LEVELS):
                            act.wait_ge(q_["lev_x_psum"], i * 6 + l)
                            nc.scalar.activation(X[:, :], psum[5][:, :], ACT.Copy).then_inc(q_["lev_x"], 1)
                            if more and l == 1:
                                tap(0, i + 1)
                            if more and l == 3:
                                g.split_hi(act, 2, i + 1, hi)
                            if more and l == 5:
                                tanh(0, i + 1)
                        act.wait_ge(q_["wT_psum"], i + 1)
                        nc.scalar.activation(nwT[:, :], psum[4][:, :], ACT.Copy, scale=-1.0).then_inc(q_["wT_ready"], 1)
                        for n in range(NT):
                            c = slice(n * P, (n + 1) * P)
                            act.wait_ge(q_["vn_psum"], i * 4 + (n + 1))
                            nc.scalar.activation(vn[:, c], psum[5][:, c], ACT.Copy).then_inc(q_["vn_ready"], 1)
                            if more and n == 0:
                                tap(1, i + 1)
                            if more and n == 3:
                                tanh(1, i + 1)
                        act.wait_ge(q_["o_psum"], i + 1)
                        nc.scalar.activation(sq[:, 0], v3(psum[7][:, :]), ACT.Square).then_inc(q_["tok_sq"], 1)
                        if more:
                            g.split_hi(act, 3, i + 1, hi)
                            tap(2, i + 1)
                            tanh(2, i + 1)

                    for j in range(2):
                        g.split_hi(act, j, 0, hi)
                    for k in range(KT):
                        nc.scalar.activation(xhi[:, k, :], xsplit[:, k, :], ACT.Copy).then_inc(q_["x_moved"], 1)
                    for j in range(3):
                        tap(j, 0)
                        if j < 2:
                            g.split_hi(act, j + 2, 0, hi)
                        tanh(j, 0)
                    in_turns(act, GH, body)

                @block.gpsimd
                def _(pool):
                    def log_decays(i):
                        nc.gpsimd.tensor_tensor(lla[:, :, :], cst[:, K_L:K_L + P].unsqueeze(1).to_broadcast([P, NT, P]),
                                                la[:, :, ds(i, 1)].to_broadcast([P, NT, P]), ALU.mult).then_inc(q_["lla_ready"], 1)

                    def body(i, more):
                        pool.wait_ge(q_["rs_in"], i * 2 + 1)
                        nc.gpsimd.tensor_tensor(rs[:, 0:8], ssq[:, 0:8], half[:, 0:8], ALU.pow).then_inc(q_["rs_out"], 1)
                        if more:
                            for j in range(2):
                                g.split_lo(pool, nc.gpsimd, j, i + 1, hi)
                        pool.wait_ge(q_["score_done"], i * 2 + 1)
                        for l in range(1, LEVELS):
                            nc.gpsimd.tensor_tensor(v3(Cl[:, l - 1, :]), v3(AT[:, :]), cst[:, K_MASK + l * P:K_MASK + (l + 1) * P].unsqueeze(1).to_broadcast([P, NT, P]),
                                                    ALU.mult).then_inc(q_["cl_ready"], 1)
                        if more:
                            log_decays(i + 1)
                            g.split_lo(pool, nc.gpsimd, 2, i + 1, hi)
                        pool.wait_ge(q_["rs_in"], i * 2 + 2)
                        nc.gpsimd.tensor_tensor(rs[:, 8:12], ssq[:, 8:12], half[:, 0:4], ALU.pow).then_inc(q_["rs_out"], 1)
                        if more:
                            g.split_lo(pool, nc.gpsimd, 3, i + 1, hi)

                    log_decays(0)
                    in_turns(pool, GH, body)

                @block.vector
                def _(dve):
                    def tap(j, i, m):
                        if m == 1:
                            dve.wait_ge(q_["conv_acc"], i * 3 + (j + 1))
                        ins = nc.vector.scalar_tensor_tensor(out=acc[:, j, m:S], in0=psum[j % 2][:, 0:S - m], scalar=cw_g[:, 3 - m, ds(i + 8 * j, 1)],
                                                             in1=acc[:, j, m:S], op0=ALU.mult, op1=ALU.add)
                        if m < 3:
                            ins.then_inc(q_["conv_fm"], 1)
                            dve.wait_ge(q_["conv_fm"], i * 6 + (2 * j + m))
                        else:
                            ins.then_inc(g_free[j % 2], 1)

                    def silu(j, i):
                        if j < 3:
                            dve.wait_ge(q_["conv_th"], i * 3 + (j + 1))
                        else:
                            g.wait_read(dve, 3, i)
                        nc.vector.scalar_tensor_tensor(out=fm[:, j, :] if j < 3 else sz, in0=th[:, j, :], scalar=1.0, in1=acc[:, j, :], op0=ALU.add, op1=ALU.mult).then_inc(q_["fm_done"], 1)

                    def body(i, more):
                        link = Count(dve, q_["g_dve"], 3, i)
                        dve.wait_ge(q_["tok_sq"], i * 3 + 2)
                        link(nc.vector.tensor_reduce(ssq[:, 0:8], sq[:, 0:2].rearrange("p a n c -> p (a n) c"), AX.X, ALU.add))
                        link(nc.vector.tensor_scalar(ssq[:, 0:4], ssq[:, 0:4], RMS_EPS, float(P), ALU.add, ALU.mult))
                        nc.vector.tensor_scalar(ssq[:, 4:8], ssq[:, 4:8], RMS_EPS, None, ALU.add).then_inc(q_["rs_in"], 1)
                        dve.wait_ge(q_["tok_psum"], i * 3 + 3)

                        def by(dst, src, scale, w):
                            nc.vector.tensor_tensor(dst[:, :, :], src, scale.to_broadcast([P, NT, P]), ALU.mult).then_inc(q_["tok_norm"], 1)

                        dve.wait_ge(q_["rs_out"], i * 2 + 1)
                        by(kn, v3(psum[3][:, :]), rs[:, 4:8].unsqueeze(2), 1)
                        dve.wait_ge(q_["tok_norm"], i * 7 + 1)
                        by(kb, kn[:, :, :], beta[:, :, ds(i, 1)], 2)
                        by(vb, v3(psum[4][:, :]), beta[:, :, ds(i, 1)], 3)
                        by(qn, v3(psum[2][:, :]), rs[:, 0:4].unsqueeze(2), 4)
                        dve.wait_ge(q_["tok_norm"], i * 7 + 4)
                        by(qd, qn[:, :, :], ecum[:, :, ds(i, 1)], 5)
                        by(kbe, kn[:, :, :], becum[:, :, ds(i, 1)], 6)
                        by(kd, kn[:, :, :], ekw[:, :, ds(i, 1)], 7)
                        silu(3, i)
                        dve.wait_ge(q_["dec_ready"], i + 1)
                        dve.wait_ge(q_["score_psum"], i * 2 + 1)
                        nc.vector.tensor_tensor(AT[:, :], psum[6][:, :], dec[:, :], ALU.mult).then_inc(q_["score_done"], 1)
                        dve.wait_ge(q_["score_done"], i * 2 + 1)
                        nc.vector.tensor_tensor(v3(X[:, :]), v3(AT[:, :]), cst[:, K_MASK:K_MASK + P].unsqueeze(1).to_broadcast([P, NT, P]), ALU.mult).then_inc(q_["x0"], 1)
                        dve.wait_ge(q_["x0"], i + 1)
                        nc.vector.tensor_tensor(v3(TT[:, :]), ident.unsqueeze(1).to_broadcast([P, NT, P]), v3(X[:, :]), ALU.subtract).then_inc(q_["lev_tt"], 1)
                        dve.wait_ge(q_["score_psum"], i * 2 + 2)
                        nc.vector.tensor_tensor(atT[:, :], psum[7][:, :], dec[:, :], ALU.mult).then_inc(q_["score_done"], 1)
                        dve.wait_ge(q_["t0_psum"], i + 1)
                        nc.vector.tensor_copy(T[:, :], psum[4][:, :]).then_inc(q_["lev_t"], 1)
                        for l in range(1, LEVELS):
                            if l < LEVELS - 1:
                                dve.wait_ge(q_["lev_y_psum"], i * 11 + (2 * l - 1))
                                dve.wait_ge(q_["lev_t"], i * 6 + l)
                                nc.vector.tensor_tensor(T[:, :], T[:, :], psum[7][:, :], ALU.subtract).then_inc(q_["lev_t"], 1)
                            dve.wait_ge(q_["lev_y_psum"], i * 11 + min(2 * l, 11))
                            dve.wait_ge(q_["lev_tt"], i * 7 + l)
                            nc.vector.tensor_tensor(TT[:, :], TT[:, :], psum[6][:, :], ALU.subtract).then_inc(q_["lev_tt"], 1)
                            if more and l in (2, 3, 4):
                                tap(0, i + 1, l - 1)
                        if more:
                            silu(0, i + 1)
                        for n in range(NT - 1):
                            c = slice(n * P, (n + 1) * P)
                            dve.wait_ge(q_["kv_psum"], i * 3 + (n + 1))
                            if n == 0:
                                nc.vector.tensor_copy(St[:, 0, :], psum[6][:, c]).then_inc(q_["state"], 1)
                            else:
                                dve.wait_ge(q_["state"], i * 3 + n)
                                nc.vector.scalar_tensor_tensor(out=St[:, n, :], in0=St[:, n - 1, :], scalar=etot[:, n, ds(i, 1)], in1=psum[6][:, c],
                                                               op0=ALU.mult, op1=ALU.add).then_inc(q_["state"], 1)
                            if more:
                                tap(1, i + 1, n + 1)
                        if more:
                            silu(1, i + 1)
                        dve.wait_ge(q_["tok_sq"], i * 3 + 3)
                        link(nc.vector.tensor_reduce(ssq[:, 8:12], sq[:, 0], AX.X, ALU.add))
                        nc.vector.tensor_scalar(ssq[:, 8:12], ssq[:, 8:12], 1.0 / P, RMS_EPS, ALU.mult, ALU.add).then_inc(q_["rs_in"], 1)
                        dve.wait_ge(q_["rs_out"], i * 2 + 2)
                        nc.vector.tensor_tensor(v3(on[:, :]), v3(psum[7][:, :]), rs[:, 8:12].unsqueeze(2).to_broadcast([P, NT, P]), ALU.mult).then_inc(q_["on_ready"], 1)
                        if more:
                            tap(2, i + 1, 1)
                        dve.wait_ge(q_["oT_psum"], i + 1)
                        nc.vector.scalar_tensor_tensor(out=yT[:, 0, ds(i, 1), :].rearrange("p a c -> p (a c)"), in0=psum[2][:, :], scalar=nw_g[:, 0:1], in1=sz,
                                                       op0=ALU.mult, op1=ALU.mult).then_inc(q_["y_done"], 1)
                        if more:
                            tap(2, i + 1, 2)
                            tap(2, i + 1, 3)
                            silu(2, i + 1)
                        link.done()

                    for free in ("on_ready", "y_done"):
                        dve.sem_inc(q_[free], 1)
                    for j in range(2):
                        g.split_lo(dve, nc.vector, j, 0, hi)
                    for j in range(3):
                        for m in (1, 2, 3):
                            tap(j, 0, m)
                            if m == 1 and j < 2:
                                g.split_lo(dve, nc.vector, j + 2, 0, hi)
                        silu(j, 0)
                    in_turns(dve, GH, body)

        end_phase()
        mT, mlo = pair(mid, "mT", [P, KT, S])
        wide = [pair(mid, "wide0", [P, KT, F])]

        def load_wide(sp_, w, h):
            sp_.dma_start(wide[h][0][:, :, :], w_cols(w, h * F, F)).then_inc(wide_in[h], 16)

        def load_rows(sp_, g_dram, b_dram):
            sp_.dma_start(rows[:, 0, :], g_dram).then_inc(rows_in, 16)
            sp_.dma_start(rows[:, 1, :], b_dram).then_inc(rows_in, 16)

        with ExitStack() as c2:
            def b2(name, shape, dt=f32):
                return c2.enter_context(nc.sbuf_tensor("m_" + name, shape, dt))

            yhi = b2("yhi", [P, 2, KT, S], f32r)
            gt, pr = b2("gt", [P, 2, S]), b2("pr", [P, S])
            hi = [ringlo[:, 4 + b] for b in range(2)]
            names = "y_hi y_lo pr_done m_done".split()
            q_ = {n_: sem("m_" + n_) for n_ in names}
            MT = KT // 2

            def tile_of(ap, k):
                return ap[:, ds(k, 1), :].rearrange("p a c -> p (a c)")

            def following(b, j, i, more):
                if j < 2:
                    return mrg_g[b], j + 2, i
                if more:
                    return mrg_g[b], j - 2, i + 1
                return (mrg_g[b + 1], j - 2, 0) if b < 2 else None

            with nc.Block() as block:
                @block.sync
                def _(sp_):
                    load_wide(sp_, t["mix_w_out"][0], 0)
                    for b in range(3):
                        in_turns(sp_, MT, lambda i, more: [mrg_g[b].load_next(sp_, j, i) for j in range(4)] if more else None)
                        for j in range(4):
                            mrg_g[b].wait_ready(sp_, j, MT - 1)
                            if b < 2:
                                mrg_g[b + 1].load_first(sp_, j)
                            else:
                                xa_g.load_first(sp_, j)
                    for j in range(4, 6):
                        xa_g.load_first(sp_, j)

                @block.tensor
                def _(pe):
                    for b in range(3):
                        g = mrg_g[b]

                        def body(i, first):
                            for j in range(4):
                                if j % 2 == 0:
                                    g.features3(pe, j, i, hi, xhi, xlo)
                                else:
                                    g.features3(pe, j, i, hi, yhi[:, b % 2], ylo[:, b], rhs_split=(lambda k: pe.wait_ge(q_["y_lo"], b * KT + k + 1)) if first and j == 1 else None)

                        body(0, True)
                        with pe.Fori(1, MT) as i:
                            body(i, False)

                @block.scalar
                def _(act):
                    def y_hi(b, k):
                        nc.scalar.activation(tile_of(yhi[:, b % 2], k), tile_of(yT[:, b], k), ACT.Copy).then_inc(q_["y_hi"], 1)

                    mrg_g[0].split_hi(act, 0, 0, hi)
                    mrg_g[0].split_hi(act, 1, 0, hi)
                    for k in range(KT):
                        y_hi(0, k)
                    for b in range(3):
                        g = mrg_g[b]

                        def body(i, more):
                            for j in range(4):
                                g.wait_ready(act, j, i)
                                if j % 2 == 0:
                                    nc.scalar.activation(gt[:, j // 2, :], psum[0][:, :], ACT.Tanh, scale=0.5).then_inc(g_free[0], 1)
                                nxt = following(b, j, i, more)
                                if nxt:
                                    nxt[0].split_hi(act, nxt[1], nxt[2], hi)
                                if b < 2 and j >= 2:
                                    y_hi(b + 1, i * 2 + (j - 2))

                        in_turns(act, MT, body)

                @block.vector
                def _(dve):
                    def y_lo(b, k):
                        dve.wait_ge(q_["y_hi"], k + (b * KT + 1))
                        nc.vector.tensor_tensor(tile_of(ylo[:, b], k), tile_of(yT[:, b], k), tile_of(yhi[:, b % 2], k).bitcast(f32), ALU.subtract).then_inc(q_["y_lo"], 1)

                    mrg_g[0].split_lo(dve, nc.vector, 0, 0, hi)
                    mrg_g[0].split_lo(dve, nc.vector, 1, 0, hi)
                    for k in range(KT):
                        y_lo(0, k)
                    for b in range(3):
                        g = mrg_g[b]

                        def body(i, more):
                            for j in range(4):
                                if j % 2:
                                    g.wait_ready(dve, j, i)
                                    g.wait_read(dve, j - 1, i)
                                    tile = mT[:, ds(i * 2 + j // 2, 1), :].rearrange("p a c -> p (a c)")
                                    nc.vector.scalar_tensor_tensor(out=pr[:, :] if b else tile, in0=gt[:, j // 2, :], scalar=1.0, in1=psum[1][:, :],
                                                                   op0=ALU.add, op1=ALU.mult).then_inc(g_free[1], 1)
                                    if b:
                                        g.wait_read(dve, j, i)
                                        nc.vector.tensor_tensor(tile, tile, pr[:, :], ALU.add).then_inc(q_["m_done"], 1)
                                        dve.wait_ge(q_["m_done"], i * 2 + ((b - 1) * KT + j // 2 + 1))
                                nxt = following(b, j, i, more)
                                if nxt:
                                    nxt[0].split_lo(dve, nc.vector, nxt[1], nxt[2], hi)
                                if b < 2 and j >= 2:
                                    y_lo(b + 1, i * 2 + (j - 2))

                        in_turns(dve, MT, body)

        wide.append(pair(mid, "wide1", [P, KT, F]))
        rows = mid.enter_context(nc.sbuf_tensor("rows", [P, 2, D], f32))

        def norm_rows(dve, stats, mv, var, rs, n, rs_in, rs_out, nsem, grow, brow, ready, done):
            for h in range(2):
                nc.vector.bn_stats(stats[:, n, h, :], xres[:, n, h * F:(h + 1) * F]).then_inc(nsem, 1)
            dve.wait_ge(nsem, n * 5 + 2)
            nc.vector.bn_aggr(mv[:, n, :], stats[:, n, :, :].rearrange("p h c -> p (h c)")).then_inc(nsem, 1)
            dve.wait_ge(nsem, n * 5 + 3)
            nc.vector.tensor_scalar(var[:, n:n + 1], mv[:, n, 1:2], LN_EPS, None, ALU.add).then_inc(rs_in, 1)
            dve.wait_ge(rs_out, n + 1)
            nc.vector.tensor_scalar(xres[:, n, :], xres[:, n, :], mv[:, n, 0:1], rs[:, n:n + 1], ALU.subtract, ALU.mult).then_inc(nsem, 1)
            dve.wait_ge(nsem, n * 5 + 4)
            nc.vector.tensor_tensor(xres[:, n, :], xres[:, n, :], grow, ALU.mult).then_inc(nsem, 1)
            dve.wait_ge(nsem, n * 5 + 5)
            nc.vector.tensor_tensor(xres[:, n, :], xres[:, n, :], brow, ALU.add).then_inc(done, 1)

        def dense_and_norm(tag, before, scale, split_x, sync_part):
            with ExitStack() as c2:
                def b2(name, shape, dt=f32):
                    return c2.enter_context(nc.sbuf_tensor(f"{tag}_{name}", shape, dt))

                stats, mv, var, rs = b2("stats", [P, NT, 2, 6]), b2("mv", [P, NT, 2]), b2("var", [P, NT]), b2("rs", [P, NT])
                ax, prod, z_done, nsem = sem(tag + "_alpha_x"), sem(tag + "_prod"), sem(tag + "_z_done"), sem(tag + "_norm")
                rs_in, rs_out, x_done, t_psum, t_hi, t_done = [sem(f"{tag}_{n_}") for n_ in ("rs_in", "rs_out", "x_done", "t_psum", "t_hi", "t_done")]
                m_hi, m_lo = sem(tag + "_m_hi"), sem(tag + "_m_lo")
                v_hi, v_lo = [[sem(f"{tag}_w_{n_}{h}") for h in range(2)] for n_ in ("hi", "lo")]
                mhi = ylo[:, 0]
                whi = [ylo[:, 1], ylo[:, 2]]
                with nc.Block() as block:
                    @block.sync
                    def _(sp_):
                        sync_part(sp_)

                    @block.tensor
                    def _(pe):
                        for n in range(NT):
                            for h in range(2):
                                u = 2 * n + h
                                if u >= 4:
                                    pe.wait_ge(z_done, u - 3)
                                for k in range(KT):
                                    if n == 0:
                                        pe.wait_ge(m_lo, k + 1)
                                        pe.wait_ge(v_lo[h], k + 1)
                                    c = slice(n * P, (n + 1) * P)
                                    for m, (a, b) in enumerate(((mhi, whi[h]), (mhi, wide[h][1]), (mlo, whi[h]))):
                                        ins = nc.tensor.matmul(psum[u % 4][:, :], a[:, k, c], b[:, k, :], start=(k + m == 0), stop=(k == KT - 1 and m == 2))
                                ins.then_inc(prod, 1)
                        for n in range(NT):
                            pe.wait_ge(x_done, n + 1)
                            for a in range(2):
                                u = 2 * n + a
                                if u >= 4:
                                    pe.wait_ge(t_done, u - 3)
                                for k in range(4):
                                    ins = nc.tensor.transpose(psum[4 + u % 4][:, k * P:(k + 1) * P], xres[:, n, (4 * a + k) * P:(4 * a + k + 1) * P], ident)
                                ins.then_inc(t_psum, 1)

                    @block.scalar
                    def _(act):
                        for h in range(2):
                            act.wait_ge(wide_in[h], before * 16 + 16)
                            for k in range(KT):
                                if h == 0:
                                    nc.scalar.activation(mhi[:, k, :], mT[:, k, :], ACT.Copy).then_inc(m_hi, 1)
                                nc.scalar.activation(whi[h][:, k, :], wide[h][0][:, k, :], ACT.Copy).then_inc(v_hi[h], 1)
                        for n in range(NT):
                            nc.scalar.activation(xres[:, n, :], xres[:, n, :], ACT.Copy, scale=ALPHA).then_inc(ax, 1)
                        for u in range(2 * NT):
                            n, a = u // 2, u % 2
                            act.wait_ge(t_psum, u + 1)
                            dst = xhi if split_x else xT
                            nc.scalar.activation(dst[:, 4 * a:4 * a + 4, n * P:(n + 1) * P], v3(psum[4 + u % 4][:, :]), ACT.Copy).then_inc(t_hi if split_x else t_done, 1)

                    @block.gpsimd
                    def _(pool):
                        for n in range(NT):
                            pool.wait_ge(rs_in, n + 1)
                            nc.gpsimd.tensor_tensor(rs[:, n:n + 1], var[:, n:n + 1], half[:, 0:1], ALU.pow).then_inc(rs_out, 1)

                    @block.vector
                    def _(dve):
                        for h in range(2):
                            for k in range(KT):
                                if h == 0:
                                    dve.wait_ge(m_hi, k + 1)
                                    nc.vector.tensor_tensor(mlo[:, k, :], mT[:, k, :], mhi[:, k, :].bitcast(f32), ALU.subtract).then_inc(m_lo, 1)
                                dve.wait_ge(v_hi[h], k + 1)
                                nc.vector.tensor_tensor(wide[h][1][:, k, :], wide[h][0][:, k, :], whi[h][:, k, :].bitcast(f32), ALU.subtract).then_inc(v_lo[h], 1)

                        def x_lo(n):
                            for u in (2 * n, 2 * n + 1):
                                dve.wait_ge(t_hi, u + 1)
                                at = (slice(None), slice(4 * (u % 2), 4 * (u % 2) + 4), slice(n * P, (n + 1) * P))
                                nc.vector.tensor_tensor(xlo[at], v3(psum[4 + u % 4][:, :]), xhi[at].bitcast(f32), ALU.subtract).then_inc(t_done, 1)

                        dve.wait_ge(rows_in, before * 32 + 32)
                        for n in range(NT):
                            dve.wait_ge(ax, n + 1)
                            for h in range(2):
                                u = 2 * n + h
                                dve.wait_ge(prod, u + 1)
                                c = slice(h * F, (h + 1) * F)
                                nc.vector.scalar_tensor_tensor(out=xres[:, n, c], in0=psum[u % 4][:, :], scalar=scale, in1=xres[:, n, c], op0=ALU.mult, op1=ALU.add).then_inc(z_done, 1)
                            dve.wait_ge(z_done, 2 * n + 2)
                            norm_rows(dve, stats, mv, var, rs, n, rs_in, rs_out, nsem, rows[:, 0, :], rows[:, 1, :], None, x_done)
                        if split_x:
                            for n in range(NT):
                                x_lo(n)

        end_phase()
        w_sets = [t["moe_w_gate"][0], t["moe_w_up"][0], t["moe_w_down"][0]]

        def part_view(w, part):
            return w if part < 2 else w.rearrange("p k s -> p (k s)").rearrange("p (k s) -> p k s", k=4)

        def load_expert(sp_, w, e, part, done):
            src = w_sets[part][ds(e, 1)].rearrange("a (k p) f -> p (a k) f", p=P)
            sp_.dma_start(part_view(w[:, part], part), src).then_inc(done, 16)

        mem_tok, mem_in = mid.enter_context(nc.sbuf_tensor("mem_tok", [P, 2, D], f32)), psem("mem_in")

        def load_mem(sp_):
            load_wide(sp_, t["mix_w_out"][0], 1)
            load_rows(sp_, t["ln_mix_g"], t["ln_mix_b"])
            for m in range(2):
                sp_.dma_start(mem_tok[:, m, :], t["mem"][0, m * P:(m + 1) * P, :]).then_inc(mem_in, 16)

        dense_and_norm("mix", 0, 0.5, True, load_mem)

        end_phase()
        with ExitStack() as c2:
            def b2(name, shape, dt=f32):
                return c2.enter_context(nc.sbuf_tensor("x_" + name, shape, dt))

            def tiles(a, n, c):
                return yT[:, 0, a:a + n * c // S, :].rearrange("p k s -> p (k s)").rearrange("p (k c) -> p k c", k=n)

            hi = [ylo[:, 1, 2 * b:2 * b + 2, :].rearrange("p k s -> p (k s)").rearrange("p (k c) -> p k c", k=KT) for b in range(2)]
            hi_v = ylo[:, 0, 0:4, :].rearrange("p a s -> p (a s)").rearrange("p (a k c) -> p a k c", a=2, k=KT)
            hi = hi + hi + [hi_v[:, b] for b in range(2)]
            memhi, memlo = [ylo[:, 2, 4 * b:4 * b + 4, :].rearrange("p k s -> p (k s)").rearrange("p (k c) -> p k c", k=KT) for b in range(2)]
            qT, kT, v = tiles(4, 2, S), tiles(6, 2, MEM), tiles(7, 4, P).rearrange("p (m c) f -> p m c f", m=2)
            mx, nb, sm_, ri = b2("mx", [P, NT]), b2("nb", [P, NT]), b2("sm", [P, NT]), b2("ri", [P, NT])
            pe_ = b2("pexp", [P, NT, MEM])
            pT = yT[:, 1, 4:6, :]
            names = ("mem_psum mem_hi mem_done q_done k_done v_done s_psum mx_done nb_done e_done ri_done pn_done pT_psum pT_done o_psum o_done").split()
            q_ = {n_: sem("x_" + n_) for n_ in names}
            g = xa_g
            SC = (D // XH) ** -0.5

            with nc.Block() as block:
                @block.sync
                def _(sp_):
                    for h in range(2):
                        load_wide(sp_, t["xa_w_o"][0], h)
                    load_rows(sp_, t["ln_xa_g"], t["ln_xa_b"])
                    in_turns(sp_, XH, lambda i, more: [g.load_next(sp_, j, i) for j in range(6)] if more else None)

                @block.tensor
                def _(pe):
                    def product(j, i):
                        if j < 4:
                            g.features3(pe, j, i, hi, (xhi, memhi)[j // 2], (xlo, memlo)[j // 2], cols=(S, MEM)[j // 2])
                        else:
                            g.pair_tokens3(pe, 4, j - 4, i, hi_v, memhi, memlo, tiles=1)

                    def body(i, more):
                        pe.wait_ge(q_["q_done"], i * 2 + 2)
                        pe.wait_ge(q_["k_done"], i * 2 + 2)
                        for n in range(NT):
                            for c in range(2):
                                ins = nc.tensor.matmul(psum[2 + n // 2][:, (n % 2) * MEM:(n % 2 + 1) * MEM], qT[:, c, n * P:(n + 1) * P], kT[:, c, :], start=(c == 0), stop=(c == 1))
                        ins.then_inc(q_["s_psum"], 1)
                        product(4, i)
                        product(5, i)
                        if more:
                            product(0, i + 1)
                        pe.wait_ge(q_["pn_done"], i + 1)
                        for m in range(2):
                            for n in range(NT):
                                ins = nc.tensor.transpose(psum[4 + m][:, n * P:(n + 1) * P], pe_[:, n, m * P:(m + 1) * P], ident)
                            ins.then_inc(q_["pT_psum"], 1)
                        if more:
                            product(1, i + 1)
                        pe.wait_ge(q_["pT_done"], i * 2 + 2)
                        pe.wait_ge(q_["v_done"], i * 2 + 2)
                        pe.wait_ge(q_["o_done"], i * 2 + 2)
                        for c in range(2):
                            for m in range(2):
                                ins = nc.tensor.matmul(psum[6 + c][:, :], v[:, m, c, :], pT[:, m, :], start=(m == 0), stop=(m == 1))
                            ins.then_inc(q_["o_psum"], 1)
                        if more:
                            product(2, i + 1)
                            product(3, i + 1)

                    product(0, 0)
                    pe.wait_ge(mem_in, 32)
                    for k2 in range(4):
                        for kk in range(2):
                            for m in range(2):
                                ins = nc.tensor.transpose(psum[2 + k2][:, (2 * kk + m) * P:(2 * kk + m + 1) * P], mem_tok[:, m, (2 * k2 + kk) * P:(2 * k2 + kk + 1) * P], ident)
                        ins.then_inc(q_["mem_psum"], 1)
                    for j in range(1, 4):
                        if j == 2:
                            pe.wait_ge(q_["mem_done"], 4)
                        product(j, 0)
                    in_turns(pe, XH, body)

                @block.scalar
                def _(act):
                    def take(j, i):
                        b = j % 2
                        key = ("q_done", "k_done", "v_done")[j // 2]
                        dst, src = ((qT[:, b, :], psum[b][:, :]), (kT[:, b, :], psum[b][:, 0:MEM]),
                                    (v[:, b], psum[b][:, 0:256].rearrange("p (c f) -> p c f", c=2)))[j // 2]
                        g.wait_ready(act, j, i)
                        nc.scalar.activation(dst, src, ACT.Copy).then_inc(g_free[b], 1)
                        g.wait_read(act, j, i)
                        act.sem_inc(q_[key], 1)

                    def body(i, more):
                        act.wait_ge(q_["nb_done"], i + 1)
                        for n in range(NT):
                            nc.scalar.activation(pe_[:, n, :], psum[2 + n // 2][:, (n % 2) * MEM:(n % 2 + 1) * MEM], ACT.Exp, bias=nb[:, n:n + 1], scale=SC,
                                                 accum_out=sm_[:, n:n + 1]).then_inc(q_["e_done"], 1)
                        if more:
                            g.split_hi(act, 0, i + 1, hi)
                            g.split_hi(act, 1, i + 1, hi)
                        take(4, i)
                        take(5, i)
                        if more:
                            take(0, i + 1)
                            g.split_hi(act, 2, i + 1, hi)
                        for m in range(2):
                            act.wait_ge(q_["pT_psum"], i * 2 + (m + 1))
                            nc.scalar.activation(pT[:, m, :], psum[4 + m][:, :], ACT.Copy).then_inc(q_["pT_done"], 1)
                        if more:
                            take(1, i + 1)
                            g.split_hi(act, 3, i + 1, hi)
                            for j in (4, 5):
                                g.split_hi(act, j, i + 1, hi)
                        for c in range(2):
                            act.wait_ge(q_["o_psum"], i * 2 + (c + 1))
                            nc.scalar.activation(mT[:, ds(i * 2 + c, 1), :].rearrange("p a c -> p (a c)"), psum[6 + c][:, :], ACT.Copy).then_inc(q_["o_done"], 1)
                        if more:
                            take(2, i + 1)
                            take(3, i + 1)

                    act.sem_inc(q_["o_done"], 2)
                    for j in range(2):
                        g.split_hi(act, j, 0, hi)
                    take(0, 0)
                    g.split_hi(act, 2, 0, hi)
                    for k2 in range(4):
                        act.wait_ge(q_["mem_psum"], k2 + 1)
                        nc.scalar.activation(memhi[:, 2 * k2:2 * k2 + 2, :].rearrange("p k m -> p (k m)"), psum[2 + k2][:, :], ACT.Copy).then_inc(q_["mem_hi"], 1)
                    take(1, 0)
                    g.split_hi(act, 3, 0, hi)
                    for j in (4, 5):
                        g.split_hi(act, j, 0, hi)
                    take(2, 0)
                    take(3, 0)
                    in_turns(act, XH, body)

                @block.vector
                def _(dve):
                    def body(i, more):
                        dve.wait_ge(q_["s_psum"], i + 1)
                        for b in range(2):
                            nc.vector.tensor_reduce(mx[:, 2 * b:2 * b + 2], psum[2 + b][:, :].rearrange("p (n c) -> p n c", n=2), AX.X, ALU.max).then_inc(q_["mx_done"], 1)
                        dve.wait_ge(q_["mx_done"], i * 2 + 2)
                        nc.vector.tensor_scalar(nb[:, :], mx[:, :], -SC, None, ALU.mult).then_inc(q_["nb_done"], 1)
                        dve.wait_ge(q_["e_done"], i * 4 + 4)
                        nc.vector.reciprocal(ri[:, :], sm_[:, :]).then_inc(q_["ri_done"], 1)
                        dve.wait_ge(q_["ri_done"], i + 1)
                        nc.vector.tensor_tensor(pe_[:, :, :], pe_[:, :, :], ri[:, :].unsqueeze(2).to_broadcast([P, NT, MEM]), ALU.mult).then_inc(q_["pn_done"], 1)
                        if more:
                            for j in range(6):
                                g.split_lo(dve, nc.vector, j, i + 1, hi)

                    for j in range(3):
                        g.split_lo(dve, nc.vector, j, 0, hi)
                    for k2 in range(4):
                        dve.wait_ge(q_["mem_hi"], k2 + 1)
                        nc.vector.tensor_tensor(memlo[:, 2 * k2:2 * k2 + 2, :].rearrange("p k m -> p (k m)"), psum[2 + k2][:, :],
                                                memhi[:, 2 * k2:2 * k2 + 2, :].rearrange("p k m -> p (k m)").bitcast(f32), ALU.subtract).then_inc(q_["mem_done"], 1)

                    for j in range(3, 6):
                        g.split_lo(dve, nc.vector, j, 0, hi)
                    in_turns(dve, XH, body)
        end_phase()
        router_in = psem("router_in")

        def load_router(sp_):
            sp_.dma_start(rw[:, :, :], t["router_w"].rearrange("(k p) e -> p k e", p=P)).then_inc(router_in, 16)
            sp_.dma_start(rb[:, :], t["router_rows"]).then_inc(router_in, 16)

        dense_and_norm("xa", 1, 1.0, False, load_router)
        end_phase()
        mid.close()
        w1, w1lo = pair(upper, "w1", [P, 3, KT, F])
        w, wlo = [yT, w1], [ylo, w1lo]
        first_in = [[psem(f"first_{n_}{u}") for n_ in ("gate", "up", "down")] for u in range(2)]
        BIG = 1e9
        with ExitStack() as c2:
            def b2(name, shape, dt=f32):
                return c2.enter_context(nc.sbuf_tensor("q_" + name, shape, dt))

            R = b2("R", [P, 24, NT, NE])
            G = b2("G", [P, 12, NT, 4])
            one = b2("one", [P, 10, NT])
            E16 = b2("E16", [P, 8, NE])
            ge, ohh = b2("ge", [P, 2, NT, NB + 1]), b2("ohh", [P, 2, NT, NB])
            ohl = b2("ohl", [P, 2, NT, P])
            lo = b2("lo", [P, 2, NT])
            thr = b2("thr", [P, NB + 1])
            eo = b2("eo", [P, 8, NE])
            tab = b2("tab", [P, 8])
            lg_psum, e_done, oh_done, rk_psum, list_in, list_psum, chain, x2_st = [sem("q_" + n_) for n_ in
                ("logit_psum", "e_done", "oh_done", "rank_psum", "list_in", "list_psum", "chain", "x2_stored")]
            with nc.Block() as block:
                @block.sync
                def _(sp_):
                    for n in range(NT):
                        sp_.dma_start(x2_dram[n * P:(n + 1) * P, :], xres[:, n, :]).then_inc(x2_st, 16)
                    for u in range(2):
                        for part in range(3):
                            load_expert(sp_, w[u], u, part, first_in[u][part])
                    sp_.wait_ge(x2_st, 16 * NT)

                @block.tensor
                def _(pe):
                    pe.wait_ge(router_in, 32)
                    for n in range(NT):
                        for k in range(KT):
                            ins = nc.tensor.matmul(psum[0][:, n * NE:(n + 1) * NE], xT[:, k, n * P:(n + 1) * P], rw[:, k, :], start=(k == 0), stop=(k == KT - 1))
                    ins.then_inc(lg_psum, 1)
                    pe.wait_ge(oh_done, 1)
                    for n in range(NT):
                        for m in range(n + 1):
                            ins = nc.tensor.matmul(psum[1][:, n * NE:(n + 1) * NE], cst[:, K_U:K_U + P] if m == n else cst[:, K_ONE:K_ONE + P], R[:, 12, m, :], start=(m == 0), stop=(m == n))
                    for m in range(NT):
                        ins = nc.tensor.matmul(psum[1][:, NT * NE:(NT + 1) * NE], cst[:, K_ONE:K_ONE + P], R[:, 12, m, :], start=(m == 0), stop=(m == NT - 1))
                    ins.then_inc(rk_psum, 1)
                    pe.wait_ge(list_in, 1)
                    for c in range(2):
                        for n in range(NT):
                            ins = nc.tensor.matmul(psum[2][:, 0:NB], ohl[:, c, n, :], ohh[:, c, n, :], start=(c + n == 0), stop=(c == 1 and n == NT - 1))
                    ins.then_inc(list_psum, 1)

                @block.scalar
                def _(act):
                    act.wait_ge(lg_psum, 1)
                    nc.scalar.activation(R[:, 0], psum[0][:, 0:NT * NE].rearrange("p (n e) -> p n e", n=NT), ACT.Exp, scale=-1.0).then_inc(e_done, 1)

                iota = cst[:, K_SLOT:K_SLOT + NE].unsqueeze(1).to_broadcast([P, NT, NE])
                iota4 = cst[:, K_SLOT:K_SLOT + 4].unsqueeze(1).to_broadcast([P, NT, 4])

                @block.vector
                def _(dve):
                    link = Count(dve, chain, 0)
                    V = nc.vector

                    def first_max(vals, io, mxv, eq, cand, idx, oh, n_):
                        link(V.tensor_reduce(mxv, vals, AX.X, ALU.max))
                        link(V.tensor_tensor(eq, vals, mxv.unsqueeze(2).to_broadcast([P, NT, n_]), ALU.is_equal))
                        link(V.scalar_tensor_tensor(out=cand, in0=eq, scalar=-64.0, in1=io, op0=ALU.mult, op1=ALU.add))
                        link(V.tensor_reduce(idx, cand, AX.X, ALU.min))
                        link(V.tensor_scalar(idx, idx, 64.0, None, ALU.add))
                        link(V.tensor_tensor(oh, io, idx.unsqueeze(2).to_broadcast([P, NT, n_]), ALU.is_equal))

                    link(V.tensor_scalar(thr[:, :], cst[:, K_SLOT:K_SLOT + NB + 1], float(P), None, ALU.mult))
                    link(V.tensor_scalar(E16[:, 6], cst[:, K_SLOT:K_SLOT + NE], float(P), None, ALU.mult))
                    dve.wait_ge(e_done, 1)
                    link(V.tensor_scalar(R[:, 1], R[:, 0], 1.0, None, ALU.add))
                    link(V.reciprocal(R[:, 2], R[:, 1]))
                    link(V.tensor_tensor(R[:, 3], R[:, 2], rb[:, :].unsqueeze(1).to_broadcast([P, NT, NE]), ALU.add))
                    s4 = R[:, 3].rearrange("p n (g e) -> p n g e", g=4)
                    a_, b_, c_, d_ = [s4[:, :, :, j] for j in range(4)]
                    link(V.tensor_tensor(G[:, 0], a_, b_, ALU.max))
                    link(V.tensor_tensor(G[:, 1], a_, b_, ALU.min))
                    link(V.tensor_tensor(G[:, 2], c_, d_, ALU.max))
                    link(V.tensor_tensor(G[:, 3], c_, d_, ALU.min))
                    link(V.tensor_tensor(G[:, 4], G[:, 0], G[:, 2], ALU.max))
                    link(V.tensor_tensor(G[:, 5], G[:, 0], G[:, 2], ALU.min))
                    link(V.tensor_tensor(G[:, 6], G[:, 1], G[:, 3], ALU.max))
                    link(V.tensor_tensor(G[:, 5], G[:, 5], G[:, 6], ALU.max))
                    link(V.tensor_tensor(G[:, 7], G[:, 4], G[:, 5], ALU.add))
                    first_max(G[:, 7], iota4, one[:, 0], G[:, 8], G[:, 9], one[:, 1], G[:, 10], 4)
                    link(V.tensor_scalar(G[:, 11], G[:, 10], -1.0, BIG, ALU.add, ALU.mult))
                    link(V.tensor_tensor(R[:, 4].rearrange("p n (g e) -> p n g e", g=4), s4, G[:, 11].unsqueeze(3).to_broadcast([P, NT, 4, 4]), ALU.add))
                    first_max(R[:, 4], iota, one[:, 0], R[:, 5], R[:, 6], one[:, 1], R[:, 10], NE)
                    link(V.scalar_tensor_tensor(out=R[:, 8], in0=R[:, 10], scalar=-4 * BIG, in1=R[:, 4], op0=ALU.mult, op1=ALU.add))
                    first_max(R[:, 8], iota, one[:, 0], R[:, 5], R[:, 6], one[:, 1], R[:, 11], NE)
                    link(V.tensor_tensor(R[:, 12], R[:, 10], R[:, 11], ALU.add))
                    dve.sem_inc(oh_done, 1)
                    oh2, tmp2, four = R[:, 10:12], R[:, 20:22], [P, 2, NT, NE]
                    link(V.tensor_tensor(tmp2, oh2, R[:, 2].unsqueeze(1).to_broadcast(four), ALU.mult))
                    link(V.tensor_reduce(one[:, 2:4], tmp2, AX.X, ALU.add))
                    link(V.tensor_tensor(one[:, 4], one[:, 2], one[:, 3], ALU.add))
                    link(V.reciprocal(one[:, 5], one[:, 4]))
                    link(V.tensor_tensor(r_g[:, :, :], one[:, 2:4], one[:, 5].unsqueeze(1).to_broadcast([P, 2, NT]), ALU.mult))
                    dve.wait_ge(rk_psum, 1)
                    cnt = psum[1][:, NT * NE:(NT + 1) * NE]
                    link(V.tensor_scalar(E16[:, 0], cnt, float(P), None, ALU.is_gt))
                    link(V.tensor_scalar(E16[:, 1], cnt, 2.0 * P, None, ALU.is_gt))
                    link(V.tensor_scalar(E16[:, 2], cnt, 3.0 * P, None, ALU.is_gt))
                    link(V.tensor_tensor(E16[:, 0], E16[:, 0], E16[:, 1], ALU.add))
                    link(V.tensor_tensor(E16[:, 0], E16[:, 0], E16[:, 2], ALU.add))
                    link(V.tensor_copy(E16[:, 3], E16[:, 0]))
                    src, dst = 3, 4
                    for sh in (1, 2, 4, 8):
                        link(V.tensor_copy(E16[:, dst, 0:sh], E16[:, src, 0:sh]))
                        link(V.tensor_tensor(E16[:, dst, sh:NE], E16[:, src, sh:NE], E16[:, src, 0:NE - sh], ALU.add))
                        src, dst = dst, src
                    inc = E16[:, src]
                    link(V.tensor_tensor(E16[:, 5], inc, E16[:, 0], ALU.subtract))
                    link(V.tensor_tensor(R[:, 14], psum[1][:, 0:NT * NE].rearrange("p (n e) -> p n e", n=NT), R[:, 12], ALU.subtract))
                    link(V.tensor_scalar(R[:, 15], R[:, 14], float(P), None, ALU.is_ge))
                    link(V.tensor_scalar(E16[:, 7], E16[:, 5], float(P), float((NE - 1) * P), ALU.mult, ALU.add))
                    link(V.tensor_tensor(E16[:, 7], E16[:, 7], E16[:, 6], ALU.subtract))
                    link(V.tensor_tensor(R[:, 16], R[:, 15], E16[:, 7].unsqueeze(1).to_broadcast([P, NT, NE]), ALU.mult))
                    link(V.tensor_tensor(R[:, 16], R[:, 16], E16[:, 6].unsqueeze(1).to_broadcast([P, NT, NE]), ALU.add))
                    link(V.tensor_tensor(R[:, 16], R[:, 16], R[:, 14], ALU.add))
                    slot = one[:, 6:8]
                    link(V.tensor_tensor(tmp2, oh2, R[:, 16].unsqueeze(1).to_broadcast(four), ALU.mult))
                    link(V.tensor_reduce(slot, tmp2, AX.X, ALU.add))
                    wide_ = [P, 2, NT, NB + 1]
                    link(V.tensor_tensor(ge[:, :], slot.unsqueeze(3).to_broadcast(wide_), thr[:, :].unsqueeze(1).unsqueeze(1).to_broadcast(wide_), ALU.is_ge))
                    link(V.tensor_tensor(ohh[:, :], ge[:, :, :, 0:NB], ge[:, :, :, 1:NB + 1], ALU.subtract))
                    link(V.tensor_reduce(lo[:, :], ge[:, :, :, 1:NB + 1], AX.X, ALU.add))
                    link(V.scalar_tensor_tensor(out=lo[:, :], in0=lo[:, :], scalar=-float(P), in1=slot, op0=ALU.mult, op1=ALU.add))
                    link(V.tensor_tensor(ohl[:, :], lo[:, :].unsqueeze(3).to_broadcast([P, 2, NT, P]), cst[:, K_SLOT:K_SLOT + P].unsqueeze(1).unsqueeze(1).to_broadcast([P, 2, NT, P]), ALU.is_equal))
                    link(V.tensor_tensor(ohh[:, :], ohh[:, :], cst[:, K_TOK:K_TOK + NT].unsqueeze(1).unsqueeze(3).to_broadcast([P, 2, NT, NB]), ALU.mult))
                    dve.sem_inc(list_in, 1)
                    link(V.tensor_copy(r_slot[:, :, :], slot))
                    link(V.tensor_tensor(eo[:, :, :], inc.unsqueeze(1).to_broadcast([P, 8, NE]), cst[:, K_SLOT:K_SLOT + 8].unsqueeze(2).to_broadcast([P, 8, NE]), ALU.is_le))
                    link(V.tensor_reduce(tab[:, :], eo[:, :, :], AX.X, ALU.add))
                    link(V.tensor_copy(tab[:, 7:8], inc[:, NE - 1:NE]))
                    link(V.tensor_copy(r_tab[0:1, :], tab[0:1, :]))
                    dve.wait_ge(list_psum, 1)
                    link(V.tensor_copy(r_idx[:, :], psum[2][:, 0:NB]))

        end_phase()
        mrows = ub_("mrows", [P, 2, D])
        with ExitStack() as c2:
            def b2(name, shape, dt=f32):
                return c2.enter_context(nc.sbuf_tensor("e_" + name, shape, dt))

            whi = [xlo, b2("whi", [P, KT, F], f32r)]
            idx = b2("idx", [P, 2], i32)
            xg, xghi, xglo = b2("xg", [P, 2, D]), b2("xghi", [P, KT, P], f32r), b2("xglo", [P, KT, P], f32r)
            gt, sg, hid = b2("gt", [P, 2, F]), b2("sg", [P, F]), b2("hid", [P, F])
            hhi, hlo, ye = b2("hhi", [P, 4, P], f32r), b2("hlo", [P, 4, P], f32r), b2("ye", [P, 2, D])

            def expert_sems(tag):
                names = "turn idx xT_psum xT_hi xT_done gate_psum up_psum gt sg hid hT_psum hT_hi hT_done y_psum ye w_hi w_lo".split()
                names += [f"{n_}{u}" for n_ in ("gate_in", "up_in", "down_in", "xg_in", "stored") for u in range(2)]
                return {n_: sem(f"{tag}_{n_}") for n_ in names}

            main, over = expert_sems("e"), expert_sems("o")
            parts_in = ("gate_in", "up_in", "down_in")
            CH = 4

            def chunk(ap, c):
                return ap[:, 2 * c:2 * c + 2, :]

            def split_hi(act, s, part, u, q):
                act.wait_ge(s[f"{parts_in[part]}{u}"], (q + 1) * 16)
                for c in range(CH):
                    nc.scalar.activation(chunk(whi[(1 - u, u, u)[part]], c), chunk(w[u][:, part], c), ACT.Copy).then_inc(s["w_hi"], 1)

            def split_lo(dve, s, part, u, first):
                for c in range(CH):
                    dve.wait_ge(s["w_hi"], first + (c + 1))
                    nc.vector.tensor_tensor(chunk(wlo[u][:, part], c), chunk(w[u][:, part], c), chunk(whi[(1 - u, u, u)[part]], c).bitcast(f32),
                                            ALU.subtract).then_inc(s["w_lo"], 1)

            def pe_rows(pe, s, m, q, u):
                pe.wait_ge(s[f"xg_in{u}"], (q + 1) * 16)
                for a in range(2):
                    for k in range(4):
                        ins = nc.tensor.transpose(psum[a][:, k * P:(k + 1) * P], xg[:, u, (4 * a + k) * P:(4 * a + k + 1) * P], ident)
                    ins.then_inc(s["xT_psum"], 1)

            def pe_up(pe, s, m, u, part, first):
                for k in range(KT):
                    if part == 0 and k % 4 == 0:
                        pe.wait_ge(s["xT_done"], m * 2 + (k // 4 + 1))
                    if k % 2 == 0:
                        pe.wait_ge(s["w_lo"], first + (k // 2 + 1))
                    hi, lo = whi[(1 - u, u)[part]][:, k, :], wlo[u][:, part, k, :]
                    for p_, (a, b) in enumerate(((xghi, hi), (xghi, lo), (xglo, hi))):
                        ins = nc.tensor.matmul(psum[4 if part else 2 + u][:, :], a[:, k, :], b, start=(k + p_ == 0), stop=(k == KT - 1 and p_ == 2))
                ins.then_inc(s["up_psum" if part else "gate_psum"], 1)

            def pe_hidden(pe, s, m):
                pe.wait_ge(s["hid"], m + 1)
                for f in range(4):
                    ins = nc.tensor.transpose(psum[5][:, f * P:(f + 1) * P], hid[:, f * P:(f + 1) * P], ident)
                ins.then_inc(s["hT_psum"], 1)

            def pe_down(pe, s, m, u, first):
                pe.wait_ge(s["hT_done"], m + 1)
                hi, lo = part_view(whi[u], 2), part_view(wlo[u][:, 2], 2)
                for h in range(2):
                    pe.wait_ge(s["ye"], m * 2 + (h + 1))
                    for f in range(4):
                        if h == 0:
                            pe.wait_ge(s["w_lo"], first + (f + 1))
                        c = slice(h * F, (h + 1) * F)
                        for p_, (a, b) in enumerate(((hhi, hi), (hhi, lo), (hlo, hi))):
                            ins = nc.tensor.matmul(psum[6 + h][:, :], a[:, f, :], b[:, f, c], start=(f + p_ == 0), stop=(f == 3 and p_ == 2))
                    ins.then_inc(s["y_psum"], 1)

            def act_rows(act, s, m):
                for a in range(2):
                    act.wait_ge(s["xT_psum"], m * 2 + (a + 1))
                    nc.scalar.activation(xghi[:, 4 * a:4 * a + 4, :], v3(psum[a][:, :]), ACT.Copy).then_inc(s["xT_hi"], 1)

            def act_gate(act, s, m, u):
                act.wait_ge(s["gate_psum"], m + 1)
                nc.scalar.activation(gt[:, u, :], psum[2 + u][:, :], ACT.Tanh, scale=0.5).then_inc(s["gt"], 1)

            def dve_rows(dve, s, m):
                for a in range(2):
                    dve.wait_ge(s["xT_hi"], m * 2 + (a + 1))
                    nc.vector.tensor_tensor(xglo[:, 4 * a:4 * a + 4, :], v3(psum[a][:, :]), xghi[:, 4 * a:4 * a + 4, :].bitcast(f32), ALU.subtract).then_inc(s["xT_done"], 1)

            def dve_hT(dve, s, m):
                dve.wait_ge(s["hT_hi"], m + 1)
                nc.vector.tensor_tensor(hlo[:, :, :], v3(psum[5][:, :]), hhi[:, :, :].bitcast(f32), ALU.subtract).then_inc(s["hT_done"], 1)

            def act_hidden(act, s, m):
                act.wait_ge(s["hT_psum"], m + 1)
                nc.scalar.activation(hhi[:, :, :], v3(psum[5][:, :]), ACT.Copy).then_inc(s["hT_hi"], 1)

            def dve_hidden(dve, s, m, u):
                dve.wait_ge(s["gt"], m + 1)
                nc.vector.scalar_tensor_tensor(out=sg[:, :], in0=gt[:, u, :], scalar=1.0, in1=psum[2 + u][:, :], op0=ALU.add, op1=ALU.mult).then_inc(s["sg"], 1)
                dve.wait_ge(s["sg"], m + 1)
                dve.wait_ge(s["up_psum"], m + 1)
                nc.vector.scalar_tensor_tensor(out=hid[:, :], in0=sg[:, :], scalar=0.5, in1=psum[4][:, :], op0=ALU.mult, op1=ALU.mult).then_inc(s["hid"], 1)
                dve.wait_ge(s["hid"], m + 1)

            def dve_out(dve, s, m, q, u):
                dve.wait_ge(s[f"stored{u}"], (q + 1) * 16)
                for h in range(2):
                    dve.wait_ge(s["y_psum"], m * 2 + (h + 3))
                    nc.vector.tensor_copy(ye[:, u, h * F:(h + 1) * F], psum[6 + h][:, :]).then_inc(s["ye"], 1)

            def dve_free(dve, s):
                dve.sem_inc(s["ye"], 2)
                for u in range(2):
                    dve.sem_inc(s[f"stored{u}"], 16)

            def pairs(eng, step):
                with eng.Fori(0, NE // 2 - 1) as i:
                    for u in range(2):
                        step(i * 2 + u, i, u, 2)
                i = NE // 2 - 1
                for u in range(2):
                    step(2 * i + u, i, u, 1 - u)

            def before_step(m, ahead):
                return m * 3 * CH + 3 * CH - (0 if ahead else CH)

            with nc.Block() as block:
                @block.sync
                def _(sp_):
                    sp_.dma_start(mrows[:, 0, :], t["ln_moe_g"]).then_inc(rows_in, 16)
                    sp_.dma_start(mrows[:, 1, :], t["ln_moe_b"]).then_inc(rows_in, 16)
                    for u in range(2):
                        for part in range(3):
                            sp_.wait_ge(first_in[u][part], 16)
                            sp_.sem_inc(main[f"{parts_in[part]}{u}"], 16)

                    def rows_out(m, i, u):
                        sp_.wait_ge(main["ye"], m * 2 + 4)
                        sp_.sem_inc(main["turn"], 1)
                        sp_.dma_start(y_dram[ds(i * 256 + u * P, P), :], ye[:, u, :]).then_inc(main[f"stored{u}"], 16)

                    def refill(part, m, e, u):
                        used, done = ((main["gate_psum"], m + 1), (main["up_psum"], m + 1), (main["y_psum"], m * 2 + 4))[part]
                        sp_.wait_ge(used, done)
                        sp_.sem_inc(main["turn"], 1)
                        load_expert(sp_, w[u], e, part, main[f"{parts_in[part]}{u}"])

                    def step(i, u, refill_up, refill_down):
                        m = i * 2 + u
                        if refill_up:
                            for part in range(2):
                                refill(part, m + 1, m + 3, 1 - u)
                        if refill_down:
                            refill(2, m, m + 2, u)
                        rows_out(m, i, u)

                    for part in range(2):
                        refill(part, 0, 2, 0)
                    with sp_.Fori(0, NE // 2 - 2) as i:
                        for u in range(2):
                            step(i, u, True, True)
                    for m in range(NE - 4, NE):
                        step(m // 2, m % 2, m + 3 < NE, m + 2 < NE)
                    for u in range(2):
                        sp_.wait_ge(main[f"stored{u}"], 16 * (NE // 2 + 1))
                    nov = sp_.value_load(r_tab[0:1, 7:8], min_val=0, max_val=NOV)
                    with sp_.Fori(0, NOV) as j:
                        with sp_.If(nov > j):
                            e = sp_.value_load(r_tab[0:1, ds(j, 1)], min_val=0, max_val=NE - 1)
                            for part in range(3):
                                load_expert(sp_, w[0], e, part, over[f"{parts_in[part]}0"])
                            sp_.wait_ge(over["ye"], j * 2 + 4)
                            sp_.sem_inc(over["turn"], 1)
                            sp_.dma_start(y_dram[ds(j * P + NE * P, P), :], ye[:, 0, :]).then_inc(over["stored0"], 16)
                            sp_.wait_ge(over["stored0"], (j + 2) * 16)
                            sp_.sem_inc(over["turn"], 1)

                @block.gpsimd
                def _(pool):
                    def gather(s, m, q, u, col):
                        nc.gpsimd.tensor_copy(idx[:, u:u + 1], col).then_inc(s["idx"], 1)
                        pool.wait_ge(s["idx"], m + 1)
                        pool.sem_inc(s["turn"], 1)
                        nc.gpsimd.indirect_dma_start(xg[:, u, :], None, x2_dram, bass.IndirectOffsetOnAxis(ap=idx[:, u:u + 1], axis=0)).then_inc(s[f"xg_in{u}"], 16)

                    for u in range(2):
                        gather(main, u, 0, u, r_idx[:, u:u + 1])
                    with pool.Fori(0, NE // 2 - 1) as i:
                        for u in range(2):
                            pool.wait_ge(main[f"xg_in{u}"], (i + 1) * 16)
                            pool.wait_ge(main["xT_psum"], i * 4 + (2 * u + 2))
                            gather(main, i * 2 + (u + 2), i + 1, u, r_idx[:, ds(i * 2 + (u + 2), 1)])
                    nov = pool.value_load(r_tab[0:1, 7:8], min_val=0, max_val=NOV)
                    for u in range(2):
                        pool.wait_ge(main[f"xg_in{u}"], 16 * (NE // 2))
                    pool.wait_ge(main["xT_psum"], 2 * NE)
                    with pool.Fori(0, NOV) as j:
                        with pool.If(nov > j):
                            gather(over, j, j, 0, r_idx[:, ds(j + NE, 1)])
                            pool.wait_ge(over["xg_in0"], (j + 1) * 16)
                            pool.wait_ge(over["stored0"], (j + 2) * 16)
                            pool.sem_inc(over["turn"], 1)

                @block.tensor
                def _(pe):
                    def step(m, i, u, ahead):
                        first = before_step(m, ahead)
                        if ahead:
                            pe_up(pe, main, m + 1, 1 - u, 0, first - CH)
                        pe_hidden(pe, main, m)
                        if ahead:
                            pe_up(pe, main, m + 1, 1 - u, 1, first)
                        if ahead == 2:
                            pe_rows(pe, main, m + 2, i + 1, u)
                        pe_down(pe, main, m, u, first + (CH if ahead else 0))

                    for s in (main, over):
                        pe.sem_inc(s["y_psum"], 2)
                    pe_rows(pe, main, 0, 0, 0)
                    pe_up(pe, main, 0, 0, 0, 0)
                    pe_up(pe, main, 0, 0, 1, CH)
                    pe_rows(pe, main, 1, 0, 1)
                    pairs(pe, step)
                    nov = pe.value_load(r_tab[0:1, 7:8], min_val=0, max_val=NOV)
                    with pe.Fori(0, NOV) as j:
                        with pe.If(nov > j):
                            pe_rows(pe, over, j, j, 0)
                            for part in range(2):
                                pe_up(pe, over, j, 0, part, j * 3 * CH + part * CH)
                            pe_hidden(pe, over, j)
                            pe_down(pe, over, j, 0, j * 3 * CH + 2 * CH)

                @block.scalar
                def _(act):
                    def step(m, i, u, ahead):
                        if ahead:
                            act.wait_ge(main["y_psum"], m * 2 + 2)
                            split_hi(act, main, 1, 1 - u, i + u)
                            act_gate(act, main, m + 1, 1 - u)
                        else:
                            act.wait_ge(main["up_psum"], m + 1)
                        act_hidden(act, main, m)
                        split_hi(act, main, 2, u, i)
                        if ahead == 2:
                            act_rows(act, main, m + 2)
                            split_hi(act, main, 0, u, i + 1)

                    act_rows(act, main, 0)
                    for part in range(2):
                        split_hi(act, main, part, 0, 0)
                    act_gate(act, main, 0, 0)
                    act_rows(act, main, 1)
                    split_hi(act, main, 0, 1, 0)
                    pairs(act, step)
                    nov = act.value_load(r_tab[0:1, 7:8], min_val=0, max_val=NOV)
                    with act.Fori(0, NOV) as j:
                        with act.If(nov > j):
                            act_rows(act, over, j)
                            for part in range(2):
                                split_hi(act, over, part, 0, j)
                            act_gate(act, over, j, 0)
                            act.wait_ge(over["up_psum"], j + 1)
                            split_hi(act, over, 2, 0, j)
                            act_hidden(act, over, j)

                @block.vector
                def _(dve):
                    def step(m, i, u, ahead):
                        first = before_step(m, ahead)
                        if ahead:
                            split_lo(dve, main, 1, 1 - u, first)
                        dve_hT(dve, main, m)
                        split_lo(dve, main, 2, u, first + (CH if ahead else 0))
                        if ahead:
                            dve_hidden(dve, main, m + 1, 1 - u)
                        if ahead == 2:
                            dve_rows(dve, main, m + 2)
                            split_lo(dve, main, 0, u, first + 2 * CH)
                        dve_out(dve, main, m, i, u)

                    dve_free(dve, main)
                    dve_rows(dve, main, 0)
                    for part in range(2):
                        split_lo(dve, main, part, 0, part * CH)
                    dve_hidden(dve, main, 0, 0)
                    dve_rows(dve, main, 1)
                    split_lo(dve, main, 0, 1, 2 * CH)
                    pairs(dve, step)
                    nov = dve.value_load(r_tab[0:1, 7:8], min_val=0, max_val=NOV)
                    for u in range(2):
                        dve.wait_ge(main[f"stored{u}"], 16 * (NE // 2 + 1))
                    dve_free(dve, over)
                    with dve.Fori(0, NOV) as j:
                        with dve.If(nov > j):
                            dve_rows(dve, over, j)
                            for part in range(2):
                                split_lo(dve, over, part, 0, j * 3 * CH + part * CH)
                            dve_hidden(dve, over, j, 0)
                            split_lo(dve, over, 2, 0, j * 3 * CH + 2 * CH)
                            dve_hT(dve, over, j)
                            dve_out(dve, over, j, j, 0)

        end_phase()
        with ExitStack() as c2:
            def b2(name, shape, dt=f32):
                return c2.enter_context(nc.sbuf_tensor("c_" + name, shape, dt))

            stats, mv, var, rs = b2("stats", [P, NT, 2, 6]), b2("mv", [P, NT, 2]), b2("var", [P, NT]), b2("rs", [P, NT])
            nmr, nmr_done, normed = b2("nmr", [P, NT]), sem("c_shift_done"), sem("c_normed")
            yg = b2("yg", [P, NT, 2, D])
            ax, nsem, rs_in, rs_out, x_done, z1, out_st = [sem("c_" + n_) for n_ in ("alpha_x", "norm", "rs_in", "rs_out", "x_done", "z", "out_stored")]
            y_in = [sem(f"c_y_in{n}") for n in range(NT)]
            sidx = b2("sidx", [P, 2 * NT], i32)
            with nc.Block() as block:
                @block.sync
                def _(sp_):
                    for n in range(NT):
                        sp_.wait_ge(x_done, n + 1)
                        sp_.dma_start(out[0, n * P:(n + 1) * P, :], xres[:, n, :]).then_inc(out_st, 16)
                    sp_.wait_ge(out_st, 16 * NT)

                @block.gpsimd
                def _(pool):
                    for n in range(NT):
                        for c in range(2):
                            nc.gpsimd.indirect_dma_start(yg[:, n, c, :], None, y_dram, bass.IndirectOffsetOnAxis(ap=r_slot[:, c, n:n + 1], axis=0)).then_inc(y_in[n], 16)
                    for n in range(NT):
                        pool.wait_ge(rs_in, n + 1)
                        nc.gpsimd.tensor_tensor(rs[:, n:n + 1], var[:, n:n + 1], half[:, 0:1], ALU.pow).then_inc(rs_out, 1)

                @block.scalar
                def _(act):
                    for n in range(NT):
                        nc.scalar.activation(xres[:, n, :], xres[:, n, :], ACT.Copy, scale=ALPHA).then_inc(ax, 1)
                    for n in range(NT):
                        act.wait_ge(nmr_done, n + 1)
                        nc.scalar.activation(xres[:, n, :], xres[:, n, :], ACT.Identity, scale=rs[:, n:n + 1], bias=nmr[:, n:n + 1]).then_inc(normed, 1)

                @block.vector
                def _(dve):
                    def weigh(n):
                        dve.wait_ge(y_in[n], 32)
                        dve.wait_ge(ax, n + 1)
                        for c in range(2):
                            nc.vector.scalar_tensor_tensor(out=xres[:, n, :], in0=yg[:, n, c, :], scalar=r_g[:, c, n:n + 1], in1=xres[:, n, :], op0=ALU.mult, op1=ALU.add).then_inc(z1, 1)
                            dve.wait_ge(z1, 2 * n + (c + 1))
                        for h in range(2):
                            nc.vector.bn_stats(stats[:, n, h, :], xres[:, n, h * F:(h + 1) * F]).then_inc(nsem, 1)
                        before = 4 * n - 1 if n else 0
                        dve.wait_ge(nsem, before + 2)
                        nc.vector.bn_aggr(mv[:, n, :], stats[:, n, :, :].rearrange("p h c -> p (h c)")).then_inc(nsem, 1)
                        dve.wait_ge(nsem, before + 3)
                        nc.vector.tensor_scalar(var[:, n:n + 1], mv[:, n, 1:2], LN_EPS, None, ALU.add).then_inc(rs_in, 1)

                    def shift(n):
                        dve.wait_ge(rs_out, n + 1)
                        nc.vector.tensor_scalar(nmr[:, n:n + 1], mv[:, n, 0:1], rs[:, n:n + 1], -1.0, ALU.mult, ALU.mult).then_inc(nmr_done, 1)

                    def gain(n):
                        dve.wait_ge(normed, n + 1)
                        nc.vector.tensor_tensor(xres[:, n, :], xres[:, n, :], mrows[:, 0, :], ALU.mult).then_inc(nsem, 1)
                        dve.wait_ge(nsem, 4 * n + (7 if n < NT - 1 else 4))
                        nc.vector.tensor_tensor(xres[:, n, :], xres[:, n, :], mrows[:, 1, :], ALU.add).then_inc(x_done, 1)

                    dve.wait_ge(rows_in, 96)
                    for n in range(NT):
                        weigh(n)
                        if n:
                            gain(n - 1)
                        shift(n)
                    gain(NT - 1)
        upper.close()


def kernel(**inputs):
    import numpy as _np
    import concourse.bacc as _bacc
    from concourse import mybir as _mybir
    from concourse.bass_utils import run_bass_kernel_spmd as _run

    nc = _bacc.Bacc("TRN2", target_bir_lowering=False, num_devices=1)
    a = {k: _np.asarray(v) for k, v in inputs.items()}
    lay = {n: a[n] for n in ("x", "mem", "mix_w_in", "w_proj_gdn", "w_proj_ssd", "w_proj_ret", "mix_w_out", "xa_w_q", "xa_w_k", "xa_w_v", "xa_w_o",
                              "router_w", "moe_w_gate", "moe_w_up", "moe_w_down")}
    for n in ("ln_mix_g", "ln_mix_b", "ln_xa_g", "ln_xa_b", "ln_moe_g", "ln_moe_b"):
        lay[n] = _np.broadcast_to(a[n][0], (P, D))
    lay["router_rows"] = _np.broadcast_to(a["router_b"], (P, NE))
    rows = _np.concatenate([a["gdn_a_log"][0], a["ssd_a_log"][0], a["gdn_dt_bias"][0], a["ssd_dt_bias"][0], a["ssd_d"][0]])
    lay["par_rows"] = _np.broadcast_to(rows, (P, 64))
    lay["conv_g"] = a["gdn_conv_w"][0].reshape(4, 24, P).transpose(2, 0, 1)
    lay["conv_s"] = a["ssd_conv_w"][0].reshape(4, 16, P).transpose(2, 0, 1)
    lay["convb_s"] = a["ssd_conv_b"][0].reshape(16, P).T
    lay["norm_g"] = a["gdn_norm_w"][0].reshape(P, 1)
    lay["norm_s"] = a["ssd_norm_w"][0].reshape(KT, P).T
    lay["consts"] = shape_constants()
    arrays, t = {}, {}
    for name, v in lay.items():
        v = _np.ascontiguousarray(v)
        arrays[f"in_{name}"] = v
        t[name] = nc.dram_tensor(f"in_{name}", v.shape, _mybir.dt.from_np(v.dtype), kind="ExternalInput").ap()
    out = nc.dram_tensor("out_0", (1, S, D), _mybir.dt.float32, kind="ExternalOutput").ap()
    x2_dram = nc.dram_tensor("x2_rows", (S, D), _mybir.dt.float32, kind="Internal").ap()
    y_dram = nc.dram_tensor("expert_rows", (NB * P, D), _mybir.dt.float32, kind="Internal").ap()
    program(nc, t, out, x2_dram, y_dram)
    r = _run(nc, [arrays], core_ids=[0])
    return r.results[0]["out_0"]
```
